# Optimizing a Trainium2 kernel written in Bass

```python
import math
import jax, jax.numpy as jnp
from jax import lax
import numpy as np

D_MODEL = 1024
BATCH = 1
SEQ = 512
DEPTH = 2

A_HEADS = 4
A_HEAD_DIM = 128
IDX_HEADS = 8
IDX_DIM = 64
TOPK_MAX = 256
Q_BLOCK = 128
B_HEADS = 4
B_HEAD_DIM = 128
CONV_WIDTH = 4
GDN_CHUNK = 64
C_HEADS = 4
C_KEY_DIM = 64
C_VAL_DIM = 128
RET_CHUNK = 64
D_FF = 4 * D_MODEL
ROPE_THETA = 10000.0
EPS = 1e-6
N_BRANCH = 3
A_W = A_HEADS * A_HEAD_DIM
B_W = B_HEADS * B_HEAD_DIM
C_W = C_HEADS * C_VAL_DIM
C_QK = C_HEADS * C_KEY_DIM
IN_WIDTHS = (A_W, A_HEAD_DIM, A_HEAD_DIM, IDX_HEADS * IDX_DIM, IDX_DIM, IDX_HEADS,
             B_W, B_W, B_W, B_HEADS, B_HEADS, B_W,
             C_QK, C_QK, C_W, C_W,
             N_BRANCH * D_MODEL)
IN_WIDTH = sum(IN_WIDTHS)

kernel_name = "hybrid_dsa_gdn_retention_gated_merge"

def rms_norm(x, gain=None):
    xf = x.astype(jnp.float32)
    y = xf * lax.rsqrt(jnp.mean(xf * xf, axis=-1, keepdims=True) + EPS)
    if gain is not None:
        y = y * gain.astype(jnp.float32)
    return y.astype(x.dtype)

def l2_norm(x):
    xf = x.astype(jnp.float32)
    return xf * lax.rsqrt(jnp.sum(xf * xf, axis=-1, keepdims=True) + EPS)

def rope_angles(seq, dim):
    pos = jnp.arange(seq, dtype=jnp.float32)
    inv = ROPE_THETA ** (-jnp.arange(0, dim, 2, dtype=jnp.float32) / dim)
    return pos[:, None] * inv[None, :]

def retnet_angles(seq, dim):
    pos = jnp.arange(seq, dtype=jnp.float32)
    inv = 1.0 / (ROPE_THETA ** jnp.linspace(0.0, 1.0, dim // 2, dtype=jnp.float32))
    return pos[:, None] * inv[None, :]

def rotate(x, angles):
    half = x.shape[-1] // 2
    cos = jnp.cos(angles)[None, :, None, :].astype(x.dtype)
    sin = jnp.sin(angles)[None, :, None, :].astype(x.dtype)
    x1, x2 = x[..., :half], x[..., half:]
    return jnp.concatenate([x1 * cos - x2 * sin, x2 * cos + x1 * sin], axis=-1)

def split_projection(p):
    offsets = [int(o) for o in np.cumsum(np.array(IN_WIDTHS))[:-1]]
    return jnp.split(p, offsets, axis=-1)

def to_chunks(a, chunk):
    bsz, seq = a.shape[:2]
    a = a.astype(jnp.float32).reshape((bsz, seq // chunk, chunk) + a.shape[2:])
    return jnp.moveaxis(a, 3, 1)

def dsa_attention(q, k, v, iq, ik, iw):
    bsz, seq = q.shape[:2]
    n_sel = min(TOPK_MAX, seq // 4)
    nb = seq // Q_BLOCK
    f32 = jnp.float32
    ik32 = ik.astype(f32)
    kpos = jnp.arange(seq)

    def blocks(a):
        return jnp.swapaxes(a.reshape((bsz, nb, Q_BLOCK) + a.shape[2:]), 0, 1)

    def one_block(args):
        qb, iqb, iwb, pb = args
        logits = jnp.einsum('bthd,bsd->bths', iqb.astype(f32), ik32) * (IDX_DIM ** -0.5)
        scores = jnp.einsum('bths,bth->bts', jax.nn.relu(logits), iwb.astype(f32) * (IDX_HEADS ** -0.5))
        causal = kpos[None, :] <= pb[:, None]
        scores = jnp.where(causal[None], scores, -jnp.inf)
        _, idx = lax.top_k(scores, n_sel)
        valid = idx <= pb[None, :, None]
        k_sel = jax.vmap(lambda kk, ii: kk[ii])(k, idx)
        v_sel = jax.vmap(lambda vv, ii: vv[ii])(v, idx)
        s = jnp.einsum('bthd,btkd->bthk', qb, k_sel).astype(f32) * (A_HEAD_DIM ** -0.5)
        s = jnp.where(valid[:, :, None, :], s, -jnp.inf)
        p = jax.nn.softmax(s, axis=-1).astype(v.dtype)
        return jnp.einsum('bthk,btkd->bthd', p, v_sel)

    qpos = jnp.arange(seq).reshape(nb, Q_BLOCK)
    out = lax.map(one_block, (blocks(q), blocks(iq), blocks(iw), qpos))
    return jnp.swapaxes(out, 0, 1).reshape(bsz, seq, A_W)

def causal_conv_silu(x, w):
    ch = x.shape[-1]
    y = lax.conv_general_dilated(x, w[:, None, :].astype(x.dtype), window_strides=(1,),
                                 padding=[(CONV_WIDTH - 1, 0)],
                                 dimension_numbers=('NWC', 'WIO', 'NWC'),
                                 feature_group_count=ch)
    return jax.nn.silu(y)

def gated_delta_rule(q, k, v, g, beta):
    bsz, seq, nh, dk = q.shape
    dv = v.shape[-1]
    c = GDN_CHUNK
    f32 = jnp.float32
    q = to_chunks(q, c) * (dk ** -0.5)
    k = to_chunks(k, c)
    v = to_chunks(v, c)
    beta = to_chunks(beta, c)
    g = jnp.cumsum(to_chunks(g, c), axis=-1)
    row = jnp.arange(c)
    incl = row[:, None] >= row[None, :]
    strict = row[:, None] > row[None, :]
    decay = jnp.exp(jnp.where(incl, g[..., :, None] - g[..., None, :], -jnp.inf))
    k_beta = k * beta[..., None]
    m = jnp.where(strict, jnp.einsum('bhncd,bhnmd->bhncm', k_beta, k) * decay, 0.0)
    eye = jnp.eye(c, dtype=f32)
    t_inv = lax.linalg.triangular_solve(eye + m, jnp.broadcast_to(eye, m.shape),
                                        left_side=True, lower=True, unit_diagonal=True)
    u = jnp.einsum('bhncm,bhnme->bhnce', t_inv, v * beta[..., None])
    w = jnp.einsum('bhncm,bhnmd->bhncd', t_inv, k_beta * jnp.exp(g)[..., None])
    a_intra = jnp.einsum('bhncd,bhnmd->bhncm', q, k) * decay
    xs = tuple(jnp.moveaxis(a, 2, 0) for a in (q, k, u, w, g, a_intra))

    def step(state, inp):
        q_i, k_i, u_i, w_i, g_i, a_i = inp
        v_new = u_i - jnp.einsum('bhcd,bhde->bhce', w_i, state)
        o = (jnp.einsum('bhcd,bhde->bhce', q_i * jnp.exp(g_i)[..., None], state)
             + jnp.einsum('bhcm,bhme->bhce', a_i, v_new))
        g_last = g_i[..., -1:]
        state = (state * jnp.exp(g_last)[..., None]
                 + jnp.einsum('bhcd,bhce->bhde', k_i * jnp.exp(g_last - g_i)[..., None], v_new))
        return state, o

    s0 = jnp.zeros((bsz, nh, dk, dv), f32)
    _, o = lax.scan(step, s0, xs)
    o = jnp.moveaxis(o, 0, 2)
    return jnp.moveaxis(o, 1, 3).reshape(bsz, seq, nh, dv)

def retention(q, k, v):
    bsz, seq, nh, dk = q.shape
    dv = v.shape[-1]
    c = RET_CHUNK
    f32 = jnp.float32
    q = to_chunks(q, c)
    k = to_chunks(k, c) * (dk ** -0.5)
    v = to_chunks(v, c)
    log_gamma = jnp.log(1.0 - 2.0 ** (-5.0 - jnp.arange(nh, dtype=f32)))
    row = jnp.arange(c, dtype=f32)
    rel = row[:, None] - row[None, :]
    d_intra = jnp.where(rel >= 0, jnp.exp(jnp.maximum(rel, 0.0)[None] * log_gamma[:, None, None]), 0.0)
    scores = jnp.einsum('bhncd,bhnmd->bhncm', q, k) * d_intra[None, :, None]
    inner = jnp.einsum('bhncm,bhnme->bhnce', scores, v)
    xi = jnp.exp((row + 1.0)[None] * log_gamma[:, None])
    zeta = jnp.exp((c - 1.0 - row)[None] * log_gamma[:, None])
    g_chunk = jnp.exp(c * log_gamma)
    xs = tuple(jnp.moveaxis(a, 2, 0) for a in (q, k, v))

    def step(state, inp):
        q_i, k_i, v_i = inp
        cross = jnp.einsum('bhcd,bhde->bhce', q_i, state) * xi[None, :, :, None]
        state = (state * g_chunk[None, :, None, None]
                 + jnp.einsum('bhcd,bhce->bhde', k_i, v_i * zeta[None, :, :, None]))
        return state, cross

    s0 = jnp.zeros((bsz, nh, dk, dv), f32)
    _, cross = lax.scan(step, s0, xs)
    o = inner + jnp.moveaxis(cross, 0, 2)
    return jnp.moveaxis(o, 1, 3).reshape(bsz, seq, nh, dv)

def hybrid_layer(x, ln_mix_pre, w_in, gdn_conv, gdn_a_log, gdn_dt_bias, gdn_norm,
                 w_branch, w_out, ln_mix_post, ln_mlp_pre, w_up, w_down, ln_mlp_post):
    bsz, seq, _ = x.shape
    dt = x.dtype
    h = rms_norm(x, ln_mix_pre)
    (a_q, a_k, a_v, i_q, i_k, i_w,
     b_q, b_k, b_v, b_a, b_b, b_z,
     c_q, c_k, c_v, c_g, gate_logits) = split_projection(h @ w_in)

    ang_a = rope_angles(seq, A_HEAD_DIM)
    ang_i = rope_angles(seq, IDX_DIM)
    qa = rotate(a_q.reshape(bsz, seq, A_HEADS, A_HEAD_DIM), ang_a)
    ka = rotate(a_k[:, :, None, :], ang_a)[:, :, 0]
    iq = rotate(i_q.reshape(bsz, seq, IDX_HEADS, IDX_DIM), ang_i)
    ik = rotate(i_k[:, :, None, :], ang_i)[:, :, 0]
    y_a = dsa_attention(qa, ka, a_v, iq, ik, i_w)

    qkv = causal_conv_silu(jnp.concatenate([b_q, b_k, b_v], axis=-1), gdn_conv)
    qb, kb, vb = jnp.split(qkv, [B_W, 2 * B_W], axis=-1)
    qb = l2_norm(qb.reshape(bsz, seq, B_HEADS, B_HEAD_DIM))
    kb = l2_norm(kb.reshape(bsz, seq, B_HEADS, B_HEAD_DIM))
    vb = vb.reshape(bsz, seq, B_HEADS, B_HEAD_DIM)
    g = -jnp.exp(gdn_a_log.astype(jnp.float32)) * jax.nn.softplus(b_a.astype(jnp.float32) + gdn_dt_bias.astype(jnp.float32))
    beta = jax.nn.sigmoid(b_b.astype(jnp.float32))
    o_b = gated_delta_rule(qb, kb, vb, g, beta).astype(dt)
    y_b = (rms_norm(o_b, gdn_norm) * jax.nn.silu(b_z.reshape(bsz, seq, B_HEADS, B_HEAD_DIM))).reshape(bsz, seq, B_W)

    ang_c = retnet_angles(seq, C_KEY_DIM)
    qc = rotate(c_q.reshape(bsz, seq, C_HEADS, C_KEY_DIM), ang_c)
    kc = rotate(c_k.reshape(bsz, seq, C_HEADS, C_KEY_DIM), ang_c)
    vc = c_v.reshape(bsz, seq, C_HEADS, C_VAL_DIM)
    o_c = retention(qc, kc, vc).astype(dt)
    y_c = (rms_norm(o_c) * jax.nn.silu(c_g.reshape(bsz, seq, C_HEADS, C_VAL_DIM))).reshape(bsz, seq, C_W)

    gates = jax.nn.sigmoid(gate_logits.astype(jnp.float32)).astype(dt).reshape(bsz, seq, N_BRANCH, D_MODEL)
    w_ba, w_bb, w_bc = jnp.split(w_branch, [A_W, A_W + B_W], axis=0)
    merged = (gates[:, :, 0] * (y_a @ w_ba)
              + gates[:, :, 1] * (y_b @ w_bb)
              + gates[:, :, 2] * (y_c @ w_bc))
    x = x + rms_norm(merged @ w_out, ln_mix_post)

    h2 = rms_norm(x, ln_mlp_pre)
    ff = jnp.square(jax.nn.relu(h2 @ w_up)) @ w_down
    return x + rms_norm(ff, ln_mlp_post)

def setup_inputs(seed: int = 0) -> dict:
    key = jax.random.key(seed)
    ks = jax.random.split(key, 16)
    f32 = jnp.float32

    def gain(k, width):
        return 1.0 + 0.05 * jax.random.normal(k, (DEPTH, width), f32)

    x = jax.random.normal(ks[0], (BATCH, SEQ, D_MODEL), f32)
    ln_mix_pre = gain(ks[1], D_MODEL)
    w_in = jax.random.normal(ks[2], (DEPTH, D_MODEL, IN_WIDTH), f32) * D_MODEL ** -0.5
    gdn_conv = jax.random.normal(ks[3], (DEPTH, CONV_WIDTH, 3 * B_W), f32) * CONV_WIDTH ** -0.5
    gdn_a_log = jnp.log(jax.random.uniform(ks[4], (DEPTH, B_HEADS), f32, 1.0, 16.0))
    dt_init = jnp.exp(jax.random.uniform(ks[5], (DEPTH, B_HEADS), f32, math.log(1e-3), math.log(1e-1)))
    gdn_dt_bias = dt_init + jnp.log(-jnp.expm1(-dt_init))
    gdn_norm = gain(ks[6], B_HEAD_DIM)
    w_branch = jax.random.normal(ks[7], (DEPTH, A_W + B_W + C_W, D_MODEL), f32) * A_W ** -0.5
    w_out = jax.random.normal(ks[8], (DEPTH, D_MODEL, D_MODEL), f32) * D_MODEL ** -0.5
    ln_mix_post = gain(ks[9], D_MODEL)
    ln_mlp_pre = gain(ks[10], D_MODEL)
    w_up = jax.random.normal(ks[11], (DEPTH, D_MODEL, D_FF), f32) * D_MODEL ** -0.5
    w_down = jax.random.normal(ks[12], (DEPTH, D_FF, D_MODEL), f32) * D_FF ** -0.5
    ln_mlp_post = gain(ks[13], D_MODEL)
    return {"x": x, "ln_mix_pre": ln_mix_pre, "w_in": w_in, "gdn_conv": gdn_conv,
            "gdn_a_log": gdn_a_log, "gdn_dt_bias": gdn_dt_bias, "gdn_norm": gdn_norm,
            "w_branch": w_branch, "w_out": w_out, "ln_mix_post": ln_mix_post,
            "ln_mlp_pre": ln_mlp_pre, "w_up": w_up, "w_down": w_down, "ln_mlp_post": ln_mlp_post}

def reference(x, ln_mix_pre, w_in, gdn_conv, gdn_a_log, gdn_dt_bias, gdn_norm,
              w_branch, w_out, ln_mix_post, ln_mlp_pre, w_up, w_down, ln_mlp_post):
    for l in range(DEPTH):
        x = hybrid_layer(x, ln_mix_pre[l], w_in[l], gdn_conv[l], gdn_a_log[l], gdn_dt_bias[l],
                         gdn_norm[l], w_branch[l], w_out[l], ln_mix_post[l], ln_mlp_pre[l],
                         w_up[l], w_down[l], ln_mlp_post[l])
    return x


_drawn_inputs = setup_inputs


def setup_inputs(seed=0):
    import zlib

    import numpy as np

    out = dict(_drawn_inputs(seed))
    spreads = {}
    factors = {}
    for name, (base, spread) in spreads.items():
        noise = np.random.default_rng([zlib.crc32(name.encode()), seed]).standard_normal(out[name].shape)
        drawn = base * np.exp(spread * noise) if base else spread * noise
        out[name] = __import__('jax').numpy.asarray(drawn.astype(out[name].dtype))
    for name, factor in factors.items():
        out[name] = (out[name] * factor).astype(out[name].dtype)
    return out
```

```python
from contextlib import ExitStack

import numpy as np

import concourse.bass as bass
from concourse import mybir

F32 = mybir.dt.float32
F32R = mybir.dt.float32r
ALU = mybir.AluOpType
ACT = mybir.ActivationFunctionType
AX = mybir.AxisListType

P = 128
D = 1024
S = 512
DEPTH = 2
KT = D // P
ST = S // P
H = 4
IH = 8
TOPK = min(256, S // 4)
CW = 4
FF = 4 * D
EPS = 1e-6
NEG = -1e30
GONE = -3e38
SLAB = 1024

A_Q, A_K, A_V, I_Q, I_K, I_W = 0, 512, 640, 768, 1280, 1344
B_Q, B_K, B_V, B_A, B_B, B_Z = 1352, 1864, 2376, 2888, 2892, 2896
C_Q, C_K, C_V, C_G, GATES = 3408, 3664, 3920, 4432, 4944
NMISC = IH + 2 * H

SL_BCONV = 0
SL_MISC = 12
SL_VA = 13
SL_ROT = 14
SL_CV = 28
SL_CG = 32
SL_CM = 36
SL_AM = 48
SL_BZ = 60
SL_BM = 64
SL_OUT = 76
SL_MLP = 84
GROUPS = 2
FG = FF // P // GROUPS
PER_GROUP = 2 * FG
NSLAB = SL_MLP + GROUPS * PER_GROUP
ROTS = 14
CONVS = 3 * H

TAB = {}
_at = 0
for _name, _w in (("cosA", S), ("sinA", S), ("cosI", S), ("sinI", S), ("cosR", S), ("sinR", S), ("decay", H * S),
                  ("ident", P), ("ones", P), ("tri", P), ("swapA", P), ("swapH", P), ("maskadd", P),
                  ("level", 7 * P)):
    TAB[_name] = (_at, _w)
    _at += _w
NTAB = _at
PAR = {}
_at = 0
for _name, _w in (("gmix", KT), ("gmlp", KT), ("conv", CONVS * CW), ("gnorm", 1), ("alog", H), ("dtb", H)):
    PAR[_name] = (_at, _w)
    _at += _w
NPAR = _at


def tables():
    f = np.float32
    t = np.zeros((P, NTAB), f)

    def put(name, a):
        t[:, TAB[name][0]:TAB[name][0] + TAB[name][1]] = a

    pos = np.arange(S, dtype=f)
    row = np.arange(P)

    def rotation(inv, half, c, s):
        ang = (pos[None, :] * inv[:, None].astype(f)).astype(f).astype(np.float64)
        pick = row % half
        put(c, np.cos(ang)[pick])
        put(s, np.sin(ang)[pick])

    rotation(f(10000.0) ** (-np.arange(0, 128, 2, dtype=f) / f(128)), 64, "cosA", "sinA")
    rotation(f(10000.0) ** (-np.arange(0, 64, 2, dtype=f) / f(64)), 32, "cosI", "sinI")
    rotation(f(1.0) / (f(10000.0) ** np.linspace(0.0, 1.0, 32, dtype=f)), 32, "cosR", "sinR")
    gamma = 1.0 - 2.0 ** (-5.0 - np.arange(H))
    rel = np.arange(S)[None, :] - row[:, None]
    put("decay", np.concatenate([np.where(rel >= 0, g ** np.maximum(rel, 0) * 0.125, 0.0) for g in gamma], 1))
    put("ident", np.eye(P))
    put("ones", 1.0)
    put("tri", row[:, None] <= row[None, :])
    for name, half in (("swapA", 64), ("swapH", 32)):
        m = np.zeros((P, P))
        for o in range(P):
            low = (o // half) % 2 == 0
            m[o + half if low else o - half, o] = -1.0 if low else 1.0
        put(name, m)
    put("maskadd", np.where(row[None, :] > row[:, None], NEG, 0.0))
    lv = []
    for l in range(7):
        a, b = row[:, None] >> l, row[None, :] >> l
        lv.append((b == a + 1) & (b % 2 == 1))
    put("level", np.concatenate(lv, 1))
    return t


def schedule():
    o = [("norm",)]
    for j in range(CONVS):
        o.append(("conv", j))
        if j >= 1:
            o.append(("silu", j - 1))
    o += [("misc",), ("silu", CONVS - 1), ("decays",), ("va",)]
    for r in range(ROTS):
        o.append(("rot", r))
        if r >= 1:
            o.append(("turn", r - 1))
        if 1 <= r <= 2 * H:
            o.append(("unit", r - 1))
    o += [("cv",), ("turn", ROTS - 1)]
    o += [("ret", h) for h in range(H)]
    for n in range(ST):
        o.append(("prep", n))
        if n == 0:
            o += [("soft", 0), ("attend", 0)]
        else:
            o += [("index", n), ("top", n, 0)]
        for l in range(1, 7):
            o.append(("level", n, l))
            if n and l in (2, 4):
                o.append(("top", n, l // 2))
        o.append(("scan", n))
        if n:
            o += [("top", n, 3), ("soft", n), ("attend", n)]
    for br in ("C", "A", "B"):
        o += [("fin", br, h) for h in range(H)]
        o += [("merge", br, j) for j in range(4)]
    return o


ORDER = schedule()


def bank_plan():
    uses, last, turn, done = {}, [None] * 4, 0, 0

    def use(name, bank=None):
        nonlocal turn, done
        if bank is None:
            bank = turn % 3
            turn += 1
        if name[0] not in ("ro", "ao"):
            done += 1
        uses[name] = (bank, done, last[bank])
        last[bank] = name

    for s in ORDER:
        k = s[0]
        if k == "norm":
            for i in range(KT):
                use(("hT", i))
        elif k == "decays":
            use(("gcum",))
        elif k == "turn" or k == "unit":
            use(s)
        elif k == "ret":
            use(("ro", s[1]), 3)
            for m in range(ST):
                use(("rs", s[1], m))
        elif k == "prep":
            for x in ("gb", "bb", "kk", "kq", "kn", "vn", "x0"):
                use((x, s[1]))
        elif k == "level":
            for x in ("p1", "xx", "xt"):
                if x != "xx" or s[2] < 6:
                    use((x, s[1], s[2]))
        elif k == "scan":
            for x in ("wT", "v2", "oT", "st"):
                if not (x == "wT" and s[1] == 0) and not (x == "st" and s[1] == ST - 1):
                    use((x, s[1]))
        elif k == "index":
            for i in range(IH):
                use(("il", s[1], i))
        elif k == "soft":
            for i in range(H):
                use(("as", s[1], i))
        elif k == "attend":
            use(("ao", s[1]), 3)
            for m in range(s[1] + 1):
                use(("pt", s[1], m))
        elif k == "fin" and s[1] != "A":
            use(s)
    for i in range(KT):
        use(("h2T", i), i % 4)
    return uses, last


MID, MID_LAST = bank_plan()
COUNT, _n = {}, {}
for _s in ORDER:
    _n[_s[0]] = _n.get(_s[0], 0) + 1
    COUNT[_s] = _n[_s[0]]
FIN = {(_b, _h): 4 * _i + _h + 1 for _i, _b in enumerate("CB") for _h in range(H)}


def dense_plan():
    uses, drain = {}, []

    def use(name, signals):
        uses[name] = len(drain)
        drain.extend(signals)

    for s in ORDER:
        k = s[0]
        if k == "conv":
            use(s, [("conv", s[1] + 1)])
        elif k == "misc":
            use(s, [("misc_in", 3)])
        elif k == "va":
            use(s, [("va_in", 1)])
        elif k == "rot":
            use(s, [("rot_copy", s[1] + 1)])
        elif k == "cv":
            use(s, [("cv_in", t + 1) for t in range(ST)])
        elif k == "fin" and s[1] != "A":
            use(s, [("fin_w", FIN[s[1:]])])
        elif k == "merge":
            n = 8 * "CAB".index(s[1]) + 2 * s[2]
            use(s, [("gtanh", n + 1), ("gtanh", n + 2), ("gy", n + 1), ("gy", n + 2)])
    for half in range(2):
        use(f"out{half}", [("mix_out", ST * half + t + 1) for t in range(ST)])
    return uses, drain


DENSE, DRAIN = dense_plan()


def build(nc, ws, par, post, tab, x_in, out):
    with ExitStack() as ctx:
        def sb(name, shape, dt=F32, where=ctx):
            return where.enter_context(nc.sbuf_tensor(name, shape, dt))

        sems = {}

        def sem(name):
            if name not in sems:
                sems[name] = ctx.enter_context(nc.semaphore(name))
            return sems[name]

        x_state = nc.dram_tensor("x_state", (P, ST * D), F32, kind="Internal").ap()

        tabs = sb("tabs", [P, NTAB])
        pars = sb("pars", [P, NPAR])
        a_hi = sb("a_hi", [P, KT, S], F32R)
        a_lo = sb("a_lo", [P, KT, S], F32R)
        raw = sb("raw", [P, 2, SLAB])
        w_hi = sb("w_hi", [P, 2, SLAB], F32R)
        w_lo = sb("w_lo", [P, 2, SLAB], F32R)
        wide = sb("wide", [P, ST, D])
        wt = wide[:].rearrange("p t (a s) -> p (t a) s", a=2)
        gt = sb("gt", [P, 4, S])
        small = sb("small", [P, 512])
        x = sb("x", [P, ST, D])
        xw = x[:].rearrange("p t (a s) -> p (t a) s", a=2)

        with ExitStack() as mix:
            qkv = sb("qkv", [P, CONVS, S], where=mix)
            qa = sb("qa", [P, H, S], where=mix)
            ka = sb("ka", [P, S], where=mix)
            va = sb("va", [P, ST, P], where=mix)
            iq = sb("iq", [P, H, S], where=mix)
            ik = sb("ik", [P, S], where=mix)
            oc = sb("oc", [P, H, S], where=mix)
            bw = sb("bw", [P, 10, S], where=mix)
            with ExitStack() as u:
                cqk = sb("cqk", [P, 4, S], where=u)
                cv = sb("cv", [P, ST, S], where=u)
                rp = sb("rp", [P, 2, S], where=u)
            with ExitStack() as u:
                sc = sb("sc", [P, S], where=u)
                work = sb("work", [P, S], where=u)
                rl = sb("rl", [P, 2, S], where=u)
                negb = sb("negb", [P, S], where=u)
                pr = sb("pr", [P, H, S], where=u)
                pt = sb("pt", [P, 2, S], where=u)
            with ExitStack() as u:
                y_hi = sb("y_hi", [P, H, S], F32R, where=u)
                y_lo = sb("y_lo", [P, H, S], F32R, where=u)
            pg = qkv
        with ExitStack() as mlp:
            f_hi = sb("f_hi", [P, FG, S], F32R, where=mlp)
            f_lo = sb("f_lo", [P, FG, S], F32R, where=mlp)
            post2 = sb("post2", [P, D], where=mlp)

        psD = [ctx.enter_context(nc.psum_tensor(f"psD{i}", [P, S], F32)) for i in range(4)]
        psM = [ctx.enter_context(nc.psum_tensor(f"psM{i}", [P, S], F32)) for i in range(4)]

        def T(name, i=0, w=None):
            a, n = TAB[name]
            w = w or n
            return tabs[:, a + i * w:a + (i + 1) * w]

        def par_(name):
            a, n = PAR[name]
            return pars[:, a:a + n]

        ssq, lnv, rstd = small[:, 0:4], small[:, 4:8], small[:, 8:12]
        iw = small[:, 16:48]
        ab, nab, bb_ = small[:, 48:64], small[:, 64:80], small[:, 80:96]
        e1, l1, eb, sp = small[:, 96:112], small[:, 112:128], small[:, 128:144], small[:, 144:160]
        gg, beta, gc = small[:, 160:176], small[:, 176:192], small[:, 192:208]
        ea, bhalf, b1 = small[:, 208:212], small[:, 212:228], small[:, 228:244]
        glast, gdif, egl, egc, kps = (small[:, 244 + 4 * i:248 + 4 * i] for i in range(5))
        mx8 = small[:, 264:272]
        rmax, nmax, rsum, rinv = (small[:, 272 + 4 * i:276 + 4 * i] for i in range(4))
        bneg = small[:, 288:289]
        ghalf = small[:, 289:290]

        names = ["gtri", "bI", "E", "MT", "AT", "Kp", "Kpp", "vb", "qs", "X"]
        B = {n: bw[:, i, :] for i, n in enumerate(names)}
        for i, n in enumerate(["XT", "CT", "P1", "wTn", "vn", "eg", "St", "tmp"]):
            B[n] = xw[:, i, :]

        def heads(ap):
            return ap.rearrange("p (h c) -> p h c", h=H)

        def over(ap, n):
            return ap.unsqueeze(2).broadcast_to([P, H, n])

        def each(ap):
            return ap.unsqueeze(1).broadcast_to([P, H, P])

        def cut(n):
            return slice(n * P, (n + 1) * P)

        def rot_dest(r):
            if r == 0:
                return ka[:], "A"
            if r <= 4:
                return qa[:, r - 1, :], "A"
            if r == 5:
                return ik[:], "I"
            if r <= 9:
                return iq[:, r - 6, :], "I"
            return cqk[:, r - 10, :], "R"

        def count(*step):
            return COUNT[step]

        def drained(name):
            k, a = name[0], name[1:]
            if k == "hT":
                return [("a_lo", a[0] + 1)]
            if k == "h2T":
                return [("a_lo", 2 * KT + a[0] + 1)]
            if k == "gcum":
                return [("gc", 1)]
            if k == "turn":
                return [("rot_sin", a[0] + 1)]
            if k == "unit":
                return [("unit_ln", a[0] + 1)]
            if k == "rs":
                return [("ret_p", ST * a[0] + a[1] + 1)]
            if k == "ro":
                return [("oc", a[0] + 1)]
            if k == "gb":
                return [("eg", a[0] + 1), ("glast", a[0] + 1)]
            if k == "bb":
                return [("MTb", a[0] + 1)]
            if k == "kk":
                return [("MT", a[0] + 1)]
            if k == "kq":
                return [("AT", a[0] + 1)]
            if k == "kn":
                return [("Kpp", a[0] + 1)]
            if k == "vn":
                return [("vb", a[0] + 1)]
            if k == "x0":
                return [("X", 6 * a[0] + 1)]
            if k == "p1":
                return [("P1", 6 * a[0] + a[1])]
            if k == "xx":
                return [("X", 6 * a[0] + a[1] + 1)]
            if k == "xt":
                return [("XT", 7 * a[0] + a[1] + 1)]
            if k == "wT":
                return [("wTn", a[0])]
            if k == "v2":
                return [("vnew", a[0] + 1)]
            if k == "oT":
                return [("ob", a[0] + 1)]
            if k == "st":
                return [("St", a[0] + 1)]
            if k == "il":
                return [("relu", IH * (a[0] - 1) + a[1] + 1)]
            if k == "as":
                return [("smax", H * a[0] + a[1] + 1)]
            if k == "pt":
                return [("pt", a[0] * (a[0] + 1) // 2 + a[1] + 1)]
            if k == "ao":
                return [("oa", a[0] + 1)]
            if k == "fin":
                return [("fin_ln", FIN[a])]
            raise ValueError(name)

        def mid(eng, name):
            if name[0] == "ro":
                eng.wait_ge(sem("ret_pv"), ST * name[1] + ST)
            elif name[0] == "ao":
                eng.wait_ge(sem("att_pv"), (name[1] + 1) * (name[1] + 2) // 2)
            else:
                eng.wait_ge(sem("small_done"), MID[name][1])
            return psM[MID[name][0]]

        def slab(eng, i):
            eng.wait_ge(sem("slab_done"), i + 1)

        with nc.Block() as block:
            @block.sync
            def _(sp_):
                sp_.dma_start(tabs[:], tab).then_inc(sem("tables_in"), 16)
                sp_.dma_start(x[:], x_in.rearrange("p (t d) -> p t d", t=ST)).then_inc(sem("x_in"), 16)
                sp_.wait_ge(sem("tables_in"), 16)
                sp_.wait_ge(sem("x_in"), 16)

        with nc.Fori(0, DEPTH) as layer:
            with nc.Block() as block:
                @block.sync
                def _(sp):
                    def load(i, s):
                        sp.dma_start(raw[:, s, :], ws[bass.ds(layer * NSLAB + i, 1)].rearrange("a p n -> (a p) n")) \
                            .then_inc(sem(f"raw_in{s}"), 16)

                    for s in range(2):
                        load(s, s)
                    with sp.Fori(1, NSLAB // 2) as it:
                        for s in range(2):
                            sp.wait_ge(sem("split"), it * 2 + (s - 1))
                            load(it * 2 + s, s)

                @block.gpsimd
                def _(pool):
                    def split(i, s, turn):
                        pool.wait_ge(sem(f"raw_in{s}"), turn * 16 + 16)
                        pool.tensor_tensor(w_hi[:, s, 0:1], raw[:, s, 0:1], T("ones")[:, 0:1], ALU.mult)
                        pool.tensor_scalar(w_hi[:, s, 1:], raw[:, s, 1:], 1.0, 1.0, ALU.mult, ALU.mult) \
                            .then_inc(sem("w_hi"), 1)
                        pool.wait_ge(sem("w_hi"), i + 1)
                        pool.tensor_tensor(w_lo[:, s, :], raw[:, s, :], w_hi[:, s, :].bitcast(F32), ALU.subtract) \
                            .then_inc(sem("split"), 1)

                    for s in range(2):
                        split(s, s, 0)
                    with pool.Fori(1, NSLAB // 2) as it:
                        for s in range(2):
                            pool.wait_ge(sem("slab_done"), it * 2 + (s - 1))
                            split(it * 2 + s, s, it)

                @block.tensor
                def _(pe):
                    def passes(out, lhi, llo, rhi, rlo, start, stop):
                        pe.matmul(out, lhi, rhi, start=start, stop=False)
                        pe.matmul(out, lhi, rlo, start=False, stop=False)
                        return pe.matmul(out, llo, rhi, start=False, stop=stop)

                    def tslab(out, s, ka_=KT, off=0, step=P, y=False):
                        ins = None
                        hi, lo = (y_hi, y_lo) if y else (a_hi, a_lo)
                        for k in range(ka_):
                            c = slice(k * step + off, k * step + off + P)
                            ins = passes(out, w_hi[:, s, c], w_lo[:, s, c], hi[:, k, :], lo[:, k, :],
                                         k == 0, k == ka_ - 1)
                        return ins

                    def nslab(outs, s, k0, ks, n, first, last, hi=a_hi, lo=a_lo):
                        ins = None
                        for t in range(ST):
                            for k in range(ks):
                                c = slice(k * (SLAB // ks), k * (SLAB // ks) + n)
                                ins = passes(outs[t], hi[:, k0 + k, cut(t)], lo[:, k0 + k, cut(t)],
                                             w_hi[:, s, c], w_lo[:, s, c],
                                             first and k == 0, last and k == ks - 1)
                        return ins

                    def slab_in(i):
                        pe.wait_ge(sem("split"), i + 1)
                        return i % 2

                    def bank(u):
                        if u >= 4:
                            pe.wait_ge(sem(DRAIN[u - 4][0]), DRAIN[u - 4][1])
                        return psD[u % 4]

                    def done(ins):
                        ins.then_inc(sem("slab_done"), 1)

                    def small_bank(name):
                        b, _, before = MID[name]
                        if before is not None:
                            for s, v in drained(before):
                                pe.wait_ge(sem(s), v)
                        return psM[b]

                    def small_done(ins):
                        ins.then_inc(sem("small_done"), 1)

                    def by_heads(name, lhs, rhs):
                        ps = small_bank(name)
                        for h in range(H):
                            ins = pe.matmul(ps[:, cut(h)], lhs(h), rhs(h), start=True, stop=True)
                        small_done(ins)

                    def turn_heads(name, src):
                        ps = small_bank(name)
                        for h in range(H):
                            ins = pe.transpose(ps[:, cut(h)], src(h), T("ident"))
                        small_done(ins)

                    def activation_T(which):
                        for k in range(KT):
                            ps = small_bank((which, k))
                            for t in range(ST):
                                ins = pe.transpose(ps[:, cut(t)], wide[:, t, cut(k)], T("ident"))
                            small_done(ins)

                    def norm():
                        pe.wait_ge(sem("scaled"), ST)
                        activation_T("hT")
                        pe.wait_ge(sem("a_lo"), KT)

                    def conv(j):
                        s = slab_in(SL_BCONV + j)
                        done(tslab(bank(DENSE["conv", j])[:, :], s))

                    def misc():
                        s = slab_in(SL_MISC)
                        ps = bank(DENSE[("misc",)])
                        done(nslab([ps[:, t * NMISC:(t + 1) * NMISC] for t in range(ST)], s, 0, KT, NMISC, True, True))

                    def decays():
                        pe.wait_ge(sem("g"), 1)
                        ps = small_bank(("gcum",))
                        small_done(pe.matmul(ps[:, 0:ST * H], T("tri"), gg, start=True, stop=True))

                    def va_():
                        s = slab_in(SL_VA)
                        ps = bank(DENSE[("va",)])
                        done(nslab([ps[:, cut(t)] for t in range(ST)], s, 0, KT, P, True, True))

                    def rot(r):
                        s = slab_in(SL_ROT + r)
                        done(tslab(bank(DENSE["rot", r])[:, :], s))

                    def turn(r):
                        pe.wait_ge(sem("rot_copy"), r + 1)
                        ps = small_bank(("turn", r))
                        small_done(pe.matmul(ps[:, :], T("swapA" if r < 5 else "swapH"), wt[:, r % 2, :],
                                             start=True, stop=True))

                    def unit(j):
                        pe.wait_ge(sem("unit_sq"), j + 1)
                        ps = small_bank(("unit", j))
                        small_done(pe.matmul(ps[:, :], T("ones"), wt[:, 6 + j % 2, :], start=True, stop=True))

                    def cv_():
                        u = DENSE[("cv",)]
                        ps = [bank(u + t)[:, :] for t in range(ST)]
                        for i in range(4):
                            s = slab_in(SL_CV + i)
                            done(nslab([psD[(u + t) % 4][:, :] for t in range(ST)], s, 2 * i, 2, S, i == 0, i == 3))

                    def ret(h):
                        hp = slice(64 * (h % 2), 64 * (h % 2) + 64)
                        pe.wait_ge(sem("rot_done"), ROTS)
                        pe.wait_ge(sem("cv_in"), ST)

                        def score(m):
                            ps = small_bank(("rs", h, m))
                            small_done(pe.matmul(ps[:, 0:S - m * P], cqk[hp, 2 + h // 2, cut(m)],
                                                 cqk[hp, h // 2, m * P:], start=True, stop=True))

                        def value(m, o):
                            i = ST * h + m
                            pe.wait_ge(sem("ret_p"), i + 1)
                            pe.matmul(o[:, m * P:], cv[:, m, cut(h)], rp[:, i % 2, 0:S - m * P],
                                      start=m == 0, stop=m == ST - 1).then_inc(sem("ret_pv"), 1)

                        o = small_bank(("ro", h))
                        score(0)
                        for m in range(1, ST):
                            score(m)
                            value(m - 1, o)
                        value(ST - 1, o)

                    def kB(h, n):
                        return qkv[:, h, cut(n)]

                    def prep(n):
                        for i, x_ in enumerate(("gb", "bb")):
                            pe.wait_ge(sem("gb_in"), 2 * n + i + 1)
                            ps = small_bank((x_, n))
                            small_done(pe.matmul(ps[:, :], T("ones"), B[("gtri", "bI")[i]], start=True, stop=True))
                        pe.wait_ge(sem("unit_done"), 2 * H)
                        pe.wait_ge(sem("silu"), CONVS)
                        by_heads(("kk", n), lambda h: kB(h, n), lambda h: kB(h, n))
                        by_heads(("kq", n), lambda h: kB(h, n), lambda h: qkv[:, H + h, cut(n)])
                        turn_heads(("kn", n), lambda h: kB(h, n))
                        turn_heads(("vn", n), lambda h: qkv[:, 2 * H + h, cut(n)])
                        pe.wait_ge(sem("CT"), 7 * n + 1)
                        turn_heads(("x0", n), lambda h: B["CT"][:, cut(h)])

                    def level(n, l):
                        pe.wait_ge(sem("CT"), 7 * n + l + 1)
                        pe.wait_ge(sem("X"), 6 * n + l)
                        by_heads(("p1", n, l), lambda h: B["CT"][:, cut(h)], lambda h: B["X"][:, cut(h)])
                        pe.wait_ge(sem("P1"), 6 * n + l)
                        pe.wait_ge(sem("XT"), 7 * n + l)
                        if l < 6:
                            by_heads(("xx", n, l), lambda h: B["XT"][:, cut(h)], lambda h: B["P1"][:, cut(h)])
                        by_heads(("xt", n, l), lambda h: B["P1"][:, cut(h)], lambda h: B["XT"][:, cut(h)])

                    def scan(n):
                        pe.wait_ge(sem("XT"), 7 * n + 7)
                        if n:
                            pe.wait_ge(sem("Kp"), n + 1)
                            by_heads(("wT", n), lambda h: B["Kp"][:, cut(h)], lambda h: B["XT"][:, cut(h)])
                        pe.wait_ge(sem("vb"), n + 1)
                        if n:
                            pe.wait_ge(sem("wTn"), n)
                            pe.wait_ge(sem("St"), n)
                        ps = small_bank(("v2", n))
                        for h in range(H):
                            ins = pe.matmul(ps[:, cut(h)], B["XT"][:, cut(h)], B["vb"][:, cut(h)],
                                            start=True, stop=n == 0)
                            if n:
                                ins = pe.matmul(ps[:, cut(h)], B["wTn"][:, cut(h)], B["St"][:, cut(h)],
                                                start=False, stop=True)
                        small_done(ins)
                        pe.wait_ge(sem("vnew"), n + 1)
                        pe.wait_ge(sem("AT"), n + 1)
                        pe.wait_ge(sem("qs"), n + 1)
                        ps = small_bank(("oT", n))
                        for h in range(H):
                            ins = pe.matmul(ps[:, cut(h)], B["vn"][:, cut(h)], B["AT"][:, cut(h)],
                                            start=True, stop=n == 0)
                            if n:
                                ins = pe.matmul(ps[:, cut(h)], B["St"][:, cut(h)], B["qs"][:, cut(h)],
                                                start=False, stop=True)
                        small_done(ins)
                        if n < ST - 1:
                            pe.wait_ge(sem("Kpp"), n + 1)
                            by_heads(("st", n), lambda h: B["Kpp"][:, cut(h)], lambda h: B["vn"][:, cut(h)])

                    def index(tb):
                        for i in range(IH):
                            hp = slice(64 * (i % 2), 64 * (i % 2) + 64)
                            ps = small_bank(("il", tb, i))
                            small_done(pe.matmul(ps[:, 0:(tb + 1) * P], iq[hp, i // 2, cut(tb)],
                                                 ik[hp, 0:(tb + 1) * P], start=True, stop=True))

                    def soft(tb):
                        for h in range(H):
                            ps = small_bank(("as", tb, h))
                            small_done(pe.matmul(ps[:, 0:(tb + 1) * P], qa[:, h, cut(tb)], ka[:, 0:(tb + 1) * P],
                                                 start=True, stop=True))

                    def attend(tb):
                        pe.wait_ge(sem("prob"), H * (tb + 1))
                        pe.wait_ge(sem("va_in"), 1)
                        first = tb * (tb + 1) // 2

                        def value(m, o):
                            pe.wait_ge(sem("pt"), first + m + 1)
                            pe.matmul(o[:, :], va[:, m, :], pt[:, (first + m) % 2, :],
                                      start=m == 0, stop=m == tb).then_inc(sem("att_pv"), 1)

                        o = small_bank(("ao", tb))
                        for m in range(tb + 1):
                            turn_heads(("pt", tb, m), lambda h: pr[:, h, cut(m)])
                            if m:
                                value(m - 1, o)
                        value(tb, o)

                    def fin(br, h):
                        if br == "A":
                            return
                        s = slab_in((SL_CG if br == "C" else SL_BZ) + h)
                        done(tslab(bank(DENSE["fin", br, h])[:, :], s))
                        pe.wait_ge(sem("fin_sq"), FIN[br, h])
                        ps = small_bank(("fin", br, h))
                        small_done(pe.matmul(ps[:, :], T("ones"), bw[:, 0, :], start=True, stop=True))

                    def merge(br, j):
                        b = "CAB".index(br)
                        base = (SL_CM, SL_AM, SL_BM)[b] + 3 * j
                        u = DENSE["merge", br, j]
                        for i in range(2):
                            s = slab_in(base + i)
                            done(tslab(bank(u + i)[:, :], s))
                        s = slab_in(base + 2)
                        pe.wait_ge(sem("y_lo"), H * (b + 1))
                        for i in range(2):
                            ins = tslab(bank(u + 2 + i)[:, :], s, ka_=4, off=i * P, step=2 * P, y=True)
                        done(ins)

                    steps = {"norm": norm, "conv": conv, "misc": misc, "decays": decays, "va": va_, "rot": rot,
                             "turn": turn, "unit": unit, "cv": cv_, "ret": ret, "prep": prep, "level": level,
                             "scan": scan, "index": index, "soft": soft, "attend": attend, "fin": fin, "merge": merge}
                    for kind, *args in ORDER:
                        if kind in steps:
                            steps[kind](*args)

                    for half in range(2):
                        u = DENSE[f"out{half}"]
                        outs = [bank(u + t)[:, :] for t in range(ST)]
                        for i in range(4):
                            if half == 0:
                                pe.wait_ge(sem("a_lo"), KT + 2 * i + 2)
                            s = slab_in(SL_OUT + 4 * half + i)
                            done(nslab(outs, s, 2 * i, 2, S, i == 0, i == 3))

                    pe.wait_ge(sem("scaled"), 2 * ST)
                    activation_T("h2T")
                    pe.wait_ge(sem("a_lo"), 3 * KT)
                    with pe.Fori(0, GROUPS) as g:
                        for i in range(4):
                            pe.wait_ge(sem("split"), g * PER_GROUP + (SL_MLP + i + 1))
                            pe.wait_ge(sem(f"hid_free{i}"), g + 1)
                            done(tslab(psD[i][:, :], i % 2))
                        with pe.Fori(1, FG // 4) as it:
                            for i in range(4):
                                pe.wait_ge(sem("split"), g * PER_GROUP + it * 4 + (SL_MLP + i + 1))
                                pe.wait_ge(sem("relu2"), g * FG + it * 4 + (i - 3))
                                done(tslab(psD[i][:, :], i % 2))
                        for half in range(2):
                            outs = [(psM if half == 0 else psD)[t][:, :] for t in range(ST)]
                            for t in range(ST):
                                if half == 0:
                                    pe.wait_ge(sem(f"acc_free{t}"), g + 1)
                                else:
                                    pe.wait_ge(sem("relu2"), g * FG + (FG - 3 + t))
                            for i in range(FG // 2):
                                if half == 0:
                                    pe.wait_ge(sem("f_lo"), g * FG + (2 * i + 2))
                                pe.wait_ge(sem("split"), g * PER_GROUP + (SL_MLP + FG + 8 * half + i + 1))
                                done(nslab(outs, i % 2, 2 * i, 2, S, i == 0, i == FG // 2 - 1, hi=f_hi, lo=f_lo))

                @block.scalar
                def _(act):
                    seen = {}

                    def sig(ins, name):
                        seen[name] = seen.get(name, 0) + 1
                        ins.then_inc(sem(name), 1)

                    def own(name):
                        act.wait_ge(sem(name), seen[name])

                    def rms_rows(src, wait):
                        for t in range(ST):
                            wait(t)
                            if seen.get("sq", 0) >= 1:
                                own("sq")
                            sig(act.activation(gt[:, 2 * (t % 2):2 * (t % 2) + 2, :].rearrange("p a s -> p (a s)"),
                                               src[:, t, :], ACT.Square, accum_out=ssq[:, t:t + 1]), "sq")
                        own("sq")
                        sig(act.activation(lnv, ssq, ACT.Ln, scale=1.0 / D, bias=EPS), "rln")
                        own("rln")
                        sig(act.activation(rstd, lnv, ACT.Exp, scale=-0.5), "rstd")

                    def hi_T(which, gen, gain):
                        for k in range(KT):
                            ps = mid(act, (which, k))
                            sig(act.activation(a_hi[:, k, :], ps[:, :], ACT.Copy, scale=gain[:, k:k + 1]), "a_hi")

                    act.dma_start(pars[:], par[bass.ds(layer, 1)].rearrange("a p n -> (a p) n")) \
                        .then_inc(sem("pars_in"), 16)
                    act.dma_start(x_state, x[:].rearrange("p t d -> p (t d)")).then_inc(sem("x_saved"), 16)

                    def norm():
                        rms_rows(x, lambda t: None)
                        act.wait_ge(sem("pars_in"), 16)
                        hi_T("hT", 0, par_("gmix"))

                    def silu(j):
                        act.wait_ge(sem("conv"), j + 1)
                        if j >= 2:
                            act.wait_ge(sem("silu"), j - 1)
                        sig(act.activation(gt[:, j % 2, :], qkv[:, j, :], ACT.Tanh, scale=0.5), "tanh")

                    def decays():
                        act.wait_ge(sem("misc_in"), 4)
                        sig(act.activation(e1, nab, ACT.Exp), "dec")
                        own("dec")
                        sig(act.activation(l1, e1, ACT.Ln, bias=1.0), "dec")
                        sig(act.activation(ea, par_("alog"), ACT.Exp), "dec")
                        sig(act.activation(eb, bb_, ACT.Exp, scale=-1.0), "dec")

                    def va_():
                        slab(act, SL_VA)
                        sig(act.copy(va[:].rearrange("p t d -> p (t d)"), psD[DENSE[("va",)] % 4][:, :]), "va_in")

                    def rot(r):
                        slab(act, SL_ROT + r)
                        if r >= 2:
                            act.wait_ge(sem("rot_done"), r - 1)
                        sig(act.copy(wt[:, r % 2, :], psD[DENSE["rot", r] % 4][:, :]), "rot_copy")

                    def unit(j):
                        if j >= 2:
                            mid(act, ("unit", j - 2))
                        act.wait_ge(sem("silu"), j + 1)
                        sig(act.activation(wt[:, 6 + j % 2, :], qkv[:, j, :], ACT.Square), "unit_sq")
                        ps = mid(act, ("unit", j))
                        if j >= 2:
                            act.wait_ge(sem("unit_done"), j - 1)
                        rt = gt[:, 2 + j % 2, :]
                        sig(act.activation(rt, ps[:, :], ACT.Ln, bias=4 * EPS), "unit_ln")
                        own("unit_ln")
                        sig(act.activation(rt, rt, ACT.Exp, scale=-0.5,
                                           bias=0.0 if j < H else float(-0.5 * np.log(P))), "unit_r")

                    def cv_():
                        u = DENSE[("cv",)]
                        slab(act, SL_CV + 3)
                        for t in range(ST):
                            sig(act.copy(cv[:, t, :], psD[(u + t) % 4][:, :]), "cv_in")

                    def ret(h):
                        sig(act.copy(oc[:, h, :], mid(act, ("ro", h))[:, :]), "oc")

                    def prep(n):
                        ps = mid(act, ("gb", n))
                        if n:
                            act.wait_ge(sem("St"), n)
                            act.wait_ge(sem("qs"), n)
                        else:
                            act.wait_ge(sem("x_saved"), 16)
                            act.wait_ge(sem("scaled"), ST)
                        sig(act.activation(B["eg"], ps[:, :], ACT.Exp), "eg")
                        act.wait_ge(sem("emin"), n + 1)
                        sig(act.activation(B["E"], B["E"], ACT.Exp), "E")
                        act.wait_ge(sem("glast"), n + 1)
                        sig(act.activation(egc, gc[:, n * H:(n + 1) * H], ACT.Exp), "esm")
                        act.wait_ge(sem("gdif"), n + 1)
                        sig(act.activation(kps, gdif, ACT.Exp), "esm")

                    def level(n, l):
                        if l > 1:
                            mid(act, ("xt", n, l - 1))
                        elif n:
                            mid(act, ("xt", n - 1, 6))
                        sig(act.copy(B["P1"], mid(act, ("p1", n, l))[:, :]), "P1")

                    def scan(n):
                        if n:
                            sig(act.mul(B["wTn"], mid(act, ("wT", n))[:, :], -1.0), "wTn")
                        sig(act.copy(B["vn"], mid(act, ("v2", n))[:, :]), "vnew")
                        act.wait_ge(sem("qs"), n + 1)
                        sig(act.copy(qkv[:, H:2 * H, cut(n)], heads(mid(act, ("oT", n))[:, :])), "ob")

                    def index(tb):
                        for i in range(IH):
                            ps = mid(act, ("il", tb, i))
                            q = IH * (tb - 1) + i
                            if q >= 2:
                                act.wait_ge(sem("score"), 9 * (tb - 1) + i - 1 if i >= 2 else 9 * (tb - 1))
                            sig(act.activation(rl[:, i % 2, 0:(tb + 1) * P], ps[:, 0:(tb + 1) * P], ACT.Relu,
                                               scale=0.125), "relu")

                    def soft(tb):
                        for h in range(H):
                            act.wait_ge(sem("nmax"), H * tb + h + 1)
                            w = slice(0, (tb + 1) * P)
                            sig(act.activation(pr[:, h, w], pr[:, h, w], ACT.Exp, scale=float(P) ** -0.5,
                                               bias=nmax[:, h:h + 1], accum_out=rsum[:, h:h + 1]), "sexp")

                    def attend(tb):
                        first = tb * (tb + 1) // 2
                        for m in range(tb + 1):
                            ps = mid(act, ("pt", tb, m))
                            if first + m >= 2:
                                act.wait_ge(sem("att_pv"), first + m - 1)
                            sig(act.copy(pt[:, (first + m) % 2, :], ps[:, :]), "pt")
                        sig(act.copy(qa[:, :, cut(tb)], heads(mid(act, ("ao", tb))[:, :])), "oa")

                    def fin(br, h):
                        b = "CAB".index(br)
                        if b:
                            slab(act, (SL_CM, SL_AM)[b - 1] + 11)
                        if br == "A":
                            if h == 0:
                                own("oa")
                            sig(act.copy(y_hi[:, h, :], qa[:, h, :]), "y_hi")
                            return
                        src = oc[:, h, :] if br == "C" else qkv[:, H + h, :]
                        if h == 0:
                            own("oc" if br == "C" else "ob")
                        f = FIN[br, h]
                        if f > 1:
                            act.wait_ge(sem("fy"), f - 1)
                        sig(act.activation(bw[:, 0, :], src, ACT.Square), "fin_sq")
                        ps = mid(act, ("fin", br, h))
                        sig(act.activation(bw[:, 1, :], ps[:, :], ACT.Ln, scale=1.0 / P, bias=EPS), "fin_ln")
                        own("fin_ln")
                        sig(act.activation(bw[:, 1, :], bw[:, 1, :], ACT.Exp, scale=-0.5), "fin_r")
                        sig(act.activation(bw[:, 4, :], psD[DENSE["fin", br, h] % 4][:, :], ACT.Tanh, scale=0.5),
                            "fin_t")
                        act.wait_ge(sem("fy"), f)
                        sig(act.copy(y_hi[:, h, :], bw[:, 2, :]), "y_hi")

                    def merge(br, j):
                        b = "CAB".index(br)
                        u = DENSE["merge", br, j]
                        for i in range(2):
                            n = 8 * b + 2 * j + i
                            slab(act, (SL_CM, SL_AM, SL_BM)[b] + 3 * j + i)
                            if n >= 4:
                                act.wait_ge(sem("gy"), n - 3)
                            sig(act.activation(gt[:, n % 4, :], psD[(u + i) % 4][:, :], ACT.Tanh, scale=0.5), "gtanh")

                    steps = {"norm": norm, "silu": silu, "decays": decays, "va": va_, "rot": rot,
                             "unit": unit, "cv": cv_, "ret": ret, "prep": prep, "level": level,
                             "scan": scan, "index": index, "soft": soft, "attend": attend, "fin": fin, "merge": merge}
                    for kind, *args in ORDER:
                        if kind in steps:
                            steps[kind](*args)
                        if kind == "merge" and args == ["C", 0]:
                            act.wait_ge(sem("ob"), ST)
                            act.wait_ge(sem("fy"), 1)
                            act.dma_start(x[:].rearrange("p t d -> p (t d)"), x_state).then_inc(sem("x_back"), 16)
                            act.dma_start(pg[:, 0:2, :].rearrange("p a s -> p (a s)"),
                                          post[bass.ds(layer, 1)].rearrange("a p n -> (a p) n")[:, 0:D]) \
                                .then_inc(sem("gain_in"), 16)

                    slab(act, SL_BM + 11)
                    for k in range(KT):
                        act.wait_ge(sem("merged"), KT + k + 1)
                        sig(act.mul(a_hi[:, k, :], wt[:, k, :], 0.5), "a_hi")
                    for half in range(2):
                        slab(act, SL_OUT + 4 * half + 3)
                        if half == 0:
                            act.wait_ge(sem("a_lo"), 2 * KT)
                        for t in range(ST):
                            sig(act.copy(wide[:, t, half * S:(half + 1) * S],
                                         psD[(DENSE[f"out{half}"] + t) % 4][:, :]), "mix_out")
                    own("mix_out")
                    rms_rows(wide, lambda t: None)
                    act.wait_ge(sem("mix_out"), 8)
                    rms_rows(x, lambda t: act.wait_ge(sem("x1"), t + 1))
                    hi_T("h2T", 2, par_("gmlp"))
                    act.wait_ge(sem("x1"), ST)
                    act.dma_start(post2[:], post[bass.ds(layer, 1)].rearrange("a p n -> (a p) n")[:, D:2 * D]) \
                        .then_inc(sem("gain2_in"), 16)
                    with act.Fori(0, GROUPS) as g:
                        act.wait_ge(sem("slab_done"), g * PER_GROUP + SL_MLP)
                        with act.Fori(0, FG // 4) as it:
                            for i in range(4):
                                act.wait_ge(sem("relu2"), g * FG + it * 4 + (i + 1))
                                act.copy(f_hi[:, bass.ds(it * 4 + i, 1), :].rearrange("p a s -> p (a s)"),
                                         gt[:, i, :]).then_inc(sem("f_hi"), 1)
                    for t in range(ST):
                        act.wait_ge(sem(f"acc_free{t}"), GROUPS + 1)
                        act.wait_ge(sem(f"hid_free{t}"), GROUPS + 1)
                    rms_rows(wide, lambda t: None)

                @block.vector
                def _(dve):
                    seen = {}

                    def sig(ins, name):
                        seen[name] = seen.get(name, 0) + 1
                        ins.then_inc(sem(name), 1)

                    def own(name):
                        dve.wait_ge(sem(name), seen[name])

                    def f32(ap):
                        return ap.bitcast(F32)

                    def norm_rows(gen):
                        dve.wait_ge(sem("rstd"), gen)
                        for t in range(ST):
                            sig(dve.tensor_scalar(wide[:, t, :], x[:, t, :], rstd[:, t:t + 1], None, ALU.mult), "scaled")

                    def lo_T(which, gen, gain):
                        for k in range(KT):
                            dve.wait_ge(sem("a_hi"), gen * KT + k + 1)
                            ps = psM[MID[which, k][0]]
                            sig(dve.scalar_tensor_tensor(out=a_lo[:, k, :], in0=ps[:, :], scalar=gain[:, k:k + 1],
                                                         in1=f32(a_hi[:, k, :]), op0=ALU.mult, op1=ALU.subtract), "a_lo")

                    def norm():
                        norm_rows(1)
                        dve.wait_ge(sem("pars_in"), 16)
                        sig(dve.tensor_scalar(ghalf, par_("gnorm"), 0.5, None, ALU.mult), "ghalf")
                        lo_T("hT", 0, par_("gmix"))

                    def conv(j):
                        slab(dve, SL_BCONV + j)
                        ps, dst = psD[DENSE["conv", j] % 4], qkv[:, j, :]
                        cw = par_("conv")[:, CW * j:CW * j + CW]
                        sig(dve.tensor_scalar(dst, ps[:, :], cw[:, CW - 1:CW], None, ALU.mult), "tap")
                        for d in range(1, CW):
                            own("tap")
                            ins = dve.scalar_tensor_tensor(out=dst[:, d:], in0=ps[:, 0:S - d],
                                                           scalar=cw[:, CW - 1 - d:CW - d], in1=dst[:, d:],
                                                           op0=ALU.mult, op1=ALU.add)
                            sig(ins, "tap" if d < CW - 1 else "conv")

                    def silu(j):
                        dve.wait_ge(sem("tanh"), j + 1)
                        sig(dve.scalar_tensor_tensor(out=qkv[:, j, :], in0=gt[:, j % 2, :], scalar=1.0,
                                                     in1=qkv[:, j, :], op0=ALU.add, op1=ALU.mult), "silu")

                    def misc():
                        slab(dve, SL_MISC)
                        ps = psD[DENSE[("misc",)] % 4][:, 0:ST * NMISC].rearrange("p (t n) -> p t n", t=ST)

                        def tiled(ap):
                            return ap.rearrange("p (t n) -> p t n", t=ST)

                        sig(dve.tensor_scalar(tiled(iw), ps[:, :, 0:IH], float(IH) ** -0.5, None, ALU.mult), "misc_in")
                        sig(dve.tensor_tensor(tiled(ab), ps[:, :, IH:IH + H],
                                              par_("dtb").unsqueeze(1).broadcast_to([P, ST, H]), ALU.add), "misc_in")
                        sig(dve.tensor_copy(tiled(bb_), ps[:, :, IH + H:]), "misc_in")
                        own("misc_in")
                        sig(dve.scalar_tensor_tensor(out=nab, in0=ab, scalar=-1.0, in1=ab, op0=ALU.mult,
                                                     op1=ALU.min), "misc_in")

                    def decays():
                        dve.wait_ge(sem("dec"), 4)
                        sig(dve.scalar_tensor_tensor(out=sp, in0=ab, scalar=0.0, in1=l1, op0=ALU.max, op1=ALU.add), "dd")
                        sig(dve.tensor_scalar(b1, eb, 1.0, None, ALU.add), "dd")
                        own("dd")
                        sig(dve.scalar_tensor_tensor(out=gg.rearrange("p (t n) -> p t n", t=ST),
                                                     in0=sp.rearrange("p (t n) -> p t n", t=ST), scalar=-1.0,
                                                     in1=ea.unsqueeze(1).broadcast_to([P, ST, H]),
                                                     op0=ALU.mult, op1=ALU.mult), "g")
                        sig(dve.reciprocal(beta, b1), "beta")
                        own("beta")
                        sig(dve.tensor_scalar(bhalf, beta, 0.5, None, ALU.mult), "beta")
                        ps = mid(dve, ("gcum",))
                        sig(dve.tensor_copy(gc, ps[:, 0:ST * H]), "gc")

                    def turn(r):
                        dst, kind = rot_dest(r)
                        dve.wait_ge(sem("rot_copy"), r + 1)
                        m1, m2 = wt[:, 2 + r % 2, :], wt[:, 4 + r % 2, :]
                        sig(dve.tensor_tensor(m1, wt[:, r % 2, :], T("cos" + kind), ALU.mult), "rot_cos")
                        ps = mid(dve, ("turn", r))
                        sig(dve.tensor_tensor(m2, ps[:, :], T("sin" + kind), ALU.mult), "rot_sin")
                        own("rot_cos")
                        own("rot_sin")
                        sig(dve.tensor_tensor(dst, m1, m2, ALU.add), "rot_done")

                    def unit(j):
                        dve.wait_ge(sem("unit_r"), j + 1)
                        sig(dve.tensor_tensor(qkv[:, j, :], qkv[:, j, :], gt[:, 2 + j % 2, :], ALU.mult), "unit_done")

                    def ret(h):
                        for m in range(ST):
                            i, w = ST * h + m, S - m * P
                            ps = mid(dve, ("rs", h, m))
                            if i >= 2:
                                dve.wait_ge(sem("ret_pv"), i - 1)
                            sig(dve.tensor_tensor(rp[:, i % 2, 0:w], ps[:, 0:w], T("decay", h, S)[:, 0:w],
                                                  ALU.mult), "ret_p")

                    def prep(n):
                        hh = slice(n * H, (n + 1) * H)
                        if n == 0:
                            own("beta")
                            own("gc")
                        sig(dve.tensor_tensor(heads(B["gtri"]), each(T("tri")), over(gg[:, hh], P), ALU.mult), "gb_in")
                        sig(dve.tensor_tensor(heads(B["bI"]), each(T("ident")), over(beta[:, hh], P), ALU.mult), "gb_in")
                        ps = mid(dve, ("gb", n))
                        dve.wait_ge(sem("eg"), n + 1)
                        sig(dve.tensor_tensor(heads(B["E"]), heads(ps[:, :]), over(gc[:, hh], P), ALU.subtract), "esub")
                        sig(dve.tensor_copy(glast, heads(ps[:, :])[:, :, P - 1]), "glast")
                        own("esub")
                        sig(dve.tensor_scalar(B["E"], B["E"], 0.0, None, ALU.min), "emin")
                        own("glast")
                        sig(dve.tensor_tensor(gdif, glast, gc[:, hh], ALU.subtract), "gdif")
                        ps = mid(dve, ("bb", n))
                        dve.wait_ge(sem("E"), n + 1)
                        sig(dve.tensor_tensor(B["MT"], B["E"], ps[:, :], ALU.mult), "MTb")
                        sig(dve.tensor_tensor(heads(B["AT"]), heads(B["E"]), each(T("tri")), ALU.mult), "ATm")
                        ps = mid(dve, ("kk", n))
                        own("MTb")
                        sig(dve.tensor_tensor(B["MT"], B["MT"], ps[:, :], ALU.mult), "MT")
                        own("MT")
                        sig(dve.tensor_tensor(heads(B["CT"]), heads(B["MT"]), each(T("level", 0, P)), ALU.mult), "CT")
                        ps = mid(dve, ("kq", n))
                        own("ATm")
                        sig(dve.tensor_tensor(B["AT"], B["AT"], ps[:, :], ALU.mult), "AT")
                        dve.wait_ge(sem("esm"), 2 * n + 2)
                        sig(dve.tensor_tensor(egl, beta[:, hh], egc, ALU.mult), "bk")
                        ps = mid(dve, ("kn", n))
                        own("bk")
                        sig(dve.tensor_tensor(heads(B["Kp"]), heads(ps[:, :]), over(egl, P), ALU.mult), "Kp")
                        sig(dve.tensor_tensor(heads(B["Kpp"]), heads(ps[:, :]), over(kps, P), ALU.mult), "Kpp")
                        ps = mid(dve, ("vn", n))
                        sig(dve.tensor_tensor(heads(B["vb"]), heads(ps[:, :]), over(bhalf[:, hh], P), ALU.mult), "vb")
                        dve.wait_ge(sem("eg"), n + 1)
                        sig(dve.tensor_tensor(heads(B["qs"]), qkv[:, H:2 * H, cut(n)], heads(B["eg"]), ALU.mult), "qs")
                        own("CT")
                        ps = mid(dve, ("x0", n))
                        sig(dve.scalar_tensor_tensor(out=heads(B["X"]), in0=heads(ps[:, :]), scalar=-1.0,
                                                     in1=each(T("ident")), op0=ALU.mult, op1=ALU.add), "X")
                        sig(dve.scalar_tensor_tensor(out=heads(B["XT"]), in0=heads(B["CT"]), scalar=-1.0,
                                                     in1=each(T("ident")), op0=ALU.mult, op1=ALU.add), "XT")

                    def level(n, l):
                        if l > 1:
                            mid(dve, ("p1", n, l - 1))
                        own("XT")
                        sig(dve.tensor_tensor(heads(B["CT"]), heads(B["MT"]), each(T("level", l, P)), ALU.mult), "CT")
                        if l < 6:
                            ps = mid(dve, ("xx", n, l))
                            own("X")
                            sig(dve.tensor_tensor(B["X"], B["X"], ps[:, :], ALU.subtract), "X")
                        ps = mid(dve, ("xt", n, l))
                        sig(dve.tensor_tensor(B["XT"], B["XT"], ps[:, :], ALU.subtract), "XT")

                    def scan(n):
                        if n == ST - 1:
                            mid(dve, ("oT", n))
                            return
                        if n:
                            mid(dve, ("oT", n))
                            own("St")
                            sig(dve.tensor_tensor(heads(B["St"]), heads(B["St"]),
                                                  heads(B["eg"])[:, :, P - 1:P].broadcast_to([P, H, P]),
                                                  ALU.mult), "Sd")
                            ps = mid(dve, ("st", n))
                            own("Sd")
                            sig(dve.tensor_tensor(B["St"], B["St"], ps[:, :], ALU.add), "St")
                        else:
                            sig(dve.tensor_copy(B["St"], mid(dve, ("st", n))[:, :]), "St")

                    def index(tb):
                        w = slice(0, (tb + 1) * P)
                        for i in range(IH):
                            q = IH * (tb - 1) + i
                            dve.wait_ge(sem("relu"), q + 1)
                            ww = iw[:, tb * IH + i:tb * IH + i + 1]
                            if i == 0:
                                sig(dve.tensor_scalar(sc[:, w], rl[:, 0, w], ww, None, ALU.mult), "score")
                            else:
                                own("score")
                                sig(dve.scalar_tensor_tensor(out=sc[:, w], in0=rl[:, i % 2, w], scalar=ww,
                                                             in1=sc[:, w], op0=ALU.mult, op1=ALU.add), "score")
                        own("score")
                        sig(dve.tensor_tensor(sc[:, cut(tb)], sc[:, cut(tb)], T("maskadd"), ALU.add), "score")

                    def top(tb, part):
                        w = slice(0, (tb + 1) * P)
                        for r in range(part * TOPK // 32, (part + 1) * TOPK // 32):
                            src = sc if r == 0 else work
                            own("score" if r == 0 else "picked")
                            sig(dve.max(mx8, src[:, w]), "best")
                            own("best")
                            sig(dve.match_replace(work[:, w], mx8, src[:, w], GONE), "picked")
                        if part == 3:
                            own("picked")
                            sig(dve.tensor_tensor(negb[:, w], work[:, w], sc[:, w], ALU.is_equal), "kept")
                            own("kept")
                            sig(dve.tensor_scalar(negb[:, w], negb[:, w], NEG, None, ALU.mult), "negb")

                    def soft(tb):
                        w = slice(0, (tb + 1) * P)
                        bias = negb[:, w] if tb else T("maskadd")
                        if tb:
                            own("negb")
                            mid(dve, ("pt", tb - 1, tb - 1))
                        for h in range(H):
                            ps = mid(dve, ("as", tb, h))
                            sig(dve.tensor_tensor_reduce(pr[:, h, w], ps[:, w], bias, 1.0, GONE, ALU.add, ALU.max,
                                                         rmax[:, h:h + 1]), "smax")
                            own("smax")
                            sig(dve.tensor_scalar(nmax[:, h:h + 1], rmax[:, h:h + 1], -float(P) ** -0.5, None,
                                                  ALU.mult), "nmax")
                        for h in range(H):
                            dve.wait_ge(sem("sexp"), H * tb + h + 1)
                            sig(dve.reciprocal(rinv[:, h:h + 1], rsum[:, h:h + 1]), "rinv")
                            own("rinv")
                            sig(dve.tensor_scalar(pr[:, h, w], pr[:, h, w], rinv[:, h:h + 1], None, ALU.mult), "prob")

                    def fin(br, h):
                        b = "CAB".index(br)
                        if b:
                            slab(dve, (SL_CM, SL_AM)[b - 1] + 11)
                        dve.wait_ge(sem("y_hi"), H * b + h + 1) if br == "A" else None
                        if br == "A":
                            sig(dve.tensor_tensor(y_lo[:, h, :], qa[:, h, :], f32(y_hi[:, h, :]), ALU.subtract), "y_lo")
                            return
                        f = FIN[br, h]
                        src = oc[:, h, :] if br == "C" else qkv[:, H + h, :]
                        on, sw = bw[:, 2, :], bw[:, 3, :]
                        dve.wait_ge(sem("fin_r"), f)
                        if f > 1:
                            own("y_lo")
                        sig(dve.tensor_tensor(on, src, bw[:, 1, :], ALU.mult), "fin_n")
                        dve.wait_ge(sem("fin_t"), f)
                        sig(dve.scalar_tensor_tensor(out=sw, in0=bw[:, 4, :], scalar=1.0,
                                                     in1=psD[DENSE["fin", br, h] % 4][:, :],
                                                     op0=ALU.add, op1=ALU.mult), "fin_w")
                        own("fin_n")
                        own("fin_w")
                        sig(dve.scalar_tensor_tensor(out=on, in0=on, scalar=0.5 if br == "C" else ghalf, in1=sw,
                                                     op0=ALU.mult, op1=ALU.mult), "fy")
                        dve.wait_ge(sem("y_hi"), H * b + h + 1)
                        sig(dve.tensor_tensor(y_lo[:, h, :], on, f32(y_hi[:, h, :]), ALU.subtract), "y_lo")

                    def merge(br, j):
                        b = "CAB".index(br)
                        u = DENSE["merge", br, j]
                        slab(dve, (SL_CM, SL_AM, SL_BM)[b] + 3 * j + 2)
                        for i in range(2):
                            n = 8 * b + 2 * j + i
                            dve.wait_ge(sem("gtanh"), n + 1)
                            dst = wt[:, 2 * j + i, :] if b == 0 else bw[:, 5 + n % 4, :]
                            sig(dve.scalar_tensor_tensor(out=dst, in0=gt[:, n % 4, :], scalar=1.0,
                                                         in1=psD[(u + 2 + i) % 4][:, :],
                                                         op0=ALU.add, op1=ALU.mult), "gy")
                        for i in range(2):
                            n, m = 8 * b + 2 * j + i, wt[:, 2 * j + i, :]
                            if b == 0:
                                continue
                            own("gy")
                            sig(dve.tensor_tensor(m, m, bw[:, 5 + n % 4, :], ALU.add), "merged")

                    steps = {"norm": norm, "conv": conv, "silu": silu, "misc": misc, "decays": decays, "turn": turn,
                             "unit": unit, "ret": ret, "prep": prep, "level": level, "scan": scan,
                             "index": index, "top": top, "soft": soft, "fin": fin, "merge": merge}
                    for kind, *args in ORDER:
                        if kind in steps:
                            steps[kind](*args)

                    for k in range(KT):
                        dve.wait_ge(sem("a_hi"), KT + k + 1)
                        sig(dve.scalar_tensor_tensor(out=a_lo[:, k, :], in0=wt[:, k, :], scalar=0.5,
                                                     in1=f32(a_hi[:, k, :]), op0=ALU.mult, op1=ALU.subtract), "a_lo")
                    def residual(gen, gain):
                        dve.wait_ge(sem("rstd"), gen)
                        for t in range(ST):
                            sig(dve.scalar_tensor_tensor(out=wide[:, t, :], in0=wide[:, t, :], scalar=rstd[:, t:t + 1],
                                                         in1=gain, op0=ALU.mult, op1=ALU.mult), "post")
                            own("post")
                            sig(dve.tensor_tensor(x[:, t, :], x[:, t, :], wide[:, t, :], ALU.add), "x1")

                    dve.wait_ge(sem("x_back"), 16)
                    dve.wait_ge(sem("gain_in"), 16)
                    residual(2, pg[:, 0:2, :].rearrange("p a s -> p (a s)"))
                    own("x1")
                    norm_rows(3)
                    lo_T("h2T", 2, par_("gmlp"))
                    mid(dve, ("h2T", KT - 1))
                    sig(dve.memset(wide[:], 0.0), "zeroed")
                    dve.wait_ge(sem("mix_out"), 8)
                    for t in range(ST):
                        dve.sem_inc(sem(f"hid_free{t}"), 1)
                        dve.sem_inc(sem(f"acc_free{t}"), 1)
                    own("zeroed")
                    with dve.Fori(0, GROUPS) as g:
                        with dve.Fori(0, FG // 4) as it:
                            for i in range(4):
                                dve.wait_ge(sem("slab_done"), g * PER_GROUP + it * 4 + (SL_MLP + i + 1))
                                dve.tensor_scalar(gt[:, i, :], psD[i][:, :], 0.0, None, ALU.max) \
                                    .then_inc(sem("relu1"), 1)
                                dve.wait_ge(sem("relu1"), g * FG + it * 4 + (i + 1))
                                dve.tensor_tensor(gt[:, i, :], gt[:, i, :], psD[i][:, :], ALU.mult) \
                                    .then_inc(sem("relu2"), 1)
                                dve.wait_ge(sem("f_hi"), g * FG + it * 4 + (i + 1))
                                dve.tensor_tensor(f_lo[:, bass.ds(it * 4 + i, 1), :].rearrange("p a s -> p (a s)"),
                                                  gt[:, i, :],
                                                  f32(f_hi[:, bass.ds(it * 4 + i, 1), :].rearrange("p a s -> p (a s)")),
                                                  ALU.subtract).then_inc(sem("f_lo"), 1)
                        for half in range(2):
                            dve.wait_ge(sem("slab_done"), g * PER_GROUP + (SL_MLP + FG + 8 * half + 8))
                            for t in range(ST):
                                w = wide[:, t, half * S:(half + 1) * S]
                                ps = (psM if half == 0 else psD)[t]
                                dve.tensor_tensor(w, w, ps[:, :], ALU.add) \
                                    .then_inc(sem(f"acc_free{t}" if half == 0 else f"hid_free{t}"), 1)
                        for t in range(ST):
                            dve.wait_ge(sem(f"acc_free{t}"), g + 2)
                            dve.wait_ge(sem(f"hid_free{t}"), g + 2)
                    dve.wait_ge(sem("gain2_in"), 16)
                    residual(4, post2[:])
                    own("x1")
            ids = [s.num for s in sems.values()]
            nc.all_engine_barrier(sems_to_clear=range(min(ids), max(ids) + 1))

        with nc.Block() as block:
            @block.sync
            def _(sp_):
                sp_.dma_start(out.rearrange("p (t d) -> p t d", t=ST), x[:]).then_inc(sem("x_out"), 16)
                sp_.wait_ge(sem("x_out"), 16)


def lay_out(i, a):
    f = np.float32
    w_in, w_branch, w_out, w_up, w_down = (a[n][i] for n in ("w_in", "w_branch", "w_out", "w_up", "w_down"))
    slabs = []

    def kn(w, k0, ks, c0, n):
        s = w[k0 * P:(k0 + ks) * P, c0:c0 + n].reshape(ks, P, -1).transpose(1, 0, 2)
        if s.shape[2] * ks < SLAB:
            s = np.concatenate([s, np.zeros((P, ks, SLAB // ks - s.shape[2]), f)], 2)
        slabs.append(s.reshape(P, SLAB))

    for c in (B_K, B_Q, B_V):
        for h in range(H):
            kn(w_in, 0, KT, c + h * P, P)
    kn(np.concatenate([w_in[:, I_W:I_W + IH], w_in[:, B_A:B_A + 2 * H]], 1), 0, KT, 0, NMISC)
    kn(w_in, 0, KT, A_V, P)
    for c in (A_K, A_Q, A_Q + P, A_Q + 2 * P, A_Q + 3 * P):
        kn(w_in, 0, KT, c, P)
    kn(np.concatenate([w_in[:, I_K:I_K + 64]] * 2, 1), 0, KT, 0, P)
    for c in (I_Q, I_Q + P, I_Q + 2 * P, I_Q + 3 * P, C_Q, C_Q + P, C_K, C_K + P):
        kn(w_in, 0, KT, c, P)
    for k in range(0, KT, 2):
        kn(w_in, k, 2, C_V, S)
    for b in (2, 0, 1):
        if b != 0:
            for h in range(H):
                kn(w_in, 0, KT, (C_G if b == 2 else B_Z) + h * P, P)
        for j in range(4):
            for t in (2 * j, 2 * j + 1):
                kn(w_in, 0, KT, GATES + b * D + t * P, P)
            kn(w_branch, 4 * b, 4, 2 * j * P, 2 * P)
    for half in range(2):
        for k in range(0, KT, 2):
            kn(w_out, k, 2, half * S, S)
    for g in range(GROUPS):
        for t in range(FG):
            kn(w_up, 0, KT, (g * FG + t) * P, P)
        for half in range(2):
            for k in range(0, FG, 2):
                kn(w_down, g * FG + k, 2, half * S, S)
    assert len(slabs) == NSLAB
    return np.stack(slabs)


def kernel(**inputs):
    import concourse.bacc as bacc
    from concourse.bass_utils import run_bass_kernel_spmd as run

    a = {n: np.asarray(v) for n, v in inputs.items()}
    f = np.float32
    ws = np.concatenate([lay_out(i, a) for i in range(DEPTH)])
    par = np.zeros((DEPTH, P, NPAR), f)
    for i in range(DEPTH):
        for n, v in (("gmix", a["ln_mix_pre"][i].reshape(KT, P).T), ("gmlp", a["ln_mlp_pre"][i].reshape(KT, P).T),
                     ("conv", a["gdn_conv"][i].reshape(CW, 3, H, P)[:, [1, 0, 2]].reshape(CW, CONVS, P)
                      .transpose(2, 1, 0).reshape(P, -1)),
                     ("gnorm", a["gdn_norm"][i][:, None]), ("alog", np.broadcast_to(a["gdn_a_log"][i], (P, H))),
                     ("dtb", np.broadcast_to(a["gdn_dt_bias"][i], (P, H)))):
            par[i, :, PAR[n][0]:PAR[n][0] + PAR[n][1]] = v
    post = np.stack([np.concatenate([np.broadcast_to(a["ln_mix_post"][i], (P, D)),
                                     np.broadcast_to(a["ln_mlp_post"][i], (P, D))], 1) for i in range(DEPTH)])
    xs = np.ascontiguousarray(a["x"].reshape(ST, P, D).transpose(1, 0, 2).reshape(P, ST * D))
    arrays = {"in_ws": ws, "in_par": par, "in_post": np.ascontiguousarray(post), "in_tab": tables(), "in_x": xs}
    nc = bacc.Bacc("TRN2", target_bir_lowering=False, num_devices=1, dynamic_dma_scratch_size=1024)
    args = [nc.dram_tensor(n, v.shape, F32, kind="ExternalInput").ap() for n, v in arrays.items()]
    out = nc.dram_tensor("out", (P, ST * D), F32, kind="ExternalOutput").ap()
    build(nc, *args, out)
    r = run(nc, [arrays], core_ids=[0])
    return np.asarray(r.results[0]["out"]).reshape(P, ST, D).transpose(1, 0, 2).reshape(1, S, D)
```

```python
from contextlib import ExitStack

import numpy as np

import concourse.bass as bass
from concourse import mybir

F32 = mybir.dt.float32
F32R = mybir.dt.float32r
ALU = mybir.AluOpType
ACT = mybir.ActivationFunctionType
AX = mybir.AxisListType

P = 128
D = 1024
S = 512
DEPTH = 2
KT = D // P
ST = S // P
H = 4
IH = 8
TOPK = min(256, S // 4)
CW = 4
FF = 4 * D
EPS = 1e-6
NEG = -1e30
GONE = -3e38
SLAB = 1024

A_Q, A_K, A_V, I_Q, I_K, I_W = 0, 512, 640, 768, 1280, 1344
B_Q, B_K, B_V, B_A, B_B, B_Z = 1352, 1864, 2376, 2888, 2892, 2896
C_Q, C_K, C_V, C_G, GATES = 3408, 3664, 3920, 4432, 4944
NMISC = IH + 2 * H

GROUPS = 2
FG = FF // P // GROUPS
PER_GROUP = 2 * FG
ROTS = 14
CONVS = 3 * H

TAB = {}
_at = 0
for _name, _w in (("cosA", S), ("sinA", S), ("cosI", S), ("sinI", S), ("cosR", S), ("sinR", S), ("decay", H * S),
                  ("ident", P), ("ones", P), ("tri", P), ("swapA", P), ("swapH", P), ("maskadd", P),
                  ("level", 7 * P)):
    TAB[_name] = (_at, _w)
    _at += _w
NTAB = _at
PAR = {}
_at = 0
for _name, _w in (("gmix", KT), ("gmlp", KT), ("conv", CONVS * CW), ("gnorm", 1), ("alog", H), ("dtb", H)):
    PAR[_name] = (_at, _w)
    _at += _w
NPAR = _at


def tables():
    f = np.float32
    t = np.zeros((P, NTAB), f)

    def put(name, a):
        t[:, TAB[name][0]:TAB[name][0] + TAB[name][1]] = a

    pos = np.arange(S, dtype=f)
    row = np.arange(P)

    def rotation(inv, half, c, s):
        ang = (pos[None, :] * inv[:, None].astype(f)).astype(f).astype(np.float64)
        pick = row % half
        put(c, np.cos(ang)[pick])
        put(s, np.sin(ang)[pick])

    rotation(f(10000.0) ** (-np.arange(0, 128, 2, dtype=f) / f(128)), 64, "cosA", "sinA")
    rotation(f(10000.0) ** (-np.arange(0, 64, 2, dtype=f) / f(64)), 32, "cosI", "sinI")
    rotation(f(1.0) / (f(10000.0) ** np.linspace(0.0, 1.0, 32, dtype=f)), 32, "cosR", "sinR")
    gamma = 1.0 - 2.0 ** (-5.0 - np.arange(H))
    rel = np.arange(S)[None, :] - row[:, None]
    put("decay", np.concatenate([np.where(rel >= 0, g ** np.maximum(rel, 0) * 0.125, 0.0) for g in gamma], 1))
    put("ident", np.eye(P))
    put("ones", 1.0)
    put("tri", row[:, None] <= row[None, :])
    for name, half in (("swapA", 64), ("swapH", 32)):
        m = np.zeros((P, P))
        for o in range(P):
            low = (o // half) % 2 == 0
            m[o + half if low else o - half, o] = -1.0 if low else 1.0
        put(name, m)
    put("maskadd", np.where(row[None, :] > row[:, None], NEG, 0.0))
    lv = []
    for l in range(7):
        a, b = row[:, None] >> l, row[None, :] >> l
        lv.append((b == a + 1) & (b % 2 == 1))
    put("level", np.concatenate(lv, 1))
    return t


def schedule():
    o = [("norm",)]
    for j in range(CONVS):
        o.append(("conv", j))
        if j >= 1:
            o.append(("silu", j - 1))
    o += [("misc",), ("silu", CONVS - 1), ("va",), ("decays",)]
    for r in range(4):
        o += [("rot", r), ("unit", 2 * r), ("turn", r), ("unit", 2 * r + 1)]
    others = [("cv",)]
    for r in range(4, ROTS):
        others += [("rot", r), ("turn", r)]
        if r % 2:
            others.append(("ret", (r - 5) // 2)) if r < 12 else None
    others += [("soft", 0), ("attend", 0)]
    dense = [("cg", h) for h in range(H)] + [("gate", "C", n) for n in range(KT)]
    for tb in range(1, ST):
        others += [("index", tb), dense.pop(0)]
        for part in range(4):
            others.append(("top", tb, part))
            if part % 2 or tb == 3:
                others.append(dense.pop(0))
        others += [("soft", tb), ("attend", tb)]
    others += dense
    others += [("fin", "C", h) for h in range(H)]
    others += [("mergeC", j) for j in range(4)]
    for h in range(H):
        others += [("fin", "A", h)]
    for j in range(4):
        others += [("merge", "A", j), ("z", j)]
    chain = []
    for n in range(ST):
        chain.append([("prep", n), ("pair", n)])
        for l in range(1, 7):
            chain += [[("left", n, l)], [("right", n, l)]]
        chain.append([("scan", n)])
    at = 0
    for i, steps in enumerate(chain):
        o += steps
        to = (i + 1) * len(others) // len(chain)
        o += others[at:to]
        at = to
    o += [("fin", "B", h) for h in range(H)]
    o += [("merge", "B", j) for j in range(4)]
    return o


ORDER = schedule()


def slab_plan():
    number, holds = {}, []

    def add(step, *what):
        for i, w in enumerate(what):
            number[step, i] = len(holds)
            holds.append(w)

    for s in ORDER:
        k = s[0]
        if k == "conv":
            add(s, ("in", 0, KT, (B_K, B_Q, B_V)[s[1] // H] + s[1] % H * P, P))
        elif k == "misc":
            add(s, ("misc", 0, KT, 0, NMISC))
        elif k == "va":
            add(s, ("in", 0, KT, A_V, P))
        elif k == "rot":
            r = s[1]
            if r == 9:
                add(s, ("ik", 0, KT, 0, P))
            else:
                add(s, ("in", 0, KT, C_Q + r * P if r < 2 else C_K + (r - 2) * P if r < 4 else A_K if r == 4
                        else A_Q + (r - 5) * P if r < 9 else I_Q + (r - 10) * P, P))
        elif k == "cv":
            add(s, *(("in", i, 2, C_V, S) for i in range(0, KT, 2)))
        elif k == "cg":
            add(s, ("in", 0, KT, C_G + s[1] * P, P))
        elif k == "z":
            add(s, ("in", 0, KT, B_Z + s[1] * P, P))
        elif k == "gate":
            add(s, ("in", 0, KT, GATES + 2 * D + s[2] * P, P))
        elif k == "mergeC":
            add(s, ("branch", 2 * H, H, s[1] * 2 * P, 2 * P))
        elif k == "merge":
            b = "AB".index(s[1])
            add(s, *(("in", 0, KT, GATES + b * D + (2 * s[2] + i) * P, P) for i in range(2)),
                ("branch", H * b, H, s[2] * 2 * P, 2 * P))
    for half in range(2):
        add(f"out{half}", *(("out", i, 2, half * S, S) for i in range(0, KT, 2)))
    for g in range(GROUPS):
        add(f"group{g}", *(("up", 0, KT, (g * FG + i) * P, P) for i in range(FG)),
            *(("down", g * FG + i, 2, half * S, S) for half in range(2) for i in range(0, FG, 2)))
    return number, holds


SLAB_OF, HOLDS = slab_plan()
NSLAB = len(HOLDS)
SL_MLP = SLAB_OF["group0", 0]


def bank_plan():
    uses, last, turn, done = {}, [None] * 4, 0, 0

    def use(name, bank=None):
        nonlocal turn, done
        if bank is None:
            bank = turn % 3
            turn += 1
        if name[0] not in ("ro", "ao"):
            done += 1
        uses[name] = (bank, done, last[bank])
        last[bank] = name

    for s in ORDER:
        k = s[0]
        if k == "norm":
            for i in range(KT):
                use(("hT", i))
        elif k == "decays":
            use(("gcum",))
        elif k in ("turn", "unit"):
            use(s)
        elif k == "ret":
            use(("ro", s[1]), 3)
            for m in range(ST):
                use(("rs", s[1], m))
        elif k == "prep":
            for x in ("gb", "bb", "kk", "kq", "kn", "vn"):
                use((x, s[1]))
        elif k == "pair":
            use(("x0", s[1]))
        elif k == "left":
            use(("p1", s[1], s[2]))
        elif k == "right":
            for x in ("xx", "xt"):
                if x != "xx" or s[2] < 6:
                    use((x, s[1], s[2]))
        elif k == "scan":
            for x in ("wT", "v2", "oT", "st"):
                if not (x == "wT" and s[1] == 0) and not (x == "st" and s[1] == ST - 1):
                    use((x, s[1]))
        elif k == "index":
            for i in range(IH):
                use(("il", s[1], i))
        elif k == "soft":
            for i in range(H):
                use(("as", s[1], i))
        elif k == "attend":
            use(("ao", s[1]), 3)
            for m in range(s[1] + 1):
                use(("pt", s[1], m))
        elif k == "fin" and s[1] != "A":
            use(s)
    for i in range(KT):
        use(("h2T", i), i % 4)
    return uses, last


MID, MID_LAST = bank_plan()
FIN = {(_b, _h): 4 * _i + _h + 1 for _i, _b in enumerate("CB") for _h in range(H)}


def dense_plan():
    uses, drain = {}, []

    def use(name, signals):
        uses[name] = len(drain)
        drain.extend(signals)

    for s in ORDER:
        k = s[0]
        if k == "conv":
            use(s, [("conv", s[1] + 1)])
        elif k == "misc":
            use(s, [("misc_in", 3)])
        elif k == "va":
            use(s, [("va_in", 1)])
        elif k == "rot":
            use(s, [("rot_copy", s[1] + 1)])
        elif k == "cv":
            use(s, [("cv_in", t + 1) for t in range(ST)])
        elif k in ("cg", "z"):
            use(s, [(k + "_w", s[1] + 1)])
        elif k == "gate":
            use(s, [("gateC", s[2] + 1)])
        elif k == "mergeC":
            use(s, [("gy", 2 * s[1] + 1), ("gy", 2 * s[1] + 2)])
        elif k == "merge":
            n = 8 * "AB".index(s[1]) + 2 * s[2]
            use(s, [("gtanh", n + 1), ("gtanh", n + 2), ("gy", KT + n + 1), ("gy", KT + n + 2)])
    assert len(drain) % 4 == 0
    for half in range(2):
        use(f"out{half}", [("mix_out", ST * half + t + 1) for t in range(ST)])
    return uses, drain


DENSE, DRAIN = dense_plan()


def build(nc, ws, par, post, tab, x_in, out):
    with ExitStack() as ctx:
        def sb(name, shape, dt=F32, where=ctx):
            return where.enter_context(nc.sbuf_tensor(name, shape, dt))

        sems = {}

        def sem(name):
            if name not in sems:
                sems[name] = ctx.enter_context(nc.semaphore(name))
            return sems[name]

        x_state = nc.dram_tensor("x_state", (P, ST * D), F32, kind="Internal").ap()

        tabs = sb("tabs", [P, NTAB])
        pars = sb("pars", [P, NPAR])
        a_hi = sb("a_hi", [P, KT, S], F32R)
        a_lo = sb("a_lo", [P, KT, S], F32R)
        raw = sb("raw", [P, 2, SLAB])
        w_hi = sb("w_hi", [P, 2, SLAB], F32R)
        w_lo = sb("w_lo", [P, 2, SLAB], F32R)
        wide = sb("wide", [P, ST, D])
        wt = wide[:].rearrange("p t (a s) -> p (t a) s", a=2)
        gt = sb("gt", [P, 4, S])
        small = sb("small", [P, 512])
        x = sb("x", [P, ST, D])
        xw = x[:].rearrange("p t (a s) -> p (t a) s", a=2)

        with ExitStack() as mix:
            qkv = sb("qkv", [P, CONVS, S], where=mix)
            qa = sb("qa", [P, H, S], where=mix)
            ka = sb("ka", [P, S], where=mix)
            va = sb("va", [P, ST, P], where=mix)
            iq = sb("iq", [P, H, S], where=mix)
            ik = sb("ik", [P, S], where=mix)
            oc = sb("oc", [P, H, S], where=mix)
            bw = sb("bw", [P, 10, S], where=mix)
            with ExitStack() as u:
                cqk = sb("cqk", [P, 4, S], where=u)
                cv = sb("cv", [P, ST, S], where=u)
                rp = sb("rp", [P, 2, S], where=u)
            with ExitStack() as u:
                sc = sb("sc", [P, S], where=u)
                work = sb("work", [P, S], where=u)
                rl = sb("rl", [P, 2, S], where=u)
                negb = sb("negb", [P, S], where=u)
                pr = sb("pr", [P, H, S], where=u)
                pt = sb("pt", [P, 2, S], where=u)
            with ExitStack() as u:
                y_hi = sb("y_hi", [P, H, S], F32R, where=u)
                y_lo = sb("y_lo", [P, H, S], F32R, where=u)
                mt = sb("mt", [P, 3, S], where=u)
            pg = qkv
        with ExitStack() as mlp:
            f_hi = sb("f_hi", [P, FG, S], F32R, where=mlp)
            f_lo = sb("f_lo", [P, FG, S], F32R, where=mlp)
            post2 = sb("post2", [P, D], where=mlp)

        psD = [ctx.enter_context(nc.psum_tensor(f"psD{i}", [P, S], F32)) for i in range(4)]
        psM = [ctx.enter_context(nc.psum_tensor(f"psM{i}", [P, S], F32)) for i in range(4)]

        def T(name, i=0, w=None):
            a, n = TAB[name]
            w = w or n
            return tabs[:, a + i * w:a + (i + 1) * w]

        def par_(name):
            a, n = PAR[name]
            return pars[:, a:a + n]

        ssq, lnv, rstd = small[:, 0:4], small[:, 4:8], small[:, 8:12]
        iw = small[:, 16:48]
        ab, nab, bb_ = small[:, 48:64], small[:, 64:80], small[:, 80:96]
        e1, l1, eb, sp = small[:, 96:112], small[:, 112:128], small[:, 128:144], small[:, 144:160]
        gg, beta, gc = small[:, 160:176], small[:, 176:192], small[:, 192:208]
        ea, bhalf, b1 = small[:, 208:212], small[:, 212:228], small[:, 228:244]
        glast, gdif, egl, egc, kps = (small[:, 244 + 4 * i:248 + 4 * i] for i in range(5))
        mx8 = small[:, 264:272]
        rmax, nmax, rsum, rinv = (small[:, 272 + 4 * i:276 + 4 * i] for i in range(4))
        bneg = small[:, 288:289]
        ghalf = small[:, 289:290]

        names = ["gtri", "bI", "E", "MT", "AT", "Kp", "Kpp", "vb", "qs", "X"]
        B = {n: bw[:, i, :] for i, n in enumerate(names)}
        for i, n in enumerate(["XT", "CT", "P1", "wTn", "vn", "eg", "St", "tmp"]):
            B[n] = xw[:, i, :]

        def heads(ap):
            return ap.rearrange("p (h c) -> p h c", h=H)

        def over(ap, n):
            return ap.unsqueeze(2).broadcast_to([P, H, n])

        def each(ap):
            return ap.unsqueeze(1).broadcast_to([P, H, P])

        def cut(n):
            return slice(n * P, (n + 1) * P)

        def rot_dest(r):
            if r < 4:
                return cqk[:, r, :], "R"
            if r == 4:
                return ka[:], "A"
            if r < 9:
                return qa[:, r - 5, :], "A"
            if r == 9:
                return ik[:], "I"
            return iq[:, r - 10, :], "I"

        def fin_scratch(f):
            return iq[:, f % 2, :], iq[:, 2 + f % 2, :], (ka, ik)[f % 2][:]

        def drained(name):
            k, a = name[0], name[1:]
            if k == "hT":
                return [("a_lo", a[0] + 1)]
            if k == "h2T":
                return [("a_lo", 2 * KT + a[0] + 1)]
            if k == "gcum":
                return [("gc", 1)]
            if k == "turn":
                return [("rot_sin", a[0] + 1)]
            if k == "unit":
                return [("unit_ln", a[0] + 1)]
            if k == "rs":
                return [("ret_p", ST * a[0] + a[1] + 1)]
            if k == "ro":
                return [("oc", a[0] + 1)]
            if k == "gb":
                return [("eg", a[0] + 1), ("glast", a[0] + 1)]
            if k == "bb":
                return [("MTb", a[0] + 1)]
            if k == "kk":
                return [("MT", a[0] + 1)]
            if k == "kq":
                return [("AT", a[0] + 1)]
            if k == "kn":
                return [("Kpp", a[0] + 1)]
            if k == "vn":
                return [("vb", a[0] + 1)]
            if k == "x0":
                return [("X", 6 * a[0] + 1)]
            if k == "p1":
                return [("P1", 6 * a[0] + a[1])]
            if k == "xx":
                return [("X", 6 * a[0] + a[1] + 1)]
            if k == "xt":
                return [("XT", 7 * a[0] + a[1] + 1)]
            if k == "wT":
                return [("wTn", a[0])]
            if k == "v2":
                return [("vnew", a[0] + 1)]
            if k == "oT":
                return [("ob", a[0] + 1)]
            if k == "st":
                return [("St", a[0] + 1)]
            if k == "il":
                return [("relu", IH * (a[0] - 1) + a[1] + 1)]
            if k == "as":
                return [("smax", H * a[0] + a[1] + 1)]
            if k == "pt":
                return [("pt", a[0] * (a[0] + 1) // 2 + a[1] + 1)]
            if k == "ao":
                return [("oa", a[0] + 1)]
            if k == "fin":
                return [("fin_ln", FIN[a])]
            raise ValueError(name)

        def mid(eng, name):
            if name[0] == "ro":
                eng.wait_ge(sem("ret_pv"), ST * name[1] + ST)
            elif name[0] == "ao":
                eng.wait_ge(sem("att_pv"), (name[1] + 1) * (name[1] + 2) // 2)
            else:
                eng.wait_ge(sem("small_done"), MID[name][1])
            return psM[MID[name][0]]

        def slab(eng, step, i=0):
            eng.wait_ge(sem("slab_done"), SLAB_OF[step, i] + 1)

        def dbank(step, i=0):
            return psD[(DENSE[step] + i) % 4]

        with nc.Block() as block:
            @block.sync
            def _(sp_):
                sp_.dma_start(tabs[:], tab).then_inc(sem("tables_in"), 16)
                sp_.dma_start(x[:], x_in.rearrange("p (t d) -> p t d", t=ST)).then_inc(sem("x_in"), 16)
                sp_.wait_ge(sem("tables_in"), 16)
                sp_.wait_ge(sem("x_in"), 16)

        with nc.Fori(0, DEPTH) as layer:
            with nc.Block() as block:
                @block.sync
                def _(sp):
                    def load(i, s):
                        sp.dma_start(raw[:, s, :], ws[bass.ds(layer * NSLAB + i, 1)].rearrange("a p n -> (a p) n")) \
                            .then_inc(sem(f"raw_in{s}"), 16)

                    for s in range(2):
                        load(s, s)
                    with sp.Fori(1, NSLAB // 2) as it:
                        for s in range(2):
                            sp.wait_ge(sem("split"), it * 2 + (s - 1))
                            load(it * 2 + s, s)

                @block.gpsimd
                def _(pool):
                    def split(i, s, turn):
                        pool.wait_ge(sem(f"raw_in{s}"), turn * 16 + 16)
                        pool.tensor_tensor(w_hi[:, s, 0:1], raw[:, s, 0:1], T("ones")[:, 0:1], ALU.mult)
                        pool.tensor_scalar(w_hi[:, s, 1:], raw[:, s, 1:], 1.0, 1.0, ALU.mult, ALU.mult) \
                            .then_inc(sem("w_hi"), 1)
                        pool.wait_ge(sem("w_hi"), i + 1)
                        pool.tensor_tensor(w_lo[:, s, :], raw[:, s, :], w_hi[:, s, :].bitcast(F32), ALU.subtract) \
                            .then_inc(sem("split"), 1)

                    for s in range(2):
                        split(s, s, 0)
                    with pool.Fori(1, NSLAB // 2) as it:
                        for s in range(2):
                            pool.wait_ge(sem("slab_done"), it * 2 + (s - 1))
                            split(it * 2 + s, s, it)

                @block.tensor
                def _(pe):
                    def passes(out, lhi, llo, rhi, rlo, start, stop):
                        pe.matmul(out, lhi, rhi, start=start, stop=False)
                        pe.matmul(out, lhi, rlo, start=False, stop=False)
                        return pe.matmul(out, llo, rhi, start=False, stop=stop)

                    def tslab(out, s, ka_=KT, off=0, step=P, y=False):
                        ins = None
                        hi, lo = (y_hi, y_lo) if y else (a_hi, a_lo)
                        for k in range(ka_):
                            c = slice(k * step + off, k * step + off + P)
                            ins = passes(out, w_hi[:, s, c], w_lo[:, s, c], hi[:, k, :], lo[:, k, :],
                                         k == 0, k == ka_ - 1)
                        return ins

                    def nslab(outs, s, k0, ks, n, first, last, hi=a_hi, lo=a_lo):
                        ins = None
                        for t in range(ST):
                            for k in range(ks):
                                c = slice(k * (SLAB // ks), k * (SLAB // ks) + n)
                                ins = passes(outs[t], hi[:, k0 + k, cut(t)], lo[:, k0 + k, cut(t)],
                                             w_hi[:, s, c], w_lo[:, s, c],
                                             first and k == 0, last and k == ks - 1)
                        return ins

                    def slab_in(step, i=0):
                        pe.wait_ge(sem("split"), SLAB_OF[step, i] + 1)
                        return SLAB_OF[step, i] % 2

                    def bank(u):
                        if u >= 4:
                            pe.wait_ge(sem(DRAIN[u - 4][0]), DRAIN[u - 4][1])
                        return psD[u % 4]

                    def done(ins):
                        ins.then_inc(sem("slab_done"), 1)

                    def small_bank(name):
                        b, _, before = MID[name]
                        if before is not None:
                            for s, v in drained(before):
                                pe.wait_ge(sem(s), v)
                        return psM[b]

                    def small_done(ins):
                        ins.then_inc(sem("small_done"), 1)

                    def by_heads(name, lhs, rhs):
                        ps = small_bank(name)
                        for h in range(H):
                            ins = pe.matmul(ps[:, cut(h)], lhs(h), rhs(h), start=True, stop=True)
                        small_done(ins)

                    def turn_heads(name, src):
                        ps = small_bank(name)
                        for h in range(H):
                            ins = pe.transpose(ps[:, cut(h)], src(h), T("ident"))
                        small_done(ins)

                    def activation_T(which):
                        for k in range(KT):
                            ps = small_bank((which, k))
                            for t in range(ST):
                                ins = pe.transpose(ps[:, cut(t)], wide[:, t, cut(k)], T("ident"))
                            small_done(ins)

                    def norm():
                        pe.wait_ge(sem("scaled"), ST)
                        activation_T("hT")
                        pe.wait_ge(sem("a_lo"), KT)

                    def dense_T(step):
                        s = slab_in(step)
                        done(tslab(bank(DENSE[step])[:, :], s))

                    def conv(j):
                        dense_T(("conv", j))

                    def misc():
                        s = slab_in(("misc",))
                        ps = bank(DENSE[("misc",)])
                        done(nslab([ps[:, t * NMISC:(t + 1) * NMISC] for t in range(ST)], s, 0, KT, NMISC, True, True))

                    def decays():
                        pe.wait_ge(sem("g"), 1)
                        ps = small_bank(("gcum",))
                        small_done(pe.matmul(ps[:, 0:ST * H], T("tri"), gg, start=True, stop=True))

                    def va_():
                        s = slab_in(("va",))
                        ps = bank(DENSE[("va",)])
                        done(nslab([ps[:, cut(t)] for t in range(ST)], s, 0, KT, P, True, True))

                    def rot(r):
                        dense_T(("rot", r))

                    def turn(r):
                        pe.wait_ge(sem("rot_copy"), r + 1)
                        ps = small_bank(("turn", r))
                        small_done(pe.matmul(ps[:, :], T("swapA" if 4 <= r < 9 else "swapH"), wt[:, r % 2, :],
                                             start=True, stop=True))

                    def unit(j):
                        pe.wait_ge(sem("unit_sq"), j + 1)
                        ps = small_bank(("unit", j))
                        small_done(pe.matmul(ps[:, :], T("ones"), wt[:, 6 + j % 2, :], start=True, stop=True))

                    def cv_():
                        u = DENSE[("cv",)]
                        ps = [bank(u + t)[:, :] for t in range(ST)]
                        for i in range(4):
                            s = slab_in(("cv",), i)
                            done(nslab([psD[(u + t) % 4][:, :] for t in range(ST)], s, 2 * i, 2, S, i == 0, i == 3))

                    def ret(h):
                        hp = slice(64 * (h % 2), 64 * (h % 2) + 64)
                        pe.wait_ge(sem("rot_done"), 4)
                        pe.wait_ge(sem("cv_in"), ST)

                        def score(m):
                            ps = small_bank(("rs", h, m))
                            small_done(pe.matmul(ps[:, 0:S - m * P], cqk[hp, 2 + h // 2, cut(m)],
                                                 cqk[hp, h // 2, m * P:], start=True, stop=True))

                        def value(m, o):
                            i = ST * h + m
                            pe.wait_ge(sem("ret_p"), i + 1)
                            pe.matmul(o[:, m * P:], cv[:, m, cut(h)], rp[:, i % 2, 0:S - m * P],
                                      start=m == 0, stop=m == ST - 1).then_inc(sem("ret_pv"), 1)

                        o = small_bank(("ro", h))
                        score(0)
                        for m in range(1, ST):
                            score(m)
                            value(m - 1, o)
                        value(ST - 1, o)

                    def kB(h, n):
                        return qkv[:, h, cut(n)]

                    def prep(n):
                        for i, x_ in enumerate(("gb", "bb")):
                            pe.wait_ge(sem("gb_in"), 2 * n + i + 1)
                            ps = small_bank((x_, n))
                            small_done(pe.matmul(ps[:, :], T("ones"), B[("gtri", "bI")[i]], start=True, stop=True))
                        pe.wait_ge(sem("unit_done"), 2 * H)
                        pe.wait_ge(sem("silu"), CONVS)
                        by_heads(("kk", n), lambda h: kB(h, n), lambda h: kB(h, n))
                        by_heads(("kq", n), lambda h: kB(h, n), lambda h: qkv[:, H + h, cut(n)])
                        turn_heads(("kn", n), lambda h: kB(h, n))
                        turn_heads(("vn", n), lambda h: qkv[:, 2 * H + h, cut(n)])

                    def pair(n):
                        pe.wait_ge(sem("CT"), 7 * n + 1)
                        turn_heads(("x0", n), lambda h: B["CT"][:, cut(h)])

                    def left(n, l):
                        pe.wait_ge(sem("CT"), 7 * n + l + 1)
                        pe.wait_ge(sem("X"), 6 * n + l)
                        by_heads(("p1", n, l), lambda h: B["CT"][:, cut(h)], lambda h: B["X"][:, cut(h)])

                    def right(n, l):
                        pe.wait_ge(sem("P1"), 6 * n + l)
                        pe.wait_ge(sem("XT"), 7 * n + l)
                        if l < 6:
                            by_heads(("xx", n, l), lambda h: B["XT"][:, cut(h)], lambda h: B["P1"][:, cut(h)])
                        by_heads(("xt", n, l), lambda h: B["P1"][:, cut(h)], lambda h: B["XT"][:, cut(h)])

                    def scan(n):
                        pe.wait_ge(sem("XT"), 7 * n + 7)
                        if n:
                            pe.wait_ge(sem("Kp"), n + 1)
                            by_heads(("wT", n), lambda h: B["Kp"][:, cut(h)], lambda h: B["XT"][:, cut(h)])
                        pe.wait_ge(sem("vb"), n + 1)
                        if n:
                            pe.wait_ge(sem("wTn"), n)
                            pe.wait_ge(sem("St"), n)
                        ps = small_bank(("v2", n))
                        for h in range(H):
                            ins = pe.matmul(ps[:, cut(h)], B["XT"][:, cut(h)], B["vb"][:, cut(h)],
                                            start=True, stop=n == 0)
                            if n:
                                ins = pe.matmul(ps[:, cut(h)], B["wTn"][:, cut(h)], B["St"][:, cut(h)],
                                                start=False, stop=True)
                        small_done(ins)
                        pe.wait_ge(sem("vnew"), n + 1)
                        pe.wait_ge(sem("AT"), n + 1)
                        pe.wait_ge(sem("qs"), n + 1)
                        ps = small_bank(("oT", n))
                        for h in range(H):
                            ins = pe.matmul(ps[:, cut(h)], B["vn"][:, cut(h)], B["AT"][:, cut(h)],
                                            start=True, stop=n == 0)
                            if n:
                                ins = pe.matmul(ps[:, cut(h)], B["St"][:, cut(h)], B["qs"][:, cut(h)],
                                                start=False, stop=True)
                        small_done(ins)
                        if n < ST - 1:
                            pe.wait_ge(sem("Kpp"), n + 1)
                            by_heads(("st", n), lambda h: B["Kpp"][:, cut(h)], lambda h: B["vn"][:, cut(h)])

                    def index(tb):
                        pe.wait_ge(sem("rot_done"), ROTS)
                        for i in range(IH):
                            hp = slice(64 * (i % 2), 64 * (i % 2) + 64)
                            ps = small_bank(("il", tb, i))
                            small_done(pe.matmul(ps[:, 0:(tb + 1) * P], iq[hp, i // 2, cut(tb)],
                                                 ik[hp, 0:(tb + 1) * P], start=True, stop=True))

                    def soft(tb):
                        pe.wait_ge(sem("rot_done"), 9)
                        for h in range(H):
                            ps = small_bank(("as", tb, h))
                            small_done(pe.matmul(ps[:, 0:(tb + 1) * P], qa[:, h, cut(tb)], ka[:, 0:(tb + 1) * P],
                                                 start=True, stop=True))

                    def attend(tb):
                        pe.wait_ge(sem("prob"), H * (tb + 1))
                        pe.wait_ge(sem("va_in"), 1)
                        first = tb * (tb + 1) // 2

                        def value(m, o):
                            pe.wait_ge(sem("pt"), first + m + 1)
                            pe.matmul(o[:, :], va[:, m, :], pt[:, (first + m) % 2, :],
                                      start=m == 0, stop=m == tb).then_inc(sem("att_pv"), 1)

                        o = small_bank(("ao", tb))
                        for m in range(tb + 1):
                            turn_heads(("pt", tb, m), lambda h: pr[:, h, cut(m)])
                            if m:
                                value(m - 1, o)
                        value(tb, o)

                    def fin(br, h):
                        if br == "A":
                            return
                        pe.wait_ge(sem("fin_sq"), FIN[br, h])
                        ps = small_bank(("fin", br, h))
                        small_done(pe.matmul(ps[:, :], T("ones"), fin_scratch(FIN[br, h])[0], start=True, stop=True))

                    def branch(step, i, gates, finished):
                        s = slab_in(step, i)
                        pe.wait_ge(sem("y_lo"), H * finished)
                        for i in range(2):
                            ins = tslab(bank(DENSE[step] + gates + i)[:, :], s, ka_=H, off=i * P, step=2 * P, y=True)
                        done(ins)

                    def mergeC(j):
                        branch(("mergeC", j), 0, 0, 1)

                    def merge(br, j):
                        for i in range(2):
                            s = slab_in(("merge", br, j), i)
                            done(tslab(bank(DENSE["merge", br, j] + i)[:, :], s))
                        branch(("merge", br, j), 2, 2, 2 + "AB".index(br))

                    steps = {"norm": norm, "conv": conv, "misc": misc, "decays": decays, "va": va_, "rot": rot,
                             "turn": turn, "unit": unit, "cv": cv_, "ret": ret, "prep": prep, "pair": pair,
                             "left": left, "right": right, "scan": scan, "index": index, "soft": soft,
                             "attend": attend, "fin": fin, "merge": merge, "mergeC": mergeC}
                    for kind, *args in ORDER:
                        if kind in steps:
                            steps[kind](*args)
                        elif kind in ("cg", "z", "gate"):
                            dense_T((kind, *args))

                    for half in range(2):
                        u = DENSE[f"out{half}"]
                        outs = [bank(u + t)[:, :] for t in range(ST)]
                        for i in range(4):
                            if half == 0:
                                pe.wait_ge(sem("a_lo"), KT + 2 * i + 2)
                            s = slab_in(f"out{half}", i)
                            done(nslab(outs, s, 2 * i, 2, S, i == 0, i == 3))

                    pe.wait_ge(sem("scaled"), 2 * ST)
                    activation_T("h2T")
                    pe.wait_ge(sem("a_lo"), 3 * KT)
                    with pe.Fori(0, GROUPS) as g:
                        for i in range(4):
                            pe.wait_ge(sem("split"), g * PER_GROUP + (SL_MLP + i + 1))
                            pe.wait_ge(sem(f"hid_free{i}"), g + 1)
                            done(tslab(psD[i][:, :], i % 2))
                        with pe.Fori(1, FG // 4) as it:
                            for i in range(4):
                                pe.wait_ge(sem("split"), g * PER_GROUP + it * 4 + (SL_MLP + i + 1))
                                pe.wait_ge(sem("relu2"), g * FG + it * 4 + (i - 3))
                                done(tslab(psD[i][:, :], i % 2))
                        for half in range(2):
                            outs = [(psM if half == 0 else psD)[t][:, :] for t in range(ST)]
                            for t in range(ST):
                                if half == 0:
                                    pe.wait_ge(sem(f"acc_free{t}"), g + 1)
                                else:
                                    pe.wait_ge(sem("relu2"), g * FG + (FG - 3 + t))
                            for i in range(FG // 2):
                                if half == 0:
                                    pe.wait_ge(sem("f_lo"), g * FG + (2 * i + 2))
                                pe.wait_ge(sem("split"), g * PER_GROUP + (SL_MLP + FG + 8 * half + i + 1))
                                done(nslab(outs, i % 2, 2 * i, 2, S, i == 0, i == FG // 2 - 1, hi=f_hi, lo=f_lo))

                @block.scalar
                def _(act):
                    seen = {}

                    def sig(ins, name):
                        seen[name] = seen.get(name, 0) + 1
                        ins.then_inc(sem(name), 1)

                    def own(name):
                        act.wait_ge(sem(name), seen[name])

                    def rms_rows(src, wait):
                        for t in range(ST):
                            wait(t)
                            if seen.get("sq", 0) >= 1:
                                own("sq")
                            sig(act.activation(gt[:, 2 * (t % 2):2 * (t % 2) + 2, :].rearrange("p a s -> p (a s)"),
                                               src[:, t, :], ACT.Square, accum_out=ssq[:, t:t + 1]), "sq")
                        own("sq")
                        sig(act.activation(lnv, ssq, ACT.Ln, scale=1.0 / D, bias=EPS), "rln")
                        own("rln")
                        sig(act.activation(rstd, lnv, ACT.Exp, scale=-0.5), "rstd")

                    def hi_T(which, gen, gain):
                        for k in range(KT):
                            ps = mid(act, (which, k))
                            sig(act.activation(a_hi[:, k, :], ps[:, :], ACT.Copy, scale=gain[:, k:k + 1]), "a_hi")

                    act.dma_start(pars[:], par[bass.ds(layer, 1)].rearrange("a p n -> (a p) n")) \
                        .then_inc(sem("pars_in"), 16)
                    act.dma_start(x_state, x[:].rearrange("p t d -> p (t d)")).then_inc(sem("x_saved"), 16)

                    def norm():
                        rms_rows(x, lambda t: None)
                        act.wait_ge(sem("pars_in"), 16)
                        hi_T("hT", 0, par_("gmix"))

                    def silu(j):
                        act.wait_ge(sem("conv"), j + 1)
                        if j >= 2:
                            act.wait_ge(sem("silu"), j - 1)
                        sig(act.activation(gt[:, j % 2, :], qkv[:, j, :], ACT.Tanh, scale=0.5), "tanh")

                    def decays():
                        act.preload_act_table_set("natural_log_exp_and_others")
                        act.wait_ge(sem("misc_in"), 4)
                        sig(act.activation(e1, nab, ACT.Exp), "dec")
                        own("dec")
                        sig(act.activation(l1, e1, ACT.Ln, bias=1.0), "dec")
                        sig(act.activation(ea, par_("alog"), ACT.Exp), "dec")
                        sig(act.activation(eb, bb_, ACT.Exp, scale=-1.0), "dec")

                    def va_():
                        slab(act, ("va",))
                        sig(act.copy(va[:].rearrange("p t d -> p (t d)"), dbank(("va",))[:, :]), "va_in")

                    def rot(r):
                        slab(act, ("rot", r))
                        if r >= 2:
                            act.wait_ge(sem("rot_done"), r - 1)
                        sig(act.copy(wt[:, r % 2, :], dbank(("rot", r))[:, :]), "rot_copy")

                    def unit(j):
                        if j >= 2:
                            mid(act, ("unit", j - 2))
                        act.wait_ge(sem("silu"), j + 1)
                        sig(act.activation(wt[:, 6 + j % 2, :], qkv[:, j, :], ACT.Square), "unit_sq")
                        ps = mid(act, ("unit", j))
                        if j >= 2:
                            act.wait_ge(sem("unit_done"), j - 1)
                        rt = gt[:, 2 + j % 2, :]
                        sig(act.activation(rt, ps[:, :], ACT.Ln, bias=4 * EPS), "unit_ln")
                        own("unit_ln")
                        sig(act.activation(rt, rt, ACT.Exp, scale=-0.5,
                                           bias=0.0 if j < H else float(-0.5 * np.log(P))), "unit_r")

                    def cv_():
                        u = DENSE[("cv",)]
                        slab(act, ("cv",), 3)
                        for t in range(ST):
                            sig(act.copy(cv[:, t, :], psD[(u + t) % 4][:, :]), "cv_in")

                    def ret(h):
                        sig(act.copy(oc[:, h, :], mid(act, ("ro", h))[:, :]), "oc")

                    def prep(n):
                        ps = mid(act, ("gb", n))
                        if n:
                            act.wait_ge(sem("St"), n)
                            act.wait_ge(sem("qs"), n)
                        else:
                            act.wait_ge(sem("x_saved"), 16)
                            act.wait_ge(sem("scaled"), ST)
                        sig(act.activation(B["eg"], ps[:, :], ACT.Exp), "eg")
                        act.wait_ge(sem("emin"), n + 1)
                        sig(act.activation(B["E"], B["E"], ACT.Exp), "E")
                        act.wait_ge(sem("glast"), n + 1)
                        sig(act.activation(egc, gc[:, n * H:(n + 1) * H], ACT.Exp), "esm")
                        act.wait_ge(sem("gdif"), n + 1)
                        sig(act.activation(kps, gdif, ACT.Exp), "esm")

                    def left(n, l):
                        if l > 1:
                            mid(act, ("xt", n, l - 1))
                        elif n:
                            mid(act, ("xt", n - 1, 6))
                        sig(act.copy(B["P1"], mid(act, ("p1", n, l))[:, :]), "P1")

                    def scan(n):
                        if n:
                            sig(act.mul(B["wTn"], mid(act, ("wT", n))[:, :], -1.0), "wTn")
                        sig(act.copy(B["vn"], mid(act, ("v2", n))[:, :]), "vnew")
                        act.wait_ge(sem("qs"), n + 1)
                        sig(act.copy(qkv[:, H:2 * H, cut(n)], heads(mid(act, ("oT", n))[:, :])), "ob")

                    def index(tb):
                        for i in range(IH):
                            ps = mid(act, ("il", tb, i))
                            q = IH * (tb - 1) + i
                            if q >= 2:
                                act.wait_ge(sem("score"), 9 * (tb - 1) + i - 1 if i >= 2 else 9 * (tb - 1))
                            sig(act.activation(rl[:, i % 2, 0:(tb + 1) * P], ps[:, 0:(tb + 1) * P], ACT.Relu,
                                               scale=0.125), "relu")

                    def soft(tb):
                        for h in range(H):
                            act.wait_ge(sem("nmax"), H * tb + h + 1)
                            w = slice(0, (tb + 1) * P)
                            sig(act.activation(pr[:, h, w], pr[:, h, w], ACT.Exp, scale=float(P) ** -0.5,
                                               bias=nmax[:, h:h + 1], accum_out=rsum[:, h:h + 1]), "sexp")

                    def attend(tb):
                        first = tb * (tb + 1) // 2
                        for m in range(tb + 1):
                            ps = mid(act, ("pt", tb, m))
                            if first + m >= 2:
                                act.wait_ge(sem("att_pv"), first + m - 1)
                            sig(act.copy(pt[:, (first + m) % 2, :], ps[:, :]), "pt")
                        sig(act.copy(qa[:, :, cut(tb)], heads(mid(act, ("ao", tb))[:, :])), "oa")

                    def fin(br, h):
                        b = "CAB".index(br)
                        if h == 0:
                            own({"C": "oc", "A": "oa", "B": "ob"}[br])
                            if b:
                                slab(act, *((("mergeC", 3), 0) if b == 1 else (("merge", "A", 3), 2)))
                        if br == "A":
                            sig(act.copy(y_hi[:, h, :], qa[:, h, :]), "y_hi")
                            return
                        if h == 0:
                            act.preload_act_table_set("natural_log_exp_and_others")
                        src = oc[:, h, :] if br == "C" else qkv[:, H + h, :]
                        f = FIN[br, h]
                        sq, rt, on = fin_scratch(f)
                        if f > 2:
                            act.wait_ge(sem("fin_n"), f - 2)
                        sig(act.activation(sq, src, ACT.Square), "fin_sq")
                        ps = mid(act, ("fin", br, h))
                        sig(act.activation(rt, ps[:, :], ACT.Ln, scale=1.0 / P, bias=EPS), "fin_ln")
                        own("fin_ln")
                        sig(act.activation(rt, rt, ACT.Exp, scale=-0.5), "fin_r")
                        act.wait_ge(sem("fy"), f)
                        sig(act.copy(y_hi[:, h, :], on), "y_hi")

                    def swish(kind, h):
                        slab(act, (kind, h))
                        if kind == "cg" and h == 0:
                            own("tanh")
                            act.wait_ge(sem("unit_done"), 2 * H)
                        if kind == "z" and h == 0:
                            act.wait_ge(sem("fin_n"), H)
                        dst = (gt if kind == "cg" else oc)[:, h, :]
                        sig(act.activation(dst, dbank((kind, h))[:, :], ACT.Tanh, scale=0.5), kind + "_t")

                    def gate(br, n):
                        slab(act, ("gate", br, n))
                        if n == 0:
                            act.wait_ge(sem("rot_done"), ROTS)
                        sig(act.activation(wt[:, n, :], dbank(("gate", br, n))[:, :], ACT.Tanh, scale=0.5), "gateC")

                    def merge(br, j):
                        for i in range(2):
                            n = 8 * "AB".index(br) + 2 * j + i
                            slab(act, ("merge", br, j), i)
                            if n == 0:
                                act.wait_ge(sem("fy"), H)
                            if n >= 4:
                                act.wait_ge(sem("gy"), KT + n - 3)
                            sig(act.activation(gt[:, n % 4, :], dbank(("merge", br, j), i)[:, :], ACT.Tanh,
                                               scale=0.5), "gtanh")

                    steps = {"norm": norm, "silu": silu, "decays": decays, "va": va_, "rot": rot,
                             "unit": unit, "cv": cv_, "ret": ret, "prep": prep, "left": left,
                             "scan": scan, "index": index, "soft": soft, "attend": attend, "fin": fin,
                             "gate": gate, "merge": merge}
                    for kind, *args in ORDER:
                        if kind in steps:
                            steps[kind](*args)
                        elif kind in ("cg", "z"):
                            swish(kind, *args)
                        if kind == "fin" and args == ["B", 3]:
                            act.dma_start(x[:].rearrange("p t d -> p (t d)"), x_state).then_inc(sem("x_back"), 16)
                            act.dma_start(pg[:, 0:2, :].rearrange("p a s -> p (a s)"),
                                          post[bass.ds(layer, 1)].rearrange("a p n -> (a p) n")[:, 0:D]) \
                                .then_inc(sem("gain_in"), 16)

                    slab(act, ("merge", "B", 3), 2)
                    act.preload_act_table_set("natural_log_exp_and_others")
                    for k in range(KT):
                        act.wait_ge(sem("merged"), KT + k + 1)
                        sig(act.mul(a_hi[:, k, :], wt[:, k, :], 0.5), "a_hi")
                    for half in range(2):
                        slab(act, f"out{half}", 3)
                        if half == 0:
                            act.wait_ge(sem("a_lo"), 2 * KT)
                        for t in range(ST):
                            sig(act.copy(wide[:, t, half * S:(half + 1) * S],
                                         psD[(DENSE[f"out{half}"] + t) % 4][:, :]), "mix_out")
                    own("mix_out")
                    rms_rows(wide, lambda t: None)
                    act.wait_ge(sem("mix_out"), 8)
                    rms_rows(x, lambda t: act.wait_ge(sem("x1"), t + 1))
                    hi_T("h2T", 2, par_("gmlp"))
                    act.wait_ge(sem("x1"), ST)
                    act.dma_start(post2[:], post[bass.ds(layer, 1)].rearrange("a p n -> (a p) n")[:, D:2 * D]) \
                        .then_inc(sem("gain2_in"), 16)
                    with act.Fori(0, GROUPS) as g:
                        act.wait_ge(sem("slab_done"), g * PER_GROUP + SL_MLP)
                        with act.Fori(0, FG // 4) as it:
                            for i in range(4):
                                act.wait_ge(sem("relu2"), g * FG + it * 4 + (i + 1))
                                act.copy(f_hi[:, bass.ds(it * 4 + i, 1), :].rearrange("p a s -> p (a s)"),
                                         gt[:, i, :]).then_inc(sem("f_hi"), 1)
                    for t in range(ST):
                        act.wait_ge(sem(f"acc_free{t}"), GROUPS + 1)
                        act.wait_ge(sem(f"hid_free{t}"), GROUPS + 1)
                    rms_rows(wide, lambda t: None)

                @block.vector
                def _(dve):
                    seen = {}

                    def sig(ins, name):
                        seen[name] = seen.get(name, 0) + 1
                        ins.then_inc(sem(name), 1)

                    def own(name):
                        dve.wait_ge(sem(name), seen[name])

                    def f32(ap):
                        return ap.bitcast(F32)

                    def norm_rows(gen):
                        dve.wait_ge(sem("rstd"), gen)
                        for t in range(ST):
                            sig(dve.tensor_scalar(wide[:, t, :], x[:, t, :], rstd[:, t:t + 1], None, ALU.mult), "scaled")

                    def lo_T(which, gen, gain):
                        for k in range(KT):
                            dve.wait_ge(sem("a_hi"), gen * KT + k + 1)
                            ps = psM[MID[which, k][0]]
                            sig(dve.scalar_tensor_tensor(out=a_lo[:, k, :], in0=ps[:, :], scalar=gain[:, k:k + 1],
                                                         in1=f32(a_hi[:, k, :]), op0=ALU.mult, op1=ALU.subtract), "a_lo")

                    def norm():
                        norm_rows(1)
                        dve.wait_ge(sem("pars_in"), 16)
                        sig(dve.tensor_scalar(ghalf, par_("gnorm"), 0.5, None, ALU.mult), "ghalf")
                        lo_T("hT", 0, par_("gmix"))

                    def conv(j):
                        slab(dve, ("conv", j))
                        ps, dst = dbank(("conv", j)), qkv[:, j, :]
                        cw = par_("conv")[:, CW * j:CW * j + CW]
                        sig(dve.tensor_scalar(dst, ps[:, :], cw[:, CW - 1:CW], None, ALU.mult), "tap")
                        for d in range(1, CW):
                            own("tap")
                            ins = dve.scalar_tensor_tensor(out=dst[:, d:], in0=ps[:, 0:S - d],
                                                           scalar=cw[:, CW - 1 - d:CW - d], in1=dst[:, d:],
                                                           op0=ALU.mult, op1=ALU.add)
                            sig(ins, "tap" if d < CW - 1 else "conv")

                    def silu(j):
                        dve.wait_ge(sem("tanh"), j + 1)
                        sig(dve.scalar_tensor_tensor(out=qkv[:, j, :], in0=gt[:, j % 2, :], scalar=1.0,
                                                     in1=qkv[:, j, :], op0=ALU.add, op1=ALU.mult), "silu")

                    def misc():
                        slab(dve, ("misc",))
                        ps = psD[DENSE[("misc",)] % 4][:, 0:ST * NMISC].rearrange("p (t n) -> p t n", t=ST)

                        def tiled(ap):
                            return ap.rearrange("p (t n) -> p t n", t=ST)

                        sig(dve.tensor_scalar(tiled(iw), ps[:, :, 0:IH], float(IH) ** -0.5, None, ALU.mult), "misc_in")
                        sig(dve.tensor_tensor(tiled(ab), ps[:, :, IH:IH + H],
                                              par_("dtb").unsqueeze(1).broadcast_to([P, ST, H]), ALU.add), "misc_in")
                        sig(dve.tensor_copy(tiled(bb_), ps[:, :, IH + H:]), "misc_in")
                        own("misc_in")
                        sig(dve.scalar_tensor_tensor(out=nab, in0=ab, scalar=-1.0, in1=ab, op0=ALU.mult,
                                                     op1=ALU.min), "misc_in")

                    def decays():
                        dve.wait_ge(sem("dec"), 4)
                        sig(dve.scalar_tensor_tensor(out=sp, in0=ab, scalar=0.0, in1=l1, op0=ALU.max, op1=ALU.add), "dd")
                        sig(dve.tensor_scalar(b1, eb, 1.0, None, ALU.add), "dd")
                        own("dd")
                        sig(dve.scalar_tensor_tensor(out=gg.rearrange("p (t n) -> p t n", t=ST),
                                                     in0=sp.rearrange("p (t n) -> p t n", t=ST), scalar=-1.0,
                                                     in1=ea.unsqueeze(1).broadcast_to([P, ST, H]),
                                                     op0=ALU.mult, op1=ALU.mult), "g")
                        sig(dve.reciprocal(beta, b1), "beta")
                        own("beta")
                        sig(dve.tensor_scalar(bhalf, beta, 0.5, None, ALU.mult), "beta")
                        ps = mid(dve, ("gcum",))
                        sig(dve.tensor_copy(gc, ps[:, 0:ST * H]), "gc")

                    def turn(r):
                        dst, kind = rot_dest(r)
                        dve.wait_ge(sem("rot_copy"), r + 1)
                        m1, m2 = wt[:, 2 + r % 2, :], wt[:, 4 + r % 2, :]
                        sig(dve.tensor_tensor(m1, wt[:, r % 2, :], T("cos" + kind), ALU.mult), "rot_cos")
                        ps = mid(dve, ("turn", r))
                        sig(dve.tensor_tensor(m2, ps[:, :], T("sin" + kind), ALU.mult), "rot_sin")
                        own("rot_cos")
                        own("rot_sin")
                        sig(dve.tensor_tensor(dst, m1, m2, ALU.add), "rot_done")

                    def unit(j):
                        dve.wait_ge(sem("unit_r"), j + 1)
                        sig(dve.tensor_tensor(qkv[:, j, :], qkv[:, j, :], gt[:, 2 + j % 2, :], ALU.mult), "unit_done")

                    def ret(h):
                        for m in range(ST):
                            i, w = ST * h + m, S - m * P
                            ps = mid(dve, ("rs", h, m))
                            if i >= 2:
                                dve.wait_ge(sem("ret_pv"), i - 1)
                            sig(dve.tensor_tensor(rp[:, i % 2, 0:w], ps[:, 0:w], T("decay", h, S)[:, 0:w],
                                                  ALU.mult), "ret_p")

                    def prep(n):
                        hh = slice(n * H, (n + 1) * H)
                        if n == 0:
                            own("beta")
                            own("gc")
                        sig(dve.tensor_tensor(heads(B["gtri"]), each(T("tri")), over(gg[:, hh], P), ALU.mult), "gb_in")
                        sig(dve.tensor_tensor(heads(B["bI"]), each(T("ident")), over(beta[:, hh], P), ALU.mult), "gb_in")
                        ps = mid(dve, ("gb", n))
                        dve.wait_ge(sem("eg"), n + 1)
                        sig(dve.tensor_tensor(heads(B["E"]), heads(ps[:, :]), over(gc[:, hh], P), ALU.subtract), "esub")
                        sig(dve.tensor_copy(glast, heads(ps[:, :])[:, :, P - 1]), "glast")
                        own("esub")
                        sig(dve.tensor_scalar(B["E"], B["E"], 0.0, None, ALU.min), "emin")
                        own("glast")
                        sig(dve.tensor_tensor(gdif, glast, gc[:, hh], ALU.subtract), "gdif")
                        ps = mid(dve, ("bb", n))
                        dve.wait_ge(sem("E"), n + 1)
                        sig(dve.tensor_tensor(B["MT"], B["E"], ps[:, :], ALU.mult), "MTb")
                        sig(dve.tensor_tensor(heads(B["AT"]), heads(B["E"]), each(T("tri")), ALU.mult), "ATm")
                        ps = mid(dve, ("kk", n))
                        own("MTb")
                        sig(dve.tensor_tensor(B["MT"], B["MT"], ps[:, :], ALU.mult), "MT")
                        own("MT")
                        sig(dve.tensor_tensor(heads(B["CT"]), heads(B["MT"]), each(T("level", 0, P)), ALU.mult), "CT")
                        ps = mid(dve, ("kq", n))
                        own("ATm")
                        sig(dve.tensor_tensor(B["AT"], B["AT"], ps[:, :], ALU.mult), "AT")
                        dve.wait_ge(sem("esm"), 2 * n + 2)
                        sig(dve.tensor_tensor(egl, beta[:, hh], egc, ALU.mult), "bk")
                        ps = mid(dve, ("kn", n))
                        own("bk")
                        sig(dve.tensor_tensor(heads(B["Kp"]), heads(ps[:, :]), over(egl, P), ALU.mult), "Kp")
                        sig(dve.tensor_tensor(heads(B["Kpp"]), heads(ps[:, :]), over(kps, P), ALU.mult), "Kpp")
                        ps = mid(dve, ("vn", n))
                        sig(dve.tensor_tensor(heads(B["vb"]), heads(ps[:, :]), over(bhalf[:, hh], P), ALU.mult), "vb")
                        dve.wait_ge(sem("eg"), n + 1)
                        sig(dve.tensor_tensor(heads(B["qs"]), qkv[:, H:2 * H, cut(n)], heads(B["eg"]), ALU.mult), "qs")

                    def pair(n):
                        own("CT")
                        ps = mid(dve, ("x0", n))
                        sig(dve.scalar_tensor_tensor(out=heads(B["X"]), in0=heads(ps[:, :]), scalar=-1.0,
                                                     in1=each(T("ident")), op0=ALU.mult, op1=ALU.add), "X")
                        sig(dve.scalar_tensor_tensor(out=heads(B["XT"]), in0=heads(B["CT"]), scalar=-1.0,
                                                     in1=each(T("ident")), op0=ALU.mult, op1=ALU.add), "XT")

                    def left(n, l):
                        if l > 1:
                            mid(dve, ("p1", n, l - 1))
                        own("XT")
                        sig(dve.tensor_tensor(heads(B["CT"]), heads(B["MT"]), each(T("level", l, P)), ALU.mult), "CT")

                    def right(n, l):
                        if l < 6:
                            ps = mid(dve, ("xx", n, l))
                            own("X")
                            sig(dve.tensor_tensor(B["X"], B["X"], ps[:, :], ALU.subtract), "X")
                        ps = mid(dve, ("xt", n, l))
                        sig(dve.tensor_tensor(B["XT"], B["XT"], ps[:, :], ALU.subtract), "XT")

                    def scan(n):
                        if n == ST - 1:
                            mid(dve, ("oT", n))
                            return
                        if n:
                            mid(dve, ("oT", n))
                            own("St")
                            sig(dve.tensor_tensor(heads(B["St"]), heads(B["St"]),
                                                  heads(B["eg"])[:, :, P - 1:P].broadcast_to([P, H, P]),
                                                  ALU.mult), "Sd")
                            ps = mid(dve, ("st", n))
                            own("Sd")
                            sig(dve.tensor_tensor(B["St"], B["St"], ps[:, :], ALU.add), "St")
                        else:
                            sig(dve.tensor_copy(B["St"], mid(dve, ("st", n))[:, :]), "St")

                    def index(tb):
                        w = slice(0, (tb + 1) * P)
                        for i in range(IH):
                            q = IH * (tb - 1) + i
                            dve.wait_ge(sem("relu"), q + 1)
                            ww = iw[:, tb * IH + i:tb * IH + i + 1]
                            if i == 0:
                                sig(dve.tensor_scalar(sc[:, w], rl[:, 0, w], ww, None, ALU.mult), "score")
                            else:
                                own("score")
                                sig(dve.scalar_tensor_tensor(out=sc[:, w], in0=rl[:, i % 2, w], scalar=ww,
                                                             in1=sc[:, w], op0=ALU.mult, op1=ALU.add), "score")
                        own("score")
                        sig(dve.tensor_tensor(sc[:, cut(tb)], sc[:, cut(tb)], T("maskadd"), ALU.add), "score")

                    def top(tb, part):
                        w = slice(0, (tb + 1) * P)
                        for r in range(part * TOPK // 32, (part + 1) * TOPK // 32):
                            src = sc if r == 0 else work
                            own("score" if r == 0 else "picked")
                            sig(dve.max(mx8, src[:, w]), "best")
                            own("best")
                            sig(dve.match_replace(work[:, w], mx8, src[:, w], GONE), "picked")
                        if part == 3:
                            own("picked")
                            sig(dve.tensor_tensor(negb[:, w], work[:, w], sc[:, w], ALU.is_equal), "kept")
                            own("kept")
                            sig(dve.tensor_scalar(negb[:, w], negb[:, w], NEG, None, ALU.mult), "negb")

                    def soft(tb):
                        w = slice(0, (tb + 1) * P)
                        bias = negb[:, w] if tb else T("maskadd")
                        if tb:
                            own("negb")
                            mid(dve, ("pt", tb - 1, tb - 1))
                        for h in range(H):
                            ps = mid(dve, ("as", tb, h))
                            sig(dve.tensor_tensor_reduce(pr[:, h, w], ps[:, w], bias, 1.0, GONE, ALU.add, ALU.max,
                                                         rmax[:, h:h + 1]), "smax")
                            own("smax")
                            sig(dve.tensor_scalar(nmax[:, h:h + 1], rmax[:, h:h + 1], -float(P) ** -0.5, None,
                                                  ALU.mult), "nmax")
                        for h in range(H):
                            dve.wait_ge(sem("sexp"), H * tb + h + 1)
                            sig(dve.reciprocal(rinv[:, h:h + 1], rsum[:, h:h + 1]), "rinv")
                            own("rinv")
                            sig(dve.tensor_scalar(pr[:, h, w], pr[:, h, w], rinv[:, h:h + 1], None, ALU.mult), "prob")

                    def fin(br, h):
                        b = "CAB".index(br)
                        if b and h == 0:
                            slab(dve, *((("mergeC", 3), 0) if b == 1 else (("merge", "A", 3), 2)))
                        if br == "A":
                            dve.wait_ge(sem("y_hi"), H * b + h + 1)
                            sig(dve.tensor_tensor(y_lo[:, h, :], qa[:, h, :], f32(y_hi[:, h, :]), ALU.subtract), "y_lo")
                            return
                        f = FIN[br, h]
                        src, gate_ = (oc[:, h, :], gt[:, h, :]) if br == "C" else (qkv[:, H + h, :], oc[:, h, :])
                        _, rt, on = fin_scratch(f)
                        dve.wait_ge(sem("fin_r"), f)
                        own("cg_w" if br == "C" else "z_w")
                        sig(dve.tensor_tensor(on, src, rt, ALU.mult), "fin_n")
                        own("fin_n")
                        sig(dve.scalar_tensor_tensor(out=on, in0=on, scalar=0.5 if br == "C" else ghalf, in1=gate_,
                                                     op0=ALU.mult, op1=ALU.mult), "fy")
                        dve.wait_ge(sem("y_hi"), H * b + h + 1)
                        sig(dve.tensor_tensor(y_lo[:, h, :], on, f32(y_hi[:, h, :]), ALU.subtract), "y_lo")

                    def swish(kind, h):
                        dst = (gt if kind == "cg" else oc)[:, h, :]
                        dve.wait_ge(sem(kind + "_t"), h + 1)
                        sig(dve.scalar_tensor_tensor(out=dst, in0=dst, scalar=1.0, in1=dbank((kind, h))[:, :],
                                                     op0=ALU.add, op1=ALU.mult), kind + "_w")

                    def mergeC(j):
                        slab(dve, ("mergeC", j))
                        for i in range(2):
                            n = 2 * j + i
                            dve.wait_ge(sem("gateC"), n + 1)
                            sig(dve.scalar_tensor_tensor(out=wt[:, n, :], in0=wt[:, n, :], scalar=1.0,
                                                         in1=dbank(("mergeC", j), i)[:, :],
                                                         op0=ALU.add, op1=ALU.mult), "gy")

                    def merge(br, j):
                        b = "AB".index(br)
                        slab(dve, ("merge", br, j), 2)
                        if "merged" in seen:
                            own("merged")
                        for i in range(2):
                            n = 8 * b + 2 * j + i
                            dve.wait_ge(sem("gtanh"), n + 1)
                            sig(dve.scalar_tensor_tensor(out=mt[:, n % 3, :], in0=gt[:, n % 4, :], scalar=1.0,
                                                         in1=dbank(("merge", br, j), 2 + i)[:, :],
                                                         op0=ALU.add, op1=ALU.mult), "gy")
                        own("gy")
                        for i in range(2):
                            n, m = 8 * b + 2 * j + i, wt[:, 2 * j + i, :]
                            sig(dve.tensor_tensor(m, m, mt[:, n % 3, :], ALU.add), "merged")

                    steps = {"norm": norm, "conv": conv, "silu": silu, "misc": misc, "decays": decays, "turn": turn,
                             "unit": unit, "ret": ret, "prep": prep, "pair": pair, "left": left, "right": right,
                             "scan": scan, "index": index, "top": top, "soft": soft, "fin": fin,
                             "mergeC": mergeC, "merge": merge}
                    for kind, *args in ORDER:
                        if kind in steps:
                            steps[kind](*args)
                        elif kind in ("cg", "z"):
                            swish(kind, *args)

                    for k in range(KT):
                        dve.wait_ge(sem("a_hi"), KT + k + 1)
                        sig(dve.scalar_tensor_tensor(out=a_lo[:, k, :], in0=wt[:, k, :], scalar=0.5,
                                                     in1=f32(a_hi[:, k, :]), op0=ALU.mult, op1=ALU.subtract), "a_lo")
                    def residual(gen, gain):
                        dve.wait_ge(sem("rstd"), gen)
                        for t in range(ST):
                            sig(dve.scalar_tensor_tensor(out=wide[:, t, :], in0=wide[:, t, :], scalar=rstd[:, t:t + 1],
                                                         in1=gain, op0=ALU.mult, op1=ALU.mult), "post")
                            own("post")
                            sig(dve.tensor_tensor(x[:, t, :], x[:, t, :], wide[:, t, :], ALU.add), "x1")

                    dve.wait_ge(sem("x_back"), 16)
                    dve.wait_ge(sem("gain_in"), 16)
                    residual(2, pg[:, 0:2, :].rearrange("p a s -> p (a s)"))
                    own("x1")
                    norm_rows(3)
                    lo_T("h2T", 2, par_("gmlp"))
                    mid(dve, ("h2T", KT - 1))
                    sig(dve.memset(wide[:], 0.0), "zeroed")
                    dve.wait_ge(sem("mix_out"), 8)
                    for t in range(ST):
                        dve.sem_inc(sem(f"hid_free{t}"), 1)
                        dve.sem_inc(sem(f"acc_free{t}"), 1)
                    own("zeroed")
                    with dve.Fori(0, GROUPS) as g:
                        with dve.Fori(0, FG // 4) as it:
                            for i in range(4):
                                dve.wait_ge(sem("slab_done"), g * PER_GROUP + it * 4 + (SL_MLP + i + 1))
                                dve.tensor_scalar(gt[:, i, :], psD[i][:, :], 0.0, None, ALU.max) \
                                    .then_inc(sem("relu1"), 1)
                                dve.wait_ge(sem("relu1"), g * FG + it * 4 + (i + 1))
                                dve.tensor_tensor(gt[:, i, :], gt[:, i, :], psD[i][:, :], ALU.mult) \
                                    .then_inc(sem("relu2"), 1)
                                dve.wait_ge(sem("f_hi"), g * FG + it * 4 + (i + 1))
                                dve.tensor_tensor(f_lo[:, bass.ds(it * 4 + i, 1), :].rearrange("p a s -> p (a s)"),
                                                  gt[:, i, :],
                                                  f32(f_hi[:, bass.ds(it * 4 + i, 1), :].rearrange("p a s -> p (a s)")),
                                                  ALU.subtract).then_inc(sem("f_lo"), 1)
                        for half in range(2):
                            dve.wait_ge(sem("slab_done"), g * PER_GROUP + (SL_MLP + FG + 8 * half + 8))
                            for t in range(ST):
                                w = wide[:, t, half * S:(half + 1) * S]
                                ps = (psM if half == 0 else psD)[t]
                                dve.tensor_tensor(w, w, ps[:, :], ALU.add) \
                                    .then_inc(sem(f"acc_free{t}" if half == 0 else f"hid_free{t}"), 1)
                        for t in range(ST):
                            dve.wait_ge(sem(f"acc_free{t}"), g + 2)
                            dve.wait_ge(sem(f"hid_free{t}"), g + 2)
                    dve.wait_ge(sem("gain2_in"), 16)
                    residual(4, post2[:])
                    own("x1")
            ids = [s.num for s in sems.values()]
            nc.all_engine_barrier(sems_to_clear=range(min(ids), max(ids) + 1))

        with nc.Block() as block:
            @block.sync
            def _(sp_):
                sp_.dma_start(out.rearrange("p (t d) -> p t d", t=ST), x[:]).then_inc(sem("x_out"), 16)
                sp_.wait_ge(sem("x_out"), 16)


def lay_out(i, a):
    f = np.float32
    w_in = a["w_in"][i]
    matrices = {"in": w_in, "branch": a["w_branch"][i], "out": a["w_out"][i], "up": a["w_up"][i],
                "down": a["w_down"][i],
                "misc": np.concatenate([w_in[:, I_W:I_W + IH], w_in[:, B_A:B_A + 2 * H]], 1),
                "ik": np.concatenate([w_in[:, I_K:I_K + 64]] * 2, 1)}
    slabs = np.zeros((NSLAB, P, SLAB), f)
    for to, (name, k0, ks, c0, n) in zip(slabs, HOLDS):
        to.reshape(P, ks, SLAB // ks)[:, :, :n] = \
            matrices[name][k0 * P:(k0 + ks) * P, c0:c0 + n].reshape(ks, P, n).transpose(1, 0, 2)
    return slabs


def kernel(**inputs):
    import concourse.bacc as bacc
    from concourse.bass_utils import run_bass_kernel_spmd as run

    a = {n: np.asarray(v) for n, v in inputs.items()}
    f = np.float32
    ws = np.concatenate([lay_out(i, a) for i in range(DEPTH)])
    par = np.zeros((DEPTH, P, NPAR), f)
    for i in range(DEPTH):
        for n, v in (("gmix", a["ln_mix_pre"][i].reshape(KT, P).T), ("gmlp", a["ln_mlp_pre"][i].reshape(KT, P).T),
                     ("conv", a["gdn_conv"][i].reshape(CW, 3, H, P)[:, [1, 0, 2]].reshape(CW, CONVS, P)
                      .transpose(2, 1, 0).reshape(P, -1)),
                     ("gnorm", a["gdn_norm"][i][:, None]), ("alog", np.broadcast_to(a["gdn_a_log"][i], (P, H))),
                     ("dtb", np.broadcast_to(a["gdn_dt_bias"][i], (P, H)))):
            par[i, :, PAR[n][0]:PAR[n][0] + PAR[n][1]] = v
    post = np.stack([np.concatenate([np.broadcast_to(a["ln_mix_post"][i], (P, D)),
                                     np.broadcast_to(a["ln_mlp_post"][i], (P, D))], 1) for i in range(DEPTH)])
    xs = np.ascontiguousarray(a["x"].reshape(ST, P, D).transpose(1, 0, 2).reshape(P, ST * D))
    arrays = {"in_ws": ws, "in_par": par, "in_post": np.ascontiguousarray(post), "in_tab": tables(), "in_x": xs}
    nc = bacc.Bacc("TRN2", target_bir_lowering=False, num_devices=1, dynamic_dma_scratch_size=1024)
    args = [nc.dram_tensor(n, v.shape, F32, kind="ExternalInput").ap() for n, v in arrays.items()]
    out = nc.dram_tensor("out", (P, ST * D), F32, kind="ExternalOutput").ap()
    build(nc, *args, out)
    r = run(nc, [arrays], core_ids=[0])
    return np.asarray(r.results[0]["out"]).reshape(P, ST, D).transpose(1, 0, 2).reshape(1, S, D)
```

```python
from contextlib import ExitStack

import numpy as np

import concourse.bass as bass
from concourse import mybir

F32 = mybir.dt.float32
F32R = mybir.dt.float32r
ALU = mybir.AluOpType
ACT = mybir.ActivationFunctionType
AX = mybir.AxisListType

P = 128
D = 1024
S = 512
DEPTH = 2
KT = D // P
ST = S // P
H = 4
IH = 8
TOPK = min(256, S // 4)
CW = 4
FF = 4 * D
EPS = 1e-6
NEG = -1e30
GONE = -3e38
SLAB = 1024

A_Q, A_K, A_V, I_Q, I_K, I_W = 0, 512, 640, 768, 1280, 1344
B_Q, B_K, B_V, B_A, B_B, B_Z = 1352, 1864, 2376, 2888, 2892, 2896
C_Q, C_K, C_V, C_G, GATES = 3408, 3664, 3920, 4432, 4944
NMISC = IH + 2 * H

GROUPS = 2
FG = FF // P // GROUPS
TOPS = 8
PER_GROUP = 2 * FG
ROTS = 14
CONVS = 3 * H

TAB = {}
_at = 0
for _name, _w in (("ident", P), ("ones", P), ("cosA", S), ("sinA", S), ("cosI", S), ("sinI", S), ("cosR", S), ("sinR", S), ("decay", H * S),
                  ("tri", P), ("maskadd", P),
                  ("level", 7 * P)):
    TAB[_name] = (_at, _w)
    _at += _w
NTAB = _at
PAR = {}
_at = 0
for _name, _w in (("gmix", KT), ("gmlp", KT), ("conv", CONVS * CW), ("gnorm", 1), ("alog", H), ("dtb", H)):
    PAR[_name] = (_at, _w)
    _at += _w
NPAR = _at


def tables():
    f = np.float32
    t = np.zeros((P, NTAB), f)

    def put(name, a):
        t[:, TAB[name][0]:TAB[name][0] + TAB[name][1]] = a

    pos = np.arange(S, dtype=f)
    row = np.arange(P)

    def rotation(inv, half, c, s):
        ang = (pos[None, :] * inv[:, None].astype(f)).astype(f).astype(np.float64)
        pick = row % half
        put(c, np.cos(ang)[pick])
        put(s, np.sin(ang)[pick] * np.where(row // half % 2 == 0, -1.0, 1.0)[:, None])

    rotation(f(10000.0) ** (-np.arange(0, 128, 2, dtype=f) / f(128)), 64, "cosA", "sinA")
    rotation(f(10000.0) ** (-np.arange(0, 64, 2, dtype=f) / f(64)), 32, "cosI", "sinI")
    rotation(f(1.0) / (f(10000.0) ** np.linspace(0.0, 1.0, 32, dtype=f)), 32, "cosR", "sinR")
    gamma = 1.0 - 2.0 ** (-5.0 - np.arange(H))
    rel = np.arange(S)[None, :] - row[:, None]
    put("decay", np.concatenate([np.where(rel >= 0, g ** np.maximum(rel, 0) * 0.125, 0.0) for g in gamma], 1))
    put("ident", np.eye(P))
    put("ones", 1.0)
    put("tri", row[:, None] <= row[None, :])
    put("maskadd", np.where(row[None, :] > row[:, None], NEG, 0.0))
    lv = []
    for l in range(7):
        a, b = row[:, None] >> l, row[None, :] >> l
        lv.append((b == a + 1) & (b % 2 == 1))
    put("level", np.concatenate(lv, 1))
    return t


def schedule():
    o = [("norm",), ("misc",)]
    for j in range(CONVS):
        o.append(("conv", j))
        if j == 0:
            o.append(("misc_turn",))
        if j >= 1:
            o.append(("silu", j - 1))
    o += [("va",), ("silu", CONVS - 1), ("unit_sq", 0), ("unit_sq", 1), ("decays",), ("rot", 0), ("va_turn",),
          ("gcum",)]
    for r in range(4):
        o.append(("rot", r + 1))
        for j in (2 * r, 2 * r + 1):
            o.append(("unit", j))
            if j + 2 < 2 * H:
                o.append(("unit_sq", j + 2))
        o.append(("turn", r))
        if r == 3:
            o.append(("pre", 0))

    slab = 2.6
    cost = {"pre": (0, 1.2, 0), "decay": (1.7, 3.6, 3.5), "prep": (3.6, 5.5, 0), "pair": (.4, 1.8, 0),
            "left": (.9, 0, .7), "right": (1.7, 1.3, 0), "scan_w": (.9, 0, .7), "scan_v": (1.7, 0, .7),
            "scan_o": (2.6, 1.2, .7), "ret": (4.3, 2.4, .7), "turn": (0, 1.2, 0), "index": (5.1, 5, .7),
            "top": (0, 2.4, 0), "soft": (2, 4, 4), "attend": (4, 0, 1.5), "fin_sq": (0, 0, .7), "fin": (.9, 1.2, 2),
            "split": (0, .6, .7), "cv": (slab, 0, .5), "rot": (slab, .6, 0), "cg": (slab, .7, .7),
            "z": (slab, .7, .7), "gate": (slab, 0, .7), "mgate": (slab, 0, .7), "mergeC": (slab, 1.2, 0),
            "merge": (slab, 2.4, 0)}
    chunks = []
    for n in range(ST):
        chunks += [("decay", n), ("prep", n), ("pair", n)]
        for l in range(1, 7):
            chunks += [("left", n, l), ("right", n, l)]
        if n + 1 < ST:
            chunks.append(("pre", n + 1))
        chunks += [("scan_w", n)] * (n > 0) + [("scan_v", n), ("scan_o", n)]
    retention = [("ret", h) for h in range(H)]
    retention += [("fin_sq", "C", 0), ("fin_sq", "C", 1), ("fin", "C", 0), ("fin", "C", 1), ("fin_sq", "C", 2),
                  ("fin_sq", "C", 3), ("fin", "C", 2), ("fin", "C", 3)]
    rotations = [("turn", r) for r in range(4, ROTS)]
    attention = []
    for tb in range(1, ST):
        attention += [("index", tb)] + [("top", tb, part) for part in range(TOPS)]
        for t in range(0 if tb == 1 else tb, tb + 1):
            attention += [("soft", t), ("attend", t)]
    attention += [("split", "C", h) for h in range(H)]
    dense = [("cv", i) for i in range(4)] + [("rot", r) for r in range(5, ROTS)] + [("cg", h) for h in range(H)]
    dense += [("gate", "C", n) for n in range(KT)]
    dense += [("mgate", "A", n) for n in range(4)] + [("mergeC", j) for j in range(4)]
    dense += [("split", "A", h) for h in range(H)] + [("z", h) for h in range(H)]

    def merges(b, early, last=2):
        return [s for j in range(4) for s in [("mgate", b, n) for n in range(early, KT)
                                              if (n // 2 if n // 2 < last else last) == j] + [("merge", b, j)]]

    dense += merges("A", 4, 3)
    after = {("ret", 0): [("cv", 3)], ("fin_sq", "C", 0): [("cg", 3)], ("index", 1): [("turn", 8), ("ret", H - 1)],
             ("soft", 0): [("turn", ROTS - 1)], ("gate", "C", 0): [("turn", ROTS - 1), ("fin", "C", 3)],
             ("cg", 0): [("unit", 7)], ("split", "C", 0): [("fin", "C", 3)], ("mergeC", 0): [("split", "C", 3)],
             ("z", 0): [("split", "C", 3)], ("mgate", "A", 0): [("fin", "C", 3)],
             ("split", "A", 0): [("attend", ST - 1), ("mergeC", 3)]}
    for r in range(5, ROTS):
        after["turn", r] = [("rot", r)]
    shifts = 2.2
    last = [("fin_sq", "B", h) for h in range(H)] + [("fin", "B", h) for h in range(H)]
    after["fin_sq", "B", 0] = [("z", H - 1)]
    dense = [s for d in dense for s in ([d] if d[0] == "split" else [("half", *d), d])]
    for s in list(after):
        if s in dense:
            after["half", *s] = after.pop(s)
    streams = [attention, rotations, chunks + last, retention, dense]
    free = [0.0, 0.0, 3.0, 0.0, 0.0]
    pe = dve = 0.0
    ends = {s: 0.0 for s in o}

    def ready(i):
        return max([free[i]] + [ends.get(s, 1e9) for s in after.get(streams[i][0], ())])

    while any(streams):
        left = [i for i in range(len(streams)) if streams[i]]
        i = next((i for i in left if ready(i) <= pe), None)
        if i is None:
            i = min(left, key=ready)
        at = ready(i)
        s = streams[i].pop(0)
        t, d, a = cost["cv" if s[0] == "half" else s[0]]
        if s[0] == "top":
            d = TOPK / TOPS / 4 * (0.06 + 0.135 * (s[1] + 1))
        if t:
            pe = max(pe, at) + t
        if d:
            dve = max(dve, at, pe + a if t or a else 0.0) + d
        ends[s] = (dve if d else max(pe, at) + a) + (shifts if s[0] == "rot" else 0)
        free[i] = pe if streams[i] is dense else ends[s] + 0.4
        o.append(s)
    o += [("split", "B", h) for h in range(H)] + merges("B", 0)
    return o


ORDER = schedule()


def slab_plan():
    number, holds = {}, []

    def add(step, *what):
        for i, w in enumerate(what):
            number[step, i] = len(holds)
            holds.append(w)

    for s in ORDER:
        k = s[0]
        if k == "conv":
            add(s, ("in", 0, KT, (B_K, B_Q, B_V)[s[1] // H] + s[1] % H * P, P))
        elif k == "misc":
            add(s, ("misc", 0, KT, 0, NMISC))
        elif k == "va":
            add(s, ("in", 0, KT, A_V, P))
        elif k == "rot":
            r = s[1]
            if r == 4:
                add(s, ("ik", 0, KT, 0, P))
            else:
                add(s, ("in", 0, KT, C_Q + r * P if r < 2 else C_K + (r - 2) * P if r < 4 else I_Q + (r - 5) * P
                        if r < 9 else A_K if r == 9 else A_Q + (r - 10) * P, P))
        elif k == "cv":
            add(s, ("in", 2 * s[1], 2, C_V, S))
        elif k == "cg":
            add(s, ("in", 0, KT, C_G + s[1] * P, P))
        elif k == "z":
            add(s, ("in", 0, KT, B_Z + s[1] * P, P))
        elif k == "gate":
            add(s, ("in", 0, KT, GATES + 2 * D + s[2] * P, P))
        elif k == "mergeC":
            add(s, ("branch", 2 * H, H, s[1] * 2 * P, 2 * P))
        elif k == "mgate":
            add(s, ("in", 0, KT, GATES + "AB".index(s[1]) * D + s[2] * P, P))
        elif k == "merge":
            add(s, ("branch", H * "AB".index(s[1]), H, s[2] * 2 * P, 2 * P))
    for half in range(2):
        add(f"out{half}", *(("out", i, 2, half * S, S) for i in range(0, KT, 2)))
    for g in range(GROUPS):
        add(f"group{g}", *(("up", 0, KT, (g * FG + i) * P, P) for i in range(FG)),
            *(("down", g * FG + i, 2, half * S, S) for half in range(2) for i in range(0, FG, 2)))
    return number, holds


SLAB_OF, HOLDS = slab_plan()
NSLAB = len(HOLDS)
SL_MLP = SLAB_OF["group0", 0]


def bank_plan():
    uses, last, turn, done = {}, [None] * 4, 0, 0

    def use(name, bank=None):
        nonlocal turn, done
        if bank is None:
            bank = turn % 3
            turn += 1
        if name[0] not in ("ro", "ao"):
            done += 1
        uses[name] = (bank, done, last[bank])
        last[bank] = name

    for s in ORDER:
        k = s[0]
        if k in ("unit", "va_turn", "misc_turn", "fin", "gcum"):
            use(s)
        elif k == "ret":
            use(("ro", s[1]), 3)
            for m in range(ST):
                use(("rs", s[1], m))
        elif k == "decay":
            for x in ("gb", "bb"):
                use((x, s[1]))
        elif k == "prep":
            for x in ("kk", "kq", "kn", "vn"):
                use((x, s[1]))
        elif k == "pair":
            use(("x0", s[1]))
        elif k == "left":
            use(("p1", s[1], s[2]))
        elif k == "right":
            for x in ("xx", "xt"):
                if x != "xx" or s[2] < 6:
                    use((x, s[1], s[2]))
        elif k == "scan_w":
            use(("wT", s[1]))
        elif k == "scan_v":
            use(("v2", s[1]))
        elif k == "scan_o":
            use(("oT", s[1]))
            if s[1] < ST - 1:
                use(("st", s[1]))
        elif k == "index":
            for i in range(IH):
                use(("il", s[1], i))
        elif k == "soft":
            for i in range(H):
                use(("as", s[1], i))
        elif k == "attend":
            use(("ao", s[1]), 3)
            for m in range(s[1] + 1):
                use(("pt", s[1], m))
    before_out = list(last)
    for i in range(KT):
        use(("h2T", i), 3)
    return uses, before_out


MID, BEFORE_OUT = bank_plan()
FIN = {(_b, _h): 4 * _i + _h + 1 for _i, _b in enumerate("CB") for _h in range(H)}


def dense_plan():
    uses, drain = {}, []

    def use(name, signals):
        uses[name] = len(drain)
        drain.extend(signals)

    for s in ORDER:
        k = s[0]
        if k == "conv":
            use(s, [("conv", s[1] + 1)])
        elif k == "misc":
            use(s, [("misc_T", 1)])
        elif k == "va":
            use(s, [("va_T", 1)])
        elif k == "rot":
            use(s, [("rot_copy", s[1] + 1)])
        elif k == "cv":
            if s[1] == 0:
                use(s, [("cv_in", t + 1) for t in range(ST)])
        elif k in ("cg", "z"):
            use(s, [(k + "_w", s[1] + 1)])
        elif k == "gate":
            use(s, [("gateC", s[2] + 1)])
        elif k == "mergeC":
            use(s, [("gy", 2 * s[1] + 1), ("gy", 2 * s[1] + 2)])
        elif k == "merge":
            n = 8 * "AB".index(s[1]) + 2 * s[2]
            use(s, [("gy", KT + n + 1), ("gy", KT + n + 2)])
        elif k == "mgate":
            use(s, [("gtanh", 8 * "AB".index(s[1]) + s[2] + 1)])
    assert len(drain) % 4 == 0
    use("out1", [("gained", ST + t + 1) for t in range(ST)])
    return uses, drain


DENSE, DRAIN = dense_plan()


def build(nc, ws, par, post, tab, x_in, out):
    with ExitStack() as ctx:
        def sb(name, shape, dt=F32, where=ctx):
            return where.enter_context(nc.sbuf_tensor(name, shape, dt))

        sems = {}

        def sem(name):
            if name not in sems:
                sems[name] = ctx.enter_context(nc.semaphore(name))
            return sems[name]

        kept = {n: ctx.enter_context(nc.semaphore(n)) for n in ("basics_in", "x_saved")}

        tabs = sb("tabs", [P, NTAB])
        pars = sb("pars", [P, NPAR])
        a_hi = sb("a_hi", [P, KT, S], F32R)
        a_lo = sb("a_lo", [P, KT, S], F32R)
        raw = sb("raw", [P, 2, SLAB])
        w_hi = sb("w_hi", [P, 2, SLAB], F32R)
        w_lo = sb("w_lo", [P, 2, SLAB], F32R)
        wide = sb("wide", [P, ST, D])
        wt = wide[:].rearrange("p t (a s) -> p (t a) s", a=2)
        gt = sb("gt", [P, 4, S])
        small = sb("small", [P, 512])
        x = sb("x", [P, ST, D])
        xw = x[:].rearrange("p t (a s) -> p (t a) s", a=2)

        with ExitStack() as mix:
            qkv = sb("qkv", [P, CONVS, S], where=mix)
            qa = sb("qa", [P, H, S], where=mix)
            ka = sb("ka", [P, S], where=mix)
            va = sb("va", [P, ST, P], where=mix)
            iq = sb("iq", [P, H, S], where=mix)
            ik = sb("ik", [P, S], where=mix)
            oc = sb("oc", [P, H, S], where=mix)
            bw = sb("bw", [P, 10, S], where=mix)
            with ExitStack() as u:
                cqk = sb("cqk", [P, 4, S], where=u)
                cv = sb("cv", [P, ST, S], where=u)
                rp = sb("rp", [P, 2, S], where=u)
            with ExitStack() as u:
                sc = sb("sc", [P, S], where=u)
                work = sb("work", [P, S], where=u)
                rl = sb("rl", [P, 2, S], where=u)
                negb = sb("negb", [P, S], where=u)
                pr = sb("pr", [P, H, S], where=u)
                pt = sb("pt", [P, 2, S], where=u)
            with ExitStack() as u:
                y_hi = sb("y_hi", [P, H, S], F32R, where=u)
                y_lo = sb("y_lo", [P, H, S], F32R, where=u)
                mt = sb("mt", [P, 3, S], where=u)
            pg = qkv
        with ExitStack() as mlp:
            f_hi = sb("f_hi", [P, FG, S], F32R, where=mlp)
            f_lo = sb("f_lo", [P, FG, S], F32R, where=mlp)
            post2 = sb("post2", [P, D], where=mlp)

        psD = [ctx.enter_context(nc.psum_tensor(f"psD{i}", [P, S], F32)) for i in range(4)]
        psM = [ctx.enter_context(nc.psum_tensor(f"psM{i}", [P, S], F32)) for i in range(4)]

        def T(name, i=0, w=None):
            a, n = TAB[name]
            w = w or n
            return tabs[:, a + i * w:a + (i + 1) * w]

        def par_(name):
            a, n = PAR[name]
            return pars[:, a:a + n]

        iw = small[:, 16:48]
        ab, nab, bb_ = small[:, 48:64], small[:, 64:80], small[:, 80:96]
        e1, l1, eb, sp = small[:, 96:112], small[:, 112:128], small[:, 128:144], small[:, 144:160]
        gg, beta, gc = small[:, 160:176], small[:, 176:192], small[:, 192:208]
        ea, bhalf, b1 = small[:, 208:212], small[:, 212:228], small[:, 228:244]
        glast, gdif, egl, egc, kps = (small[:, 244 + 4 * i:248 + 4 * i] for i in range(5))
        mx8 = small[:, 264:272]
        rmax, nmax, rsum, rinv = (small[:, 272 + 4 * i:276 + 4 * i] for i in range(4))
        bneg = small[:, 288:289]
        ghalf = small[:, 289:290]

        def norm_cols(norm, t):
            at = 296 + 28 * ("post_mix", "pre_mlp", "post_mlp", "pre_mix").index(norm) + 7 * t
            return [small[:, at + i:at + i + 1] for i in range(7)]

        def act_norm(act, sig, own, run=""):
            def squares(norm, t, part, src):
                if "any_sq" in sig.seen:
                    own(sig.seen["any_sq"])
                n = src.shape[-1] // S
                sq = gt[:, 0:n, :].rearrange("p a s -> p (a s)")
                sig(act.activation(sq, src, ACT.Square, accum_out=norm_cols(norm, t)[part]), "sq_" + norm + run)
                sig.seen["any_sq"] = "sq_" + norm + run

            def root(norm, t, parts):
                cols = norm_cols(norm, t)
                if parts == 2:
                    act.wait_ge(sem("sum_" + norm + run), t + 1)
                else:
                    own("sq_" + norm + run)
                v = cols[2 if parts == 2 else 0]
                sig(act.activation(cols[5], v, ACT.Ln, scale=1.0 / D, bias=EPS), "ln_" + norm + run)
                own("ln_" + norm + run)
                sig(act.activation(cols[4], cols[5], ACT.Exp, scale=-0.5), "r_" + norm + run)

            return squares, root

        def dve_norm(dve, sig, own, run=""):
            def total(norm, t):
                cols = norm_cols(norm, t)
                dve.wait_ge(sem("sq_" + norm + run), ST + t + 1)
                sig(dve.tensor_tensor(cols[2], cols[0], cols[1], ALU.add), "sum_" + norm + run)

            def rstd(norm, t, parts):
                cols = norm_cols(norm, t)
                dve.wait_ge(sem("r_" + norm + run), t + 1)
                v = cols[2 if parts == 2 else 0]
                sig(dve.tensor_scalar(cols[3], v, -0.5 / D, -0.5 * EPS, ALU.mult, ALU.add), "n1" + run)
                own("n1" + run)
                sig(dve.scalar_tensor_tensor(out=cols[5], in0=cols[4], scalar=cols[3], in1=cols[4],
                                             op0=ALU.mult, op1=ALU.mult), "n2" + run)
                own("n2" + run)
                sig(dve.scalar_tensor_tensor(out=cols[6], in0=cols[5], scalar=1.5, in1=cols[4],
                                             op0=ALU.add, op1=ALU.mult), "rstd" + run)
                own("rstd" + run)
                return cols[6]

            def diagonal(norm, t):
                r = rstd(norm, t, 1)
                sig(dve.tensor_scalar(wide[:, t, 0:P], T("ident"), r, None, ALU.mult), "diag_" + norm + run)

            return total, rstd, diagonal

        def signals(eng):
            seen = {}

            def sig(ins, name):
                seen[name] = seen.get(name, 0) + 1
                ins.then_inc(sem(name), 1)

            def own(name):
                eng.wait_ge(sem(name), seen[name])

            sig.seen = seen
            return seen, sig, own

        names = ["gtri", "bI", "E", "MT", "AT", "Kp", "Kpp", "vb", "qs", "X"]
        B = {n: bw[:, i, :] for i, n in enumerate(names)}
        for i, n in enumerate(["XT", "CT", "P1", "wTn", "vn", "eg", "St", "tmp"]):
            B[n] = xw[:, i, :]

        def heads(ap):
            return ap.rearrange("p (h c) -> p h c", h=H)

        def over(ap, n):
            return ap.unsqueeze(2).broadcast_to([P, H, n])

        def each(ap):
            return ap.unsqueeze(1).broadcast_to([P, H, P])

        def blocks(ap, l, odd):
            return ap.rearrange("p (m two b) -> p m two b", two=2, b=2 ** l)[:, :, odd, :]

        def packed(ps, l):
            return ps[:, 0:S // 2].rearrange("p (m b) -> p m b", b=2 ** l)

        def cut(n):
            return slice(n * P, (n + 1) * P)

        def rot_dest(r):
            if r < 4:
                return cqk[:, r, :], "R"
            if r == 4:
                return ik[:], "I"
            if r < 9:
                return iq[:, r - 5, :], "I"
            if r == 9:
                return ka[:], "A"
            return qa[:, r - 10, :], "A"

        def fin_parts(br, h):
            if br == "C":
                return oc[:, h, :], gt[:, h, :], wt[:, 6 + h % 2, :]
            return qkv[:, H + h, :], oc[:, h, :], bw[:, h, :]

        def drained(name):
            k, a = name[0], name[1:]
            if k == "h2T":
                return [("a_lo", 2 * KT + a[0] + 1)]
            if k == "gcum":
                return [("gc", 1)]
            if k == "unit":
                return [("unit_ln", a[0] + 1)]
            if k == "misc_turn":
                return [("misc_in", 3)]
            if k == "va_turn":
                return [("va_in", 1)]
            if k == "rs":
                return [("ret_p", ST * a[0] + a[1] + 1)]
            if k == "ro":
                return [("oc", a[0] + 1)]
            if k == "gb":
                return [("eg", a[0] + 1), ("glast", a[0] + 1)]
            if k == "bb":
                return [("MTb", a[0] + 1)]
            if k == "kk":
                return [("MT", a[0] + 1)]
            if k == "kq":
                return [("AT", a[0] + 1)]
            if k == "kn":
                return [("Kpp", a[0] + 1)]
            if k == "vn":
                return [("vb", a[0] + 1)]
            if k == "x0":
                return [("X", 6 * a[0] + 1)]
            if k == "p1":
                return [("P1", 6 * a[0] + a[1])]
            if k == "xx":
                return [("X", 6 * a[0] + a[1] + 1)]
            if k == "xt":
                return [("XT", 7 * a[0] + a[1] + 1)]
            if k == "wT":
                return [("wTn", a[0])]
            if k == "v2":
                return [("vnew", a[0] + 1)]
            if k == "oT":
                return [("ob", a[0] + 1)]
            if k == "st":
                return [("St", a[0] + 1)]
            if k == "il":
                return [("relu", IH * (a[0] - 1) + a[1] + 1)]
            if k == "as":
                return [("smax", H * a[0] + a[1] + 1)]
            if k == "pt":
                return [("pt", a[0] * (a[0] + 1) // 2 + a[1] + 1)]
            if k == "ao":
                return [("oa", a[0] + 1)]
            if k == "fin":
                return [("fin_ln", FIN[a])]
            raise ValueError(name)

        def mid(eng, name):
            if name[0] == "hT":
                return (psD + psM)[name[1]]
            if name[0] == "ro":
                eng.wait_ge(sem("ret_pv"), ST * name[1] + ST)
            elif name[0] == "ao":
                eng.wait_ge(sem("att_pv"), (name[1] + 1) * (name[1] + 2) // 2)
            else:
                eng.wait_ge(sem("small_done"), MID[name][1])
            if name[0] == "h2T":
                return (psM + psD)[name[1]]
            return psM[MID[name][0]]

        def slab(eng, step, i=0):
            eng.wait_ge(sem("slab_done"), SLAB_OF[step, i] + 1)

        def dbank(step, i=0):
            return psD[(DENSE[step] + i) % 4]

        def scaled_T(pe, ps, t, k):
            return pe.matmul(ps[:, cut(t)], x[:, t, cut(k)], wide[:, t, 0:P], start=True, stop=True)

        def activation_T(pe, run):
            for t in range(ST):
                pe.wait_ge(sem("diag_pre_mix" + run), t + 1)
                for k in range(KT):
                    scaled_T(pe, (psD + psM)[k], t, k)

        with nc.Block() as block:
            @block.sync
            def _(sp):
                basics = 2 * P
                sp.dma_start(tabs[:, 0:basics], tab[:, 0:basics]).then_inc(kept["basics_in"], 16)
                for t in range(ST):
                    sp.dma_start(x[:, t, :], x_in[:, t * D:(t + 1) * D]).then_inc(sem(f"x_in{t}"), 16)
                for s in range(2):
                    sp.dma_start(raw[:, s, :], ws[s]).then_inc(sem(f"first_raw_in{s}"), 16)
                sp.dma_start(pars[:], par[0]).then_inc(sem("first_pars_in"), 16)
                for t in range(ST):
                    sp.wait_ge(sem(f"x_in{t}"), 16)
                    sp.dma_start(out[:, t * D:(t + 1) * D], x[:, t, :]).then_inc(kept["x_saved"], 16)
                sp.wait_ge(sem("first_pars_in"), 16)

            @block.scalar
            def _(act):
                seen, sig, own = signals(act)
                squares, root = act_norm(act, sig, own, "_first")
                act.preload_act_table_set("natural_log_exp_and_others")
                for t in range(ST):
                    act.wait_ge(sem(f"x_in{t}"), 16)
                    squares("pre_mix", t, 0, x[:, t, :])
                    root("pre_mix", t, 1)

            @block.vector
            def _(dve):
                seen, sig, own = signals(dve)
                total, rstd, diagonal = dve_norm(dve, sig, own, "_first")
                dve.wait_ge(kept["basics_in"], 16)
                for t in range(ST):
                    diagonal("pre_mix", t)

            @block.gpsimd
            def _(pool):
                for s in range(2):
                    pool.wait_ge(sem(f"first_raw_in{s}"), 16)
                    pool.tensor_scalar(w_hi[:, s, :], raw[:, s, :], 1.0, 1.0, ALU.mult, ALU.mult) \
                        .then_inc(sem("first_w_hi"), 1)
                    pool.wait_ge(sem("first_w_hi"), s + 1)
                    pool.tensor_tensor(w_lo[:, s, :], raw[:, s, :], w_hi[:, s, :].bitcast(F32), ALU.subtract)

            @block.tensor
            def _(pe):
                activation_T(pe, "_first")

        with nc.Fori(0, DEPTH) as layer:
            with nc.Block() as block:
                @block.sync
                def _(sp):
                    def load(i, s):
                        sp.dma_start(raw[:, s, :], ws[bass.ds(layer * NSLAB + i, 1)].rearrange("a p n -> (a p) n")) \
                            .then_inc(sem(f"raw_in{s}"), 16)

                    for s in range(2):
                        load(2 + s, s)
                    sp.dma_start(tabs[:, 2 * P:], tab[:, 2 * P:]).then_inc(sem("tables_in"), 16)
                    with sp.Fori(2, NSLAB // 2 + 1) as it:
                        for s in range(2):
                            sp.wait_ge(sem("split"), it * 2 + (s - 3))
                            load(it * 2 + s, s)
                    for t in range(ST):
                        sp.wait_ge(sem("x2"), t + 1)
                        sp.dma_start(out[:, t * D:(t + 1) * D], x[:, t, :]).then_inc(kept["x_saved"], 16)

                @block.gpsimd
                def _(pool):
                    def split(i, s, turn):
                        pool.wait_ge(sem(f"raw_in{s}"), turn * 16)
                        pool.tensor_tensor(w_hi[:, s, 0:1], raw[:, s, 0:1], T("ones")[:, 0:1], ALU.mult)
                        pool.tensor_scalar(w_hi[:, s, 1:], raw[:, s, 1:], 1.0, 1.0, ALU.mult, ALU.mult) \
                            .then_inc(sem("w_hi"), 1)
                        pool.wait_ge(sem("w_hi"), i - 1)
                        pool.tensor_tensor(w_lo[:, s, :], raw[:, s, :], w_hi[:, s, :].bitcast(F32), ALU.subtract) \
                            .then_inc(sem("split"), 1)

                    for s in range(2):
                        pool.wait_ge(sem("slab_done"), s + 1)
                        split(2 + s, s, 1)
                    with pool.Fori(2, NSLAB // 2) as it:
                        for s in range(2):
                            pool.wait_ge(sem("slab_done"), it * 2 + (s - 1))
                            split(it * 2 + s, s, it)

                    def gained2(half):
                        for t in range(ST):
                            pool.wait_ge(sem("sq_post_mlp"), ST * half + t + 1)
                            w = wide[:, t, half * S:(half + 1) * S]
                            pool.tensor_tensor(w, w, post2[:, half * S:(half + 1) * S], ALU.mult) \
                                .then_inc(sem("gained2"), 1)

                    pool.wait_ge(sem("gain2_in"), 16)
                    gained2(0)
                    gained2(1)
                    for s in range(2):
                        pool.wait_ge(sem("slab_done"), NSLAB - 1 + s)
                        split(NSLAB + s, s, NSLAB // 2)

                @block.tensor
                def _(pe):
                    def passes(out, lhi, llo, rhi, rlo, start, stop):
                        pe.matmul(out, lhi, rhi, start=start, stop=False)
                        pe.matmul(out, lhi, rlo, start=False, stop=False)
                        return pe.matmul(out, llo, rhi, start=False, stop=stop)

                    def tslab(out, s, ka_=KT, off=0, step=P, y=False, n=P, ks=None):
                        ins = None
                        hi, lo = (y_hi, y_lo) if y else (a_hi, a_lo)
                        for k in ks or range(ka_):
                            c = slice(k * step + off, k * step + off + n)
                            ins = passes(out, w_hi[:, s, c], w_lo[:, s, c], hi[:, k, :], lo[:, k, :],
                                         k == 0, k == ka_ - 1)
                        return ins

                    def nslab(outs, s, k0, ks, n, first, last, hi=a_hi, lo=a_lo, ts=range(ST)):
                        ins = None
                        for t in ts:
                            for k in range(ks):
                                c = slice(k * (SLAB // ks), k * (SLAB // ks) + n)
                                ins = passes(outs[t], hi[:, k0 + k, cut(t)], lo[:, k0 + k, cut(t)],
                                             w_hi[:, s, c], w_lo[:, s, c],
                                             first and k == 0, last and k == ks - 1)
                        return ins

                    def slab_in(step, i=0):
                        if SLAB_OF[step, i] >= 2:
                            pe.wait_ge(sem("split"), SLAB_OF[step, i] - 1)
                        return SLAB_OF[step, i] % 2

                    def bank(u):
                        if u >= 4:
                            pe.wait_ge(sem(DRAIN[u - 4][0]), DRAIN[u - 4][1])
                        return psD[u % 4]

                    def done(ins):
                        ins.then_inc(sem("slab_done"), 1)

                    def small_bank(name):
                        b, _, before = MID[name]
                        if before is not None:
                            for s, v in drained(before):
                                pe.wait_ge(sem(s), v)
                        return psM[b]

                    def small_done(ins):
                        ins.then_inc(sem("small_done"), 1)

                    def by_heads(name, lhs, rhs):
                        ps = small_bank(name)
                        for h in range(H):
                            ins = pe.matmul(ps[:, cut(h)], lhs(h), rhs(h), start=True, stop=True)
                        small_done(ins)

                    def halves(name, lhs, rhs, l, odd):
                        ps = small_bank(name)
                        for h in range(H):
                            ins = pe.matmul(ps[:, h * P // 2:(h + 1) * P // 2], lhs[:, cut(h)],
                                            blocks(rhs[:, cut(h)], l, odd), start=True, stop=True)
                        small_done(ins)

                    def turn_heads(name, src):
                        ps = small_bank(name)
                        for h in range(H):
                            ins = pe.transpose(ps[:, cut(h)], src(h), T("ident"))
                        small_done(ins)

                    halved = set()

                    def dense_T(step):
                        if step in halved:
                            done(tslab(psD[DENSE[step] % 4][:, :], SLAB_OF[step, 0] % 2, ks=range(KT // 2, KT)))
                        else:
                            done(tslab(bank(DENSE[step])[:, :], slab_in(step)))

                    def half(*step):
                        halved.add(step)
                        if step[0] == "cv":
                            cv_tiles(step[1], range(ST // 2))
                        elif step[0] in ("merge", "mergeC"):
                            branch_columns(step, 0)
                        else:
                            tslab(bank(DENSE[step])[:, :], slab_in(step), ks=range(KT // 2))

                    def conv(j):
                        dense_T(("conv", j))

                    def misc():
                        s = slab_in(("misc",))
                        ps = bank(DENSE[("misc",)])
                        for k in range(KT):
                            pe.wait_ge(sem("a_lo"), k + 1)
                            ins = tslab(ps[0:NMISC, :], s, n=NMISC, ks=[k])
                        done(ins)

                    def misc_turn():
                        pe.wait_ge(sem("misc_T"), 1)
                        ps = small_bank(("misc_turn",))
                        for t in range(ST):
                            ins = pe.transpose(ps[:, t * NMISC:(t + 1) * NMISC], B["AT"][0:NMISC, cut(t)],
                                               T("ident")[0:NMISC, 0:NMISC])
                        small_done(ins)

                    def gcum():
                        pe.wait_ge(sem("tables_in"), 16)
                        pe.wait_ge(sem("g"), 1)
                        ps = small_bank(("gcum",))
                        small_done(pe.matmul(ps[:, 0:ST * H], T("tri"), gg, start=True, stop=True))

                    def va_():
                        dense_T(("va",))

                    def va_turn():
                        pe.wait_ge(sem("va_T"), 1)
                        turn_heads(("va_turn",), lambda t: B["X"][:, cut(t)])

                    def rot(r):
                        dense_T(("rot", r))

                    def unit(j):
                        if j == 0:
                            pe.wait_ge(sem("tables_in"), 16)
                        pe.wait_ge(sem("unit_sq"), j + 1)
                        ps = small_bank(("unit", j))
                        small_done(pe.matmul(ps[:, :], T("ones"), wt[:, 6 + j % 2, :], start=True, stop=True))

                    def cv_tiles(i, ts):
                        u = DENSE["cv", 0]
                        outs = {t: (bank(u + t) if i == 0 else psD[(u + t) % 4])[:, :] for t in ts}
                        return nslab(outs, slab_in(("cv", i)), 2 * i, 2, S, i == 0, i == 3, ts=ts)

                    def cv_(i):
                        done(cv_tiles(i, range(ST // 2 if ("cv", i) in halved else 0, ST)))

                    def ret(h):
                        hp = slice(64 * (h % 2), 64 * (h % 2) + 64)
                        pe.wait_ge(sem("rot_done"), 4)
                        pe.wait_ge(sem("cv_in"), ST)

                        def score(m):
                            ps = small_bank(("rs", h, m))
                            small_done(pe.matmul(ps[:, 0:S - m * P], cqk[hp, 2 + h // 2, cut(m)],
                                                 cqk[hp, h // 2, m * P:], start=True, stop=True))

                        def value(m, o):
                            i = ST * h + m
                            pe.wait_ge(sem("ret_p"), i + 1)
                            pe.matmul(o[:, m * P:], cv[:, m, cut(h)], rp[:, i % 2, 0:S - m * P],
                                      start=m == 0, stop=m == ST - 1).then_inc(sem("ret_pv"), 1)

                        o = small_bank(("ro", h))
                        score(0)
                        for m in range(1, ST):
                            score(m)
                            value(m - 1, o)
                        value(ST - 1, o)

                    def kB(h, n):
                        return qkv[:, h, cut(n)]

                    def decay(n):
                        for i, x_ in enumerate(("gb", "bb")):
                            pe.wait_ge(sem("gb_in"), 2 * n + i + 1)
                            ps = small_bank((x_, n))
                            small_done(pe.matmul(ps[:, :], T("ones"), B[("gtri", "bI")[i]], start=True, stop=True))

                    def prep(n):
                        pe.wait_ge(sem("unit_done"), 2 * H)
                        pe.wait_ge(sem("silu"), CONVS)
                        by_heads(("kk", n), lambda h: kB(h, n), lambda h: kB(h, n))
                        by_heads(("kq", n), lambda h: kB(h, n), lambda h: qkv[:, H + h, cut(n)])
                        turn_heads(("kn", n), lambda h: kB(h, n))
                        turn_heads(("vn", n), lambda h: qkv[:, 2 * H + h, cut(n)])

                    def pair(n):
                        pe.wait_ge(sem("CT"), 7 * n + 1)
                        turn_heads(("x0", n), lambda h: B["CT"][:, cut(h)])

                    def left(n, l):
                        pe.wait_ge(sem("CT"), 7 * n + l + 1)
                        pe.wait_ge(sem("X"), 6 * n + l)
                        by_heads(("p1", n, l), lambda h: B["CT"][:, cut(h)], lambda h: B["X"][:, cut(h)])

                    def right(n, l):
                        pe.wait_ge(sem("P1"), 6 * n + l)
                        pe.wait_ge(sem("XT"), 7 * n + l)
                        if l < 6:
                            halves(("xx", n, l), B["XT"], B["P1"], l, 0)
                        halves(("xt", n, l), B["P1"], B["XT"], l, 1)

                    def scan_w(n):
                        pe.wait_ge(sem("XT"), 7 * n + 7)
                        pe.wait_ge(sem("Kp"), n + 1)
                        by_heads(("wT", n), lambda h: B["Kp"][:, cut(h)], lambda h: B["XT"][:, cut(h)])

                    def scan_v(n):
                        pe.wait_ge(sem("XT"), 7 * n + 7)
                        pe.wait_ge(sem("vb"), n + 1)
                        if n:
                            pe.wait_ge(sem("wTn"), n)
                            pe.wait_ge(sem("St"), n)
                        ps = small_bank(("v2", n))
                        for h in range(H):
                            ins = pe.matmul(ps[:, cut(h)], B["XT"][:, cut(h)], B["vb"][:, cut(h)],
                                            start=True, stop=n == 0)
                            if n:
                                ins = pe.matmul(ps[:, cut(h)], B["wTn"][:, cut(h)], B["St"][:, cut(h)],
                                                start=False, stop=True)
                        small_done(ins)

                    def scan_o(n):
                        pe.wait_ge(sem("vnew"), n + 1)
                        pe.wait_ge(sem("AT"), n + 1)
                        pe.wait_ge(sem("qs"), n + 1)
                        ps = small_bank(("oT", n))
                        for h in range(H):
                            ins = pe.matmul(ps[:, cut(h)], B["vn"][:, cut(h)], B["AT"][:, cut(h)],
                                            start=True, stop=n == 0)
                            if n:
                                ins = pe.matmul(ps[:, cut(h)], B["St"][:, cut(h)], B["qs"][:, cut(h)],
                                                start=False, stop=True)
                        small_done(ins)
                        if n < ST - 1:
                            pe.wait_ge(sem("Kpp"), n + 1)
                            by_heads(("st", n), lambda h: B["Kpp"][:, cut(h)], lambda h: B["vn"][:, cut(h)])

                    def index(tb):
                        pe.wait_ge(sem("rot_done"), 9)
                        for i in range(IH):
                            hp = slice(64 * (i % 2), 64 * (i % 2) + 64)
                            ps = small_bank(("il", tb, i))
                            small_done(pe.matmul(ps[:, 0:(tb + 1) * P], iq[hp, i // 2, cut(tb)],
                                                 ik[hp, 0:(tb + 1) * P], start=True, stop=True))

                    def soft(tb):
                        pe.wait_ge(sem("rot_done"), ROTS)
                        for h in range(H):
                            ps = small_bank(("as", tb, h))
                            small_done(pe.matmul(ps[:, 0:(tb + 1) * P], qa[:, h, cut(tb)], ka[:, 0:(tb + 1) * P],
                                                 start=True, stop=True))

                    def attend(tb):
                        pe.wait_ge(sem("prob"), H * (tb + 1))
                        pe.wait_ge(sem("va_in"), 1)
                        first = tb * (tb + 1) // 2

                        def value(m, o):
                            pe.wait_ge(sem("pt"), first + m + 1)
                            pe.matmul(o[:, :], va[:, m, :], pt[:, (first + m) % 2, :],
                                      start=m == 0, stop=m == tb).then_inc(sem("att_pv"), 1)

                        o = small_bank(("ao", tb))
                        for m in range(tb + 1):
                            turn_heads(("pt", tb, m), lambda h: pr[:, h, cut(m)])
                            if m:
                                value(m - 1, o)
                        value(tb, o)

                    def fin(br, h):
                        pe.wait_ge(sem("fin_sq"), FIN[br, h])
                        ps = small_bank(("fin", br, h))
                        small_done(pe.matmul(ps[:, :], T("ones"), fin_parts(br, h)[2], start=True, stop=True))

                    def branch_columns(step, i):
                        s = slab_in(step)
                        b = 0 if step[0] == "mergeC" else 1 + "AB".index(step[1])
                        pe.wait_ge(sem("y_lo"), H * b + H)
                        return tslab(bank(DENSE[step] + i)[:, :], s, ka_=H, off=i * P, step=2 * P, y=True)

                    def branch(step):
                        if step not in halved:
                            branch_columns(step, 0)
                        done(branch_columns(step, 1))

                    def mergeC(j):
                        branch(("mergeC", j))

                    def merge(br, j):
                        branch(("merge", br, j))

                    steps = {"half": half, "conv": conv, "misc": misc, "misc_turn": misc_turn, "gcum": gcum,
                             "va": va_, "rot": rot,
                             "unit": unit, "va_turn": va_turn, "cv": cv_, "ret": ret, "decay": decay,
                             "prep": prep, "pair": pair, "left": left, "right": right, "scan_w": scan_w,
                             "scan_v": scan_v, "scan_o": scan_o, "index": index, "soft": soft,
                             "attend": attend, "fin": fin, "merge": merge, "mergeC": mergeC}
                    for kind, *args in ORDER:
                        if kind in steps:
                            steps[kind](*args)
                        elif kind in ("cg", "z", "gate", "mgate"):
                            dense_T((kind, *args))

                    for i in range(4):
                        if i == 0:
                            for b in range(4):
                                for name, v in drained(BEFORE_OUT[b]):
                                    pe.wait_ge(sem(name), v)
                        pe.wait_ge(sem("a_lo"), KT + 2 * i + 2)
                        done(nslab([psM[t][:, :] for t in range(ST)], slab_in("out0", i), 2 * i, 2, S, i == 0, i == 3))
                    outs = [bank(DENSE["out1"] + t)[:, :] for t in range(ST)]
                    assert DENSE["out1"] % 4 == 0
                    for i in range(3):
                        done(nslab(outs, slab_in("out1", i), 2 * i, 2, S, i == 0, False))
                    s = slab_in("out1", 3)
                    for t in range(ST):
                        ins = nslab(outs, s, 6, 2, S, False, True, ts=[t])
                        if t < ST - 1:
                            ins.then_inc(sem("out_tile"), 1)
                    done(ins)

                    pe.wait_ge(sem("gained"), ST)
                    for t in range(ST - 1):
                        pe.wait_ge(sem("diag_pre_mlp"), t + 1)
                        for k in range(KT):
                            if t == 0 and k == 4:
                                pe.wait_ge(sem("gained"), 2 * ST)
                            scaled_T(pe, (psM + psD)[k], t, k)
                    pe.wait_ge(sem("diag_pre_mlp"), ST)
                    for k in range(KT):
                        small_done(scaled_T(pe, (psM + psD)[k], ST - 1, k))
                    with pe.Fori(0, GROUPS) as g:
                        for i in range(4):
                            pe.wait_ge(sem("split"), g * PER_GROUP + (SL_MLP + i - 1))
                            pe.wait_ge(sem(f"hid_free{i}"), g + 1)
                            if i == 0:
                                for k in range(KT):
                                    pe.wait_ge(sem("a_lo"), 2 * KT + k + 1)
                                    ins = tslab(psM[0][:, :], 0, ks=[k])
                                done(ins)
                            else:
                                done(tslab(psM[i][:, :], i % 2))
                        with pe.Fori(1, FG // 4) as it:
                            for i in range(4):
                                pe.wait_ge(sem("split"), g * PER_GROUP + it * 4 + (SL_MLP + i - 1))
                                pe.wait_ge(sem("relu2"), g * FG + it * 4 + (i - 3))
                                done(tslab(psM[i][:, :], i % 2))
                        for half in range(2):
                            outs = [(psD if half == 0 else psM)[t][:, :] for t in range(ST)]
                            for t in range(ST):
                                if half == 0:
                                    pe.wait_ge(sem(f"acc_free{t}"), g + 1)
                                else:
                                    pe.wait_ge(sem("relu2"), g * FG + (FG - 3 + t))
                            for i in range(FG // 2):
                                if half == 0:
                                    pe.wait_ge(sem("f_lo"), g * FG + (2 * i + 2))
                                pe.wait_ge(sem("split"), g * PER_GROUP + (SL_MLP + FG + 8 * half + i - 1))
                                for t in range(ST):
                                    ins = nslab(outs, i % 2, 2 * i, 2, S, i == 0, i == FG // 2 - 1, hi=f_hi, lo=f_lo,
                                                ts=[t])
                                    if half == 1 and i == FG // 2 - 1 and t < ST - 1:
                                        ins.then_inc(sem("down_tile"), 1)
                                done(ins)
                    for t in range(ST):
                        pe.wait_ge(sem(f"acc_free{t}"), GROUPS + 1)
                        pe.wait_ge(sem(f"hid_free{t}"), GROUPS + 1)
                    activation_T(pe, "")

                @block.scalar
                def _(act):
                    seen, sig, own = signals(act)
                    squares, root = act_norm(act, sig, own)

                    def hi_T(which, gen, gain):
                        for k in range(KT):
                            ps = mid(act, (which, k))
                            sig(act.activation(a_hi[:, k, :], ps[:, :], ACT.Copy, scale=gain[:, k:k + 1]), "a_hi")


                    def norm():
                        hi_T("hT", 0, par_("gmix"))

                    def silu(j):
                        act.wait_ge(sem("conv"), j + 1)
                        if j >= 2:
                            act.wait_ge(sem("silu"), j - 1)
                        sig(act.activation(gt[:, j % 2, :], qkv[:, j, :], ACT.Tanh, scale=0.5), "tanh")

                    def decays():
                        act.preload_act_table_set("natural_log_exp_and_others")
                        act.wait_ge(sem("misc_in"), 4)
                        sig(act.activation(e1, nab, ACT.Exp), "dec")
                        own("dec")
                        sig(act.activation(l1, e1, ACT.Ln, bias=1.0), "dec")
                        sig(act.activation(ea, par_("alog"), ACT.Exp), "dec")
                        sig(act.activation(eb, bb_, ACT.Exp, scale=-1.0), "dec")

                    def misc():
                        slab(act, ("misc",))
                        sig(act.copy(B["AT"][0:NMISC, :], dbank(("misc",))[0:NMISC, :]), "misc_T")

                    def va_():
                        slab(act, ("va",))
                        sig(act.copy(B["X"], dbank(("va",))[:, :]), "va_T")

                    def va_turn():
                        sig(act.copy(va[:].rearrange("p t d -> p (t d)"), mid(act, ("va_turn",))[:, :]), "va_in")

                    def rot(r):
                        act.wait_ge(sem("rot_cos"), r + 1)
                        if r >= 2:
                            act.wait_ge(sem("rot_done"), r - 1)
                        n = 64 if r >= 9 else 32
                        for to in range(0, P, n):
                            at = to + n if to // n % 2 == 0 else to - n
                            sig(act.copy(wt[to:to + n, r % 2, :], dbank(("rot", r))[at:at + n, :]),
                                "rot_copy" if to + n == P else "rot_part")

                    def unit_sq(j):
                        if j >= 2:
                            mid(act, ("unit", j - 2))
                        act.wait_ge(sem("silu"), j + 1)
                        sig(act.activation(wt[:, 6 + j % 2, :], qkv[:, j, :], ACT.Square), "unit_sq")

                    def unit(j):
                        ps = mid(act, ("unit", j))
                        if j >= 2:
                            act.wait_ge(sem("unit_done"), j - 1)
                        rt = gt[:, 2 + j % 2, :]
                        sig(act.activation(rt, ps[:, :], ACT.Ln, bias=4 * EPS), "unit_ln")
                        own("unit_ln")
                        sig(act.activation(rt, rt, ACT.Exp, scale=-0.5,
                                           bias=0.0 if j < H else float(-0.5 * np.log(P))), "unit_r")

                    def cv_(i):
                        if i < 3:
                            return
                        u = DENSE["cv", 0]
                        slab(act, ("cv", 3))
                        for t in range(ST):
                            sig(act.copy(cv[:, t, :], psD[(u + t) % 4][:, :]), "cv_in")

                    def ret(h):
                        sig(act.copy(oc[:, h, :], mid(act, ("ro", h))[:, :]), "oc")

                    def decay(n):
                        ps = mid(act, ("gb", n))
                        if n:
                            act.wait_ge(sem("St"), n)
                            act.wait_ge(sem("qs"), n)
                        else:
                            act.wait_ge(kept["x_saved"], layer * (16 * ST) + 16 * ST)
                        sig(act.activation(B["eg"], ps[:, :], ACT.Exp), "eg")
                        act.wait_ge(sem("emin"), n + 1)
                        sig(act.activation(B["E"], B["E"], ACT.Exp), "E")
                        act.wait_ge(sem("glast"), n + 1)
                        sig(act.activation(egc, gc[:, n * H:(n + 1) * H], ACT.Exp), "esm")
                        act.wait_ge(sem("gdif"), n + 1)
                        sig(act.activation(kps, gdif, ACT.Exp), "esm")

                    def left(n, l):
                        if l > 1:
                            mid(act, ("xt", n, l - 1))
                        elif n:
                            mid(act, ("xt", n - 1, 6))
                        sig(act.copy(B["P1"], mid(act, ("p1", n, l))[:, :]), "P1")

                    def scan_w(n):
                        sig(act.mul(B["wTn"], mid(act, ("wT", n))[:, :], -1.0), "wTn")

                    def scan_v(n):
                        sig(act.copy(B["vn"], mid(act, ("v2", n))[:, :]), "vnew")

                    def scan_o(n):
                        act.wait_ge(sem("qs"), n + 1)
                        sig(act.copy(qkv[:, H:2 * H, cut(n)], heads(mid(act, ("oT", n))[:, :])), "ob")

                    def index(tb):
                        for i in range(IH):
                            ps = mid(act, ("il", tb, i))
                            q = IH * (tb - 1) + i
                            if q >= 2:
                                act.wait_ge(sem("score"), 9 * (tb - 1) + i - 1 if i >= 2 else 9 * (tb - 1))
                            sig(act.activation(rl[:, i % 2, 0:(tb + 1) * P], ps[:, 0:(tb + 1) * P], ACT.Relu,
                                               scale=0.125), "relu")

                    def soft(tb):
                        for h in range(H):
                            act.wait_ge(sem("nmax"), H * tb + h + 1)
                            w = slice(0, (tb + 1) * P)
                            sig(act.activation(pr[:, h, w], pr[:, h, w], ACT.Exp, scale=float(P) ** -0.5,
                                               bias=nmax[:, h:h + 1], accum_out=rsum[:, h:h + 1]), "sexp")

                    def attend(tb):
                        first = tb * (tb + 1) // 2
                        for m in range(tb + 1):
                            ps = mid(act, ("pt", tb, m))
                            if first + m >= 2:
                                act.wait_ge(sem("att_pv"), first + m - 1)
                            sig(act.copy(pt[:, (first + m) % 2, :], ps[:, :]), "pt")
                        sig(act.copy(qa[:, :, cut(tb)], heads(mid(act, ("ao", tb))[:, :])), "oa")

                    def fin_sq(br, h):
                        src, _, sq = fin_parts(br, h)
                        act.wait_ge(sem("oc" if br == "C" else "ob"), h + 1 if br == "C" else ST)
                        if br == "C" and h == 0:
                            act.wait_ge(sem("unit_done"), 2 * H)
                        if br == "C" and h >= 2:
                            act.wait_ge(sem("fin_n"), FIN[br, h] - 2)
                        sig(act.activation(sq, src, ACT.Square), "fin_sq")

                    def fin(br, h):
                        if h == 0:
                            act.preload_act_table_set("natural_log_exp_and_others")
                        sq = fin_parts(br, h)[2]
                        ps = mid(act, ("fin", br, h))
                        sig(act.activation(sq, ps[:, :], ACT.Ln, scale=1.0 / P, bias=EPS), "fin_ln")
                        own("fin_ln")
                        sig(act.activation(sq, sq, ACT.Exp, scale=-0.5), "fin_r")

                    def split_y(br, h):
                        b = "CAB".index(br)
                        if h == 0:
                            own("oa")
                            if b:
                                slab(act, (("mergeC", 3), ("merge", "A", 3))[b - 1])
                        if br != "A":
                            act.wait_ge(sem("fy"), FIN[br, h])
                        src = (oc[:, h, :], qa[:, h, :], qkv[:, H + h, :])[b]
                        sig(act.copy(y_hi[:, h, :], src), "y_hi")

                    def swish(kind, h):
                        slab(act, (kind, h))
                        if kind == "cg" and h == 0:
                            own("tanh")
                            act.wait_ge(sem("unit_done"), 2 * H)
                        if kind == "z" and h == 0:
                            act.wait_ge(sem("y_lo"), H)
                        dst = (gt if kind == "cg" else oc)[:, h, :]
                        sig(act.activation(dst, dbank((kind, h))[:, :], ACT.Tanh, scale=0.5), kind + "_t")

                    def gate(br, n):
                        slab(act, ("gate", br, n))
                        if n == 0:
                            act.wait_ge(sem("rot_done"), ROTS)
                            act.wait_ge(sem("fin_n"), H)
                        sig(act.activation(wt[:, n, :], dbank(("gate", br, n))[:, :], ACT.Tanh, scale=0.5), "gateC")

                    def mgate(br, n):
                        slab(act, ("mgate", br, n))
                        n += 8 * "AB".index(br)
                        if n == 0:
                            act.wait_ge(sem("fy"), H)
                        if n >= 4:
                            act.wait_ge(sem("gy"), KT + n - 3)
                        sig(act.activation(gt[:, n % 4, :], dbank(("mgate", br, n % 8))[:, :], ACT.Tanh, scale=0.5),
                            "gtanh")

                    steps = {"norm": norm, "silu": silu, "decays": decays, "va": va_, "rot": rot,
                             "unit_sq": unit_sq, "unit": unit, "misc": misc, "va_turn": va_turn, "cv": cv_, "ret": ret,
                             "decay": decay, "left": left, "scan_w": scan_w, "scan_v": scan_v, "scan_o": scan_o,
                             "index": index, "soft": soft, "attend": attend, "fin_sq": fin_sq, "fin": fin,
                             "split": split_y, "gate": gate, "mgate": mgate}
                    for kind, *args in ORDER:
                        if kind in steps:
                            steps[kind](*args)
                        elif kind in ("cg", "z"):
                            swish(kind, *args)
                        if kind == "split" and args == ["B", H - 1]:
                            act.dma_start(x[:].rearrange("p t d -> p (t d)"), out).then_inc(sem("x_back"), 16)
                            act.dma_start(pg[:, 0:2, :].rearrange("p a s -> p (a s)"),
                                          post[bass.ds(layer, 1)].rearrange("a p n -> (a p) n")[:, 0:D]) \
                                .then_inc(sem("gain_in"), 16)

                    slab(act, ("mgate", "B", KT - 1))
                    act.preload_act_table_set("natural_log_exp_and_others")
                    for k in range(KT):
                        act.wait_ge(sem("merged"), KT + k + 1)
                        sig(act.mul(a_hi[:, k, :], wt[:, k, :], 0.5), "a_hi")
                    slab(act, "out0", 3)
                    for t in range(ST):
                        squares("post_mix", t, 0, psM[t][:, :])
                    act.wait_ge(sem("a_lo"), 2 * KT)
                    for t in range(ST + 3):
                        if t < ST:
                            if t < ST - 1:
                                act.wait_ge(sem("out_tile"), t + 1)
                            else:
                                slab(act, "out1", 3)
                            squares("post_mix", t, 1, psD[t][:, :])
                        if 0 < t <= ST:
                            root("post_mix", t - 1, 2)
                        if t > 2:
                            act.wait_ge(sem("x1"), t - 2)
                            squares("pre_mlp", t - 3, 0, x[:, t - 3, :])
                            root("pre_mlp", t - 3, 1)
                    hi_T("h2T", 2, par_("gmlp"))
                    act.wait_ge(sem("a_lo"), 3 * KT)
                    act.dma_start(pars[:], par[bass.ds(layer + 1, 1)].rearrange("a p n -> (a p) n")) \
                        .then_inc(sem("pars_in"), 16)
                    act.wait_ge(sem("x1"), ST)
                    act.dma_start(post2[:], post[bass.ds(layer, 1)].rearrange("a p n -> (a p) n")[:, D:2 * D]) \
                        .then_inc(sem("gain2_in"), 16)
                    with act.Fori(0, GROUPS) as g:
                        act.wait_ge(sem("slab_done"), g * PER_GROUP + SL_MLP)
                        with act.Fori(0, FG // 4) as it:
                            for i in range(4):
                                act.wait_ge(sem("relu2"), g * FG + it * 4 + (i + 1))
                                act.copy(f_hi[:, bass.ds(it * 4 + i, 1), :].rearrange("p a s -> p (a s)"),
                                         gt[:, i, :]).then_inc(sem("f_hi"), 1)
                    for t in range(ST):
                        act.wait_ge(sem(f"acc_free{t}"), GROUPS + 1)
                        squares("post_mlp", t, 0, wide[:, t, 0:S])
                    for t in range(ST + 3):
                        if t < ST:
                            act.wait_ge(sem(f"hid_free{t}"), GROUPS + 1)
                            squares("post_mlp", t, 1, wide[:, t, S:D])
                        if 0 < t <= ST:
                            root("post_mlp", t - 1, 2)
                        if t > 2:
                            act.wait_ge(sem("x2"), t - 2)
                            squares("pre_mix", t - 3, 0, x[:, t - 3, :])
                            root("pre_mix", t - 3, 1)
                    act.wait_ge(sem("pars_in"), 16)

                @block.vector
                def _(dve):
                    seen, sig, own = signals(dve)
                    total, rstd, diagonal = dve_norm(dve, sig, own)

                    def f32(ap):
                        return ap.bitcast(F32)

                    def lo_tile(which, gen, k, gain):
                        dve.wait_ge(sem("a_hi"), gen * KT + k + 1)
                        ps = mid(dve, (which, k))
                        sig(dve.scalar_tensor_tensor(out=a_lo[:, k, :], in0=ps[:, :], scalar=gain[:, k:k + 1],
                                                     in1=f32(a_hi[:, k, :]), op0=ALU.mult, op1=ALU.subtract), "a_lo")

                    def norm():
                        sig(dve.tensor_scalar(ghalf, par_("gnorm"), 0.5, None, ALU.mult), "ghalf")
                        for k in range(KT):
                            lo_tile("hT", 0, k, par_("gmix"))

                    def conv(j):
                        slab(dve, ("conv", j))
                        ps, dst = dbank(("conv", j)), qkv[:, j, :]
                        cw = par_("conv")[:, CW * j:CW * j + CW]
                        sig(dve.tensor_scalar(dst, ps[:, :], cw[:, CW - 1:CW], None, ALU.mult), "tap")
                        for d in range(1, CW):
                            own("tap")
                            ins = dve.scalar_tensor_tensor(out=dst[:, d:], in0=ps[:, 0:S - d],
                                                           scalar=cw[:, CW - 1 - d:CW - d], in1=dst[:, d:],
                                                           op0=ALU.mult, op1=ALU.add)
                            sig(ins, "tap" if d < CW - 1 else "conv")

                    def silu(j):
                        dve.wait_ge(sem("tanh"), j + 1)
                        sig(dve.scalar_tensor_tensor(out=qkv[:, j, :], in0=gt[:, j % 2, :], scalar=1.0,
                                                     in1=qkv[:, j, :], op0=ALU.add, op1=ALU.mult), "silu")

                    def misc_turn():
                        ps = mid(dve, ("misc_turn",))[:, 0:ST * NMISC].rearrange("p (t n) -> p t n", t=ST)

                        def tiled(ap):
                            return ap.rearrange("p (t n) -> p t n", t=ST)

                        sig(dve.tensor_scalar(tiled(iw), ps[:, :, 0:IH], float(IH) ** -0.5, None, ALU.mult), "misc_in")
                        sig(dve.tensor_tensor(tiled(ab), ps[:, :, IH:IH + H],
                                              par_("dtb").unsqueeze(1).broadcast_to([P, ST, H]), ALU.add), "misc_in")
                        sig(dve.tensor_copy(tiled(bb_), ps[:, :, IH + H:]), "misc_in")
                        own("misc_in")
                        sig(dve.scalar_tensor_tensor(out=nab, in0=ab, scalar=-1.0, in1=ab, op0=ALU.mult,
                                                     op1=ALU.min), "misc_in")

                    def decays():
                        dve.wait_ge(sem("dec"), 4)
                        sig(dve.scalar_tensor_tensor(out=sp, in0=ab, scalar=0.0, in1=l1, op0=ALU.max, op1=ALU.add), "dd")
                        sig(dve.tensor_scalar(b1, eb, 1.0, None, ALU.add), "dd")
                        own("dd")
                        sig(dve.scalar_tensor_tensor(out=gg.rearrange("p (t n) -> p t n", t=ST),
                                                     in0=sp.rearrange("p (t n) -> p t n", t=ST), scalar=-1.0,
                                                     in1=ea.unsqueeze(1).broadcast_to([P, ST, H]),
                                                     op0=ALU.mult, op1=ALU.mult), "g")
                        sig(dve.reciprocal(beta, b1), "beta")
                        own("beta")
                        sig(dve.tensor_scalar(bhalf, beta, 0.5, None, ALU.mult), "beta")

                    def gcum():
                        ps = mid(dve, ("gcum",))
                        sig(dve.tensor_copy(gc, ps[:, 0:ST * H]), "gc")

                    def rot(r):
                        slab(dve, ("rot", r))
                        if r == 0:
                            dve.wait_ge(sem("tables_in"), 16)
                        if r >= 2:
                            dve.wait_ge(sem("rot_done"), r - 1)
                        sig(dve.tensor_tensor(wt[:, 2 + r % 2, :], dbank(("rot", r))[:, :], T("cos" + rot_dest(r)[1]),
                                              ALU.mult), "rot_cos")

                    def turn(r):
                        dst, kind = rot_dest(r)
                        m1, m2 = wt[:, 2 + r % 2, :], wt[:, 4 + r % 2, :]
                        dve.wait_ge(sem("rot_copy"), r + 1)
                        sig(dve.tensor_tensor(m2, wt[:, r % 2, :], T("sin" + kind), ALU.mult), "rot_sin")
                        own("rot_sin")
                        sig(dve.tensor_tensor(dst, m1, m2, ALU.add), "rot_done")

                    def unit(j):
                        dve.wait_ge(sem("unit_r"), j + 1)
                        sig(dve.tensor_tensor(qkv[:, j, :], qkv[:, j, :], gt[:, 2 + j % 2, :], ALU.mult), "unit_done")

                    def ret(h):
                        for m in range(ST):
                            i, w = ST * h + m, S - m * P
                            ps = mid(dve, ("rs", h, m))
                            if i >= 2:
                                dve.wait_ge(sem("ret_pv"), i - 1)
                            sig(dve.tensor_tensor(rp[:, i % 2, 0:w], ps[:, 0:w], T("decay", h, S)[:, 0:w],
                                                  ALU.mult), "ret_p")

                    def pre(n):
                        hh = slice(n * H, (n + 1) * H)
                        if n == 0:
                            own("beta")
                            own("gc")
                        sig(dve.tensor_tensor(heads(B["gtri"]), each(T("tri")), over(gg[:, hh], P), ALU.mult), "gb_in")
                        sig(dve.tensor_tensor(heads(B["bI"]), each(T("ident")), over(beta[:, hh], P), ALU.mult), "gb_in")

                    def decay(n):
                        hh = slice(n * H, (n + 1) * H)
                        ps = mid(dve, ("gb", n))
                        dve.wait_ge(sem("eg"), n + 1)
                        sig(dve.tensor_tensor(heads(B["E"]), heads(ps[:, :]), over(gc[:, hh], P), ALU.subtract), "esub")
                        sig(dve.tensor_copy(glast, heads(ps[:, :])[:, :, P - 1]), "glast")
                        own("esub")
                        sig(dve.tensor_scalar(B["E"], B["E"], 0.0, None, ALU.min), "emin")
                        own("glast")
                        sig(dve.tensor_tensor(gdif, glast, gc[:, hh], ALU.subtract), "gdif")
                        ps = mid(dve, ("bb", n))
                        dve.wait_ge(sem("E"), n + 1)
                        sig(dve.tensor_tensor(B["MT"], B["E"], ps[:, :], ALU.mult), "MTb")
                        sig(dve.tensor_tensor(heads(B["AT"]), heads(B["E"]), each(T("tri")), ALU.mult), "ATm")

                    def prep(n):
                        hh = slice(n * H, (n + 1) * H)
                        ps = mid(dve, ("kk", n))
                        own("MTb")
                        sig(dve.tensor_tensor(B["MT"], B["MT"], ps[:, :], ALU.mult), "MT")
                        own("MT")
                        sig(dve.tensor_tensor(heads(B["CT"]), heads(B["MT"]), each(T("level", 0, P)), ALU.mult), "CT")
                        ps = mid(dve, ("kq", n))
                        own("ATm")
                        sig(dve.tensor_tensor(B["AT"], B["AT"], ps[:, :], ALU.mult), "AT")
                        dve.wait_ge(sem("esm"), 2 * n + 2)
                        sig(dve.tensor_tensor(egl, beta[:, hh], egc, ALU.mult), "bk")
                        ps = mid(dve, ("kn", n))
                        own("bk")
                        sig(dve.tensor_tensor(heads(B["Kp"]), heads(ps[:, :]), over(egl, P), ALU.mult), "Kp")
                        sig(dve.tensor_tensor(heads(B["Kpp"]), heads(ps[:, :]), over(kps, P), ALU.mult), "Kpp")
                        ps = mid(dve, ("vn", n))
                        sig(dve.tensor_tensor(heads(B["vb"]), heads(ps[:, :]), over(bhalf[:, hh], P), ALU.mult), "vb")
                        dve.wait_ge(sem("eg"), n + 1)
                        sig(dve.tensor_tensor(heads(B["qs"]), qkv[:, H:2 * H, cut(n)], heads(B["eg"]), ALU.mult), "qs")

                    def pair(n):
                        own("CT")
                        ps = mid(dve, ("x0", n))
                        sig(dve.scalar_tensor_tensor(out=heads(B["X"]), in0=heads(ps[:, :]), scalar=-1.0,
                                                     in1=each(T("ident")), op0=ALU.mult, op1=ALU.add), "X")
                        sig(dve.scalar_tensor_tensor(out=heads(B["XT"]), in0=heads(B["CT"]), scalar=-1.0,
                                                     in1=each(T("ident")), op0=ALU.mult, op1=ALU.add), "XT")
                        own("XT")
                        level(n, 1)

                    def level(n, l):
                        sig(dve.tensor_tensor(heads(B["CT"]), heads(B["MT"]), each(T("level", l, P)), ALU.mult), "CT")

                    def right(n, l):
                        if l < 6:
                            mid(dve, ("p1", n, l))
                            level(n, l + 1)
                            ps = mid(dve, ("xx", n, l))
                            own("X")
                            even = blocks(B["X"], l, 0)
                            sig(dve.tensor_tensor(even, even, packed(ps, l), ALU.subtract), "X")
                        ps = mid(dve, ("xt", n, l))
                        odd = blocks(B["XT"], l, 1)
                        sig(dve.tensor_tensor(odd, odd, packed(ps, l), ALU.subtract), "XT")

                    def scan_o(n):
                        if n == ST - 1:
                            mid(dve, ("oT", n))
                            return
                        if n:
                            mid(dve, ("oT", n))
                            own("St")
                            sig(dve.tensor_tensor(heads(B["St"]), heads(B["St"]),
                                                  heads(B["eg"])[:, :, P - 1:P].broadcast_to([P, H, P]),
                                                  ALU.mult), "Sd")
                            ps = mid(dve, ("st", n))
                            own("Sd")
                            sig(dve.tensor_tensor(B["St"], B["St"], ps[:, :], ALU.add), "St")
                        else:
                            sig(dve.tensor_copy(B["St"], mid(dve, ("st", n))[:, :]), "St")

                    def index(tb):
                        w = slice(0, (tb + 1) * P)
                        for i in range(IH):
                            q = IH * (tb - 1) + i
                            dve.wait_ge(sem("relu"), q + 1)
                            ww = iw[:, tb * IH + i:tb * IH + i + 1]
                            if i == 0:
                                sig(dve.tensor_scalar(sc[:, w], rl[:, 0, w], ww, None, ALU.mult), "score")
                            else:
                                own("score")
                                sig(dve.scalar_tensor_tensor(out=sc[:, w], in0=rl[:, i % 2, w], scalar=ww,
                                                             in1=sc[:, w], op0=ALU.mult, op1=ALU.add), "score")
                        own("score")
                        sig(dve.tensor_tensor(sc[:, cut(tb)], sc[:, cut(tb)], T("maskadd"), ALU.add), "score")

                    def top(tb, part):
                        w = slice(0, (tb + 1) * P)
                        for r in range(part * TOPK // (8 * TOPS), (part + 1) * TOPK // (8 * TOPS)):
                            src = sc if r == 0 else work
                            own("score" if r == 0 else "picked")
                            sig(dve.max(mx8, src[:, w]), "best")
                            own("best")
                            sig(dve.match_replace(work[:, w], mx8, src[:, w], GONE), "picked")
                        if part == TOPS - 1:
                            own("picked")
                            sig(dve.tensor_tensor(negb[:, w], work[:, w], sc[:, w], ALU.is_equal), "kept")
                            own("kept")
                            sig(dve.tensor_scalar(negb[:, w], negb[:, w], NEG, None, ALU.mult), "negb")

                    def soft(tb):
                        w = slice(0, (tb + 1) * P)
                        bias = negb[:, w] if tb else T("maskadd")
                        if tb:
                            own("negb")
                            mid(dve, ("pt", tb - 1, tb - 1))
                        for h in range(H):
                            ps = mid(dve, ("as", tb, h))
                            sig(dve.tensor_tensor_reduce(pr[:, h, w], ps[:, w], bias, 1.0, GONE, ALU.add, ALU.max,
                                                         rmax[:, h:h + 1]), "smax")
                            own("smax")
                            sig(dve.tensor_scalar(nmax[:, h:h + 1], rmax[:, h:h + 1], -float(P) ** -0.5, None,
                                                  ALU.mult), "nmax")
                        for h in range(H):
                            dve.wait_ge(sem("sexp"), H * tb + h + 1)
                            sig(dve.reciprocal(rinv[:, h:h + 1], rsum[:, h:h + 1]), "rinv")
                            own("rinv")
                            sig(dve.tensor_scalar(pr[:, h, w], pr[:, h, w], rinv[:, h:h + 1], None, ALU.mult), "prob")

                    def fin(br, h):
                        src, gate_, rt = fin_parts(br, h)
                        dve.wait_ge(sem("fin_r"), FIN[br, h])
                        own("cg_w" if br == "C" else "z_w")
                        sig(dve.tensor_tensor(src, src, rt, ALU.mult), "fin_n")
                        own("fin_n")
                        sig(dve.scalar_tensor_tensor(out=src, in0=src, scalar=0.5 if br == "C" else ghalf, in1=gate_,
                                                     op0=ALU.mult, op1=ALU.mult), "fy")

                    def split_y(br, h):
                        b = "CAB".index(br)
                        if b and h == 0:
                            slab(dve, (("mergeC", 3), ("merge", "A", 3))[b - 1])
                        if br != "A":
                            dve.wait_ge(sem("fy"), FIN[br, h])
                        src = (oc[:, h, :], qa[:, h, :], qkv[:, H + h, :])[b]
                        dve.wait_ge(sem("y_hi"), H * b + h + 1)
                        sig(dve.tensor_tensor(y_lo[:, h, :], src, f32(y_hi[:, h, :]), ALU.subtract), "y_lo")

                    def swish(kind, h):
                        dst = (gt if kind == "cg" else oc)[:, h, :]
                        dve.wait_ge(sem(kind + "_t"), h + 1)
                        sig(dve.scalar_tensor_tensor(out=dst, in0=dst, scalar=1.0, in1=dbank((kind, h))[:, :],
                                                     op0=ALU.add, op1=ALU.mult), kind + "_w")

                    def mergeC(j):
                        slab(dve, ("mergeC", j))
                        for i in range(2):
                            n = 2 * j + i
                            dve.wait_ge(sem("gateC"), n + 1)
                            sig(dve.scalar_tensor_tensor(out=wt[:, n, :], in0=wt[:, n, :], scalar=1.0,
                                                         in1=dbank(("mergeC", j), i)[:, :],
                                                         op0=ALU.add, op1=ALU.mult), "gy")

                    def lo_merged(k):
                        dve.wait_ge(sem("a_hi"), KT + k + 1)
                        sig(dve.scalar_tensor_tensor(out=a_lo[:, k, :], in0=wt[:, k, :], scalar=0.5,
                                                     in1=f32(a_hi[:, k, :]), op0=ALU.mult, op1=ALU.subtract), "a_lo")

                    def merge(br, j):
                        b = "AB".index(br)
                        if b and j == 3:
                            for k in range(KT - 2):
                                lo_merged(k)
                        slab(dve, ("merge", br, j))
                        if "merged" in seen:
                            own("merged")
                        for i in range(2):
                            n = 8 * b + 2 * j + i
                            dve.wait_ge(sem("gtanh"), n + 1)
                            sig(dve.scalar_tensor_tensor(out=mt[:, n % 3, :], in0=gt[:, n % 4, :], scalar=1.0,
                                                         in1=dbank(("merge", br, j), i)[:, :],
                                                         op0=ALU.add, op1=ALU.mult), "gy")
                        own("gy")
                        for i in range(2):
                            n, m = 8 * b + 2 * j + i, wt[:, 2 * j + i, :]
                            sig(dve.tensor_tensor(m, m, mt[:, n % 3, :], ALU.add), "merged")

                    steps = {"norm": norm, "conv": conv, "silu": silu, "misc_turn": misc_turn, "decays": decays, "gcum": gcum,
                             "rot": rot, "turn": turn,
                             "unit": unit, "ret": ret, "pre": pre, "decay": decay, "prep": prep, "pair": pair,
                             "right": right, "scan_o": scan_o, "index": index, "top": top, "soft": soft, "fin": fin,
                             "split": split_y,
                             "mergeC": mergeC, "merge": merge}
                    for kind, *args in ORDER:
                        if kind in steps:
                            steps[kind](*args)
                        elif kind in ("cg", "z"):
                            swish(kind, *args)

                    for k in range(KT - 2, KT):
                        lo_merged(k)
                    gain = pg[:, 0:2, :].rearrange("p a s -> p (a s)")
                    dve.wait_ge(sem("x_back"), 16)
                    dve.wait_ge(sem("gain_in"), 16)

                    def gained(t, half):
                        dve.wait_ge(sem("sq_post_mix"), ST * half + t + 1)
                        w = slice(half * S, (half + 1) * S)
                        sig(dve.tensor_tensor(wide[:, t, w], (psM, psD)[half][t][:, :], gain[:, w], ALU.mult), "gained")

                    for t in range(ST):
                        gained(t, 0)
                    for t in range(ST + 3):
                        if t < ST:
                            total("post_mix", t)
                            gained(t, 1)
                        if 0 < t <= ST:
                            r = rstd("post_mix", t - 1, 2)
                            dve.wait_ge(sem("gained"), ST + t)
                            sig(dve.scalar_tensor_tensor(out=x[:, t - 1, :], in0=wide[:, t - 1, :], scalar=r,
                                                         in1=x[:, t - 1, :], op0=ALU.mult, op1=ALU.add), "x1")
                        if t > 2:
                            diagonal("pre_mlp", t - 3)
                    for k in range(KT):
                        lo_tile("h2T", 2, k, par_("gmlp"))
                        if k < 4:
                            own("a_lo")
                            dve.sem_inc(sem(f"hid_free{k}"), 1)
                    own("a_lo")
                    for t in range(ST):
                        dve.sem_inc(sem(f"acc_free{t}"), 1)
                    mid(dve, ("h2T", KT - 1))
                    sig(dve.memset(wide[:], 0.0), "zeroed")
                    own("zeroed")

                    def hidden(g):
                        with dve.Fori(0, FG // 4) as it:
                            for i in range(4):
                                dve.wait_ge(sem("slab_done"), it * 4 + g * PER_GROUP + (SL_MLP + i + 1))
                                dve.tensor_scalar(gt[:, i, :], psM[i][:, :], 0.0, None, ALU.max) \
                                    .then_inc(sem("relu1"), 1)
                                dve.wait_ge(sem("relu1"), it * 4 + g * FG + (i + 1))
                                dve.tensor_tensor(gt[:, i, :], gt[:, i, :], psM[i][:, :], ALU.mult) \
                                    .then_inc(sem("relu2"), 1)
                                dve.wait_ge(sem("f_hi"), it * 4 + g * FG + (i + 1))
                                dve.tensor_tensor(f_lo[:, bass.ds(it * 4 + i, 1), :].rearrange("p a s -> p (a s)"),
                                                  gt[:, i, :],
                                                  f32(f_hi[:, bass.ds(it * 4 + i, 1), :].rearrange("p a s -> p (a s)")),
                                                  ALU.subtract).then_inc(sem("f_lo"), 1)

                    def add_half0(g):
                        dve.wait_ge(sem("slab_done"), g * PER_GROUP + (SL_MLP + FG + 8))
                        for t in range(ST):
                            w = wide[:, t, 0:S]
                            dve.tensor_tensor(w, w, psD[t][:, :], ALU.add).then_inc(sem(f"acc_free{t}"), 1)

                    def add_half1(g, t):
                        if t < ST - 1:
                            dve.wait_ge(sem("down_tile"), g * (ST - 1) + (t + 1))
                        else:
                            dve.wait_ge(sem("slab_done"), g * PER_GROUP + (SL_MLP + PER_GROUP))
                        w = wide[:, t, S:D]
                        dve.tensor_tensor(w, w, psM[t][:, :], ALU.add).then_inc(sem(f"hid_free{t}"), 1)

                    with dve.Fori(0, GROUPS - 1) as g:
                        hidden(g)
                        add_half0(g)
                        for t in range(ST):
                            add_half1(g, t)
                        for t in range(ST):
                            dve.wait_ge(sem(f"acc_free{t}"), g + 2)
                            dve.wait_ge(sem(f"hid_free{t}"), g + 2)
                    hidden(GROUPS - 1)
                    add_half0(GROUPS - 1)
                    for t in range(ST + 4):
                        if t < ST:
                            add_half1(GROUPS - 1, t)
                        if 1 <= t <= ST:
                            total("post_mlp", t - 1)
                        if t == 4:
                            diagonal("pre_mix", 0)
                        if 2 <= t <= ST + 1:
                            n = t - 2
                            r = rstd("post_mlp", n, 2)
                            dve.wait_ge(sem("gained2"), ST + n + 1)
                            sig(dve.scalar_tensor_tensor(out=x[:, n, :], in0=wide[:, n, :], scalar=r,
                                                         in1=x[:, n, :], op0=ALU.mult, op1=ALU.add), "x2")
                        if t > 4:
                            diagonal("pre_mix", t - 4)
            ids = [s.num for s in sems.values()]
            nc.all_engine_barrier(sems_to_clear=range(min(ids), max(ids) + 1))

        with nc.Block() as block:
            @block.sync
            def _(sp):
                sp.wait_ge(kept["x_saved"], 16 * ST * (DEPTH + 1))


def lay_out(i, a):
    f = np.float32
    w_in = a["w_in"][i]
    matrices = {"in": w_in, "branch": a["w_branch"][i], "out": a["w_out"][i], "up": a["w_up"][i],
                "down": a["w_down"][i],
                "misc": np.concatenate([w_in[:, I_W:I_W + IH], w_in[:, B_A:B_A + 2 * H]], 1),
                "ik": np.concatenate([w_in[:, I_K:I_K + 64]] * 2, 1)}
    slabs = np.zeros((NSLAB, P, SLAB), f)
    for to, (name, k0, ks, c0, n) in zip(slabs, HOLDS):
        to.reshape(P, ks, SLAB // ks)[:, :, :n] = \
            matrices[name][k0 * P:(k0 + ks) * P, c0:c0 + n].reshape(ks, P, n).transpose(1, 0, 2)
    return slabs


def kernel(**inputs):
    import concourse.bacc as bacc
    from concourse.bass_utils import run_bass_kernel_spmd as run

    a = {n: np.asarray(v) for n, v in inputs.items()}
    f = np.float32
    ws = np.concatenate([lay_out(i, a) for i in range(DEPTH)] + [np.zeros((2, P, SLAB), f)])
    par = np.zeros((DEPTH + 1, P, NPAR), f)
    for i in range(DEPTH):
        for n, v in (("gmix", a["ln_mix_pre"][i].reshape(KT, P).T), ("gmlp", a["ln_mlp_pre"][i].reshape(KT, P).T),
                     ("conv", a["gdn_conv"][i].reshape(CW, 3, H, P)[:, [1, 0, 2]].reshape(CW, CONVS, P)
                      .transpose(2, 1, 0).reshape(P, -1)),
                     ("gnorm", a["gdn_norm"][i][:, None]), ("alog", np.broadcast_to(a["gdn_a_log"][i], (P, H))),
                     ("dtb", np.broadcast_to(a["gdn_dt_bias"][i], (P, H)))):
            par[i, :, PAR[n][0]:PAR[n][0] + PAR[n][1]] = v
    post = np.stack([np.concatenate([np.broadcast_to(a["ln_mix_post"][i], (P, D)),
                                     np.broadcast_to(a["ln_mlp_post"][i], (P, D))], 1) for i in range(DEPTH)])
    xs = np.ascontiguousarray(a["x"].reshape(ST, P, D).transpose(1, 0, 2).reshape(P, ST * D))
    arrays = {"in_ws": ws, "in_par": par, "in_post": np.ascontiguousarray(post), "in_tab": tables(), "in_x": xs}
    nc = bacc.Bacc("TRN2", target_bir_lowering=False, num_devices=1, dynamic_dma_scratch_size=1024)
    args = [nc.dram_tensor(n, v.shape, F32, kind="ExternalInput").ap() for n, v in arrays.items()]
    out = nc.dram_tensor("out", (P, ST * D), F32, kind="ExternalOutput").ap()
    build(nc, *args, out)
    r = run(nc, [arrays], core_ids=[0])
    return np.asarray(r.results[0]["out"]).reshape(P, ST, D).transpose(1, 0, 2).reshape(1, S, D)
```
